# Optimizing a Trainium2 kernel written in Bass

```python
import math
import jax
import jax.numpy as jnp
from jax import lax
import numpy as np

D_MODEL = 1024
BATCH = 1
SEQ = 256
DEPTH = 2

F32 = jnp.float32

DN_ALPHA = (2.0 * DEPTH) ** 0.25
DN_BETA = (8.0 * DEPTH) ** -0.25
LN_EPS = 1e-5

A_WIDTH = D_MODEL // 2
A_HEADS = 4
A_VDIM = A_WIDTH // A_HEADS
A_QKDIM = A_VDIM // 2
A_COLS = 3 * A_WIDTH
A_QBLOCK = 128
A_NORM_EPS = 1e-5

B_WIDTH = D_MODEL // 2
B_HEAD = 64
B_HEADS = B_WIDTH // B_HEAD
B_LORA_W = 64
B_LORA_A = 64
B_LORA_G = 128
B_COLS = 3 * B_WIDTH + B_LORA_W + B_LORA_A + B_LORA_G
B_SPLITS = (B_WIDTH, 2 * B_WIDTH, 3 * B_WIDTH, 3 * B_WIDTH + B_LORA_W, 3 * B_WIDTH + B_LORA_W + B_LORA_A)
B_LNX_EPS = 64e-5

C_DK = 128
C_DV = 128
C_KHEADS = D_MODEL // 128
C_VHEADS = 2 * C_KHEADS
C_QK_W = C_KHEADS * C_DK
C_V_W = C_VHEADS * C_DV
C_QKV_W = 2 * C_QK_W + C_V_W
C_COLS = C_QKV_W + C_V_W + 2 * C_VHEADS
C_SPLITS = (C_QKV_W, C_QKV_W + C_V_W, C_QKV_W + C_V_W + C_VHEADS)
C_CONV = 4
C_CHUNK = 64
C_NORM_EPS = 1e-6

N_EXPERTS = 64
TOP_K = 8
N_GROUPS = 8
TOPK_GROUPS = 4
D_EXPERT = D_MODEL // 4
ROUTE_SCALE = 2.5
MOE_BLOCK = 128

kernel_name = 'hybrid_diffattn_rwkv7_gdn_moe'

def layer_norm(x, g, b):
    xf = x.astype(F32)
    mu = jnp.mean(xf, -1, keepdims=True)
    var = jnp.mean(jnp.square(xf - mu), -1, keepdims=True)
    return ((xf - mu) * lax.rsqrt(var + LN_EPS) * g + b).astype(x.dtype)

def rms_norm(x, g, eps):
    xf = x.astype(F32)
    return xf * lax.rsqrt(jnp.mean(jnp.square(xf), -1, keepdims=True) + eps) * g

def l2_normalize(x, eps=1e-6):
    xf = x.astype(F32)
    return xf * lax.rsqrt(jnp.sum(jnp.square(xf), -1, keepdims=True) + eps)

def token_shift(p):
    return jnp.pad(p, ((0, 0), (1, 0), (0, 0)))[:, :-1]

def alibi_slopes(n):
    return jnp.asarray(np.array([2.0 ** (-8.0 * (i + 1) / n) for i in range(n)], dtype=np.float32))

def swiglu(h, wg, wu, wd):
    return (jax.nn.silu(h @ wg) * (h @ wu)) @ wd

def causal_depthwise_conv(x, w):
    kw, ch = w.shape
    return lax.conv_general_dilated(x, w[:, None, :].astype(x.dtype), window_strides=(1,), padding=[(kw - 1, 0)], dimension_numbers=('NWC', 'WIO', 'NWC'), feature_group_count=ch)

def blocked_diff_softmax(q, k, v, lam, slopes):
    bn, s = q.shape[0], q.shape[1]
    nb = s // A_QBLOCK
    scale = A_QKDIM ** -0.5
    pos_k = jnp.arange(s)
    qb = jnp.moveaxis(q.reshape(bn, nb, A_QBLOCK, A_HEADS, 2, A_QKDIM), 1, 0)

    def one_block(args):
        q_blk, i = args
        pos_q = i * A_QBLOCK + jnp.arange(A_QBLOCK)
        dist = (pos_q[:, None] - pos_k[None, :]).astype(F32)
        sc = jnp.einsum('bqhcd,bkhcd->bhcqk', q_blk, k).astype(F32) * scale
        sc = sc - slopes[None, :, None, None, None] * dist
        sc = jnp.where(dist >= 0, sc, -jnp.inf)
        p = jax.nn.softmax(sc, axis=-1)
        attn = p[:, :, 0] - lam * p[:, :, 1]
        return jnp.einsum('bhqk,bkhd->bqhd', attn.astype(v.dtype), v)

    out = lax.map(one_block, (qb, jnp.arange(nb)))
    return jnp.moveaxis(out, 0, 1).reshape(bn, s, A_HEADS, A_VDIM)

def diff_attention_group(pa, lam_params, norm_g, layer_idx):
    bn, s, _ = pa.shape
    q, k, v = jnp.split(pa, 3, axis=-1)
    q = q.reshape(bn, s, A_HEADS, 2, A_QKDIM)
    k = k.reshape(bn, s, A_HEADS, 2, A_QKDIM)
    v = v.reshape(bn, s, A_HEADS, A_VDIM)
    lam_init = 0.8 - 0.6 * math.exp(-0.3 * layer_idx)
    lp = lam_params.astype(F32)
    lam = jnp.exp(jnp.sum(lp[0] * lp[1])) - jnp.exp(jnp.sum(lp[2] * lp[3])) + lam_init
    o = blocked_diff_softmax(q, k, v, lam, alibi_slopes(A_HEADS))
    o = rms_norm(o, norm_g, A_NORM_EPS) * (1.0 - lam_init)
    return o.reshape(bn, s, A_WIDTH).astype(pa.dtype)

def rwkv7_scan(r, w_log, k, v, kk, a):
    bn, s, h, n = r.shape
    decay = jnp.exp(-jnp.exp(w_log.astype(F32)))
    xs = tuple(jnp.moveaxis(t.astype(F32), 1, 0) for t in (r, decay, k, v, kk, a))

    def step(state, inp):
        r_t, d_t, k_t, v_t, kk_t, a_t = inp
        sa = jnp.einsum('bhvk,bhk->bhv', state, -kk_t)
        state = state * d_t[:, :, None, :] + sa[..., None] * (kk_t * a_t)[:, :, None, :] + v_t[..., None] * k_t[:, :, None, :]
        return state, jnp.einsum('bhvk,bhk->bhv', state, r_t)

    _, ys = lax.scan(step, jnp.zeros((bn, h, n, n), F32), xs)
    return jnp.moveaxis(ys, 0, 1)

def rwkv7_group(pb, mix, w0, w2, a0, a2, g2, k_k, k_a, r_k, lnx_g, lnx_b):
    bn, s, _ = pb.shape
    pb = pb + (token_shift(pb) - pb) * mix
    r, k, v, xw, xa, xg = jnp.split(pb, B_SPLITS, axis=-1)
    w_log = -jax.nn.softplus(-(w0 + jnp.tanh(xw) @ w2)) - 0.5
    a = jax.nn.sigmoid(a0 + xa @ a2)
    g = jax.nn.sigmoid(xg) @ g2

    def hd(t):
        return t.reshape(bn, s, B_HEADS, B_HEAD)

    def hp(t):
        return t.reshape(B_HEADS, B_HEAD)

    r, k, v, w_log, a = hd(r), hd(k), hd(v), hd(w_log), hd(a)
    kk = l2_normalize(k * hp(k_k))
    k = k * (1.0 + (a - 1.0) * hp(k_a))
    y = rwkv7_scan(r, w_log, k, v, kk, a)
    mu = jnp.mean(y, -1, keepdims=True)
    var = jnp.mean(jnp.square(y - mu), -1, keepdims=True)
    y = (y - mu) * lax.rsqrt(var + B_LNX_EPS) * hp(lnx_g) + hp(lnx_b)
    y = y + jnp.sum(r * k * hp(r_k), -1, keepdims=True) * v
    return (y.reshape(bn, s, B_WIDTH) * g).astype(pb.dtype)

def attn_rwkv_mixer(x, w_in, a_lambda, a_norm_g, b_mix, b_w0, b_w2, b_a0, b_a2, b_g2, b_k_k, b_k_a, b_r_k, b_lnx_g, b_lnx_b, w_out, layer_idx):
    p = x @ w_in
    ya = diff_attention_group(p[..., :A_COLS], a_lambda, a_norm_g, layer_idx)
    yb = rwkv7_group(p[..., A_COLS:], b_mix, b_w0, b_w2, b_a0, b_a2, b_g2, b_k_k, b_k_a, b_r_k, b_lnx_g, b_lnx_b)
    return jnp.concatenate([ya, yb], axis=-1) @ w_out

def chunk_gated_delta_rule(q, k, v, g, beta):
    bn, s, h, dk = q.shape
    dv = v.shape[-1]
    n = s // C_CHUNK

    def chunks(t):
        return jnp.swapaxes(t.astype(F32).reshape((bn, n, C_CHUNK, h) + t.shape[3:]), 2, 3)

    q, k, v, g, beta = chunks(q), chunks(k), chunks(v), chunks(g), chunks(beta)
    g = jnp.cumsum(g, axis=-1)
    tri = jnp.tril(jnp.ones((C_CHUNK, C_CHUNK), bool))
    strict = jnp.tril(jnp.ones((C_CHUNK, C_CHUNK), bool), -1)
    decay = jnp.exp(jnp.where(tri, g[..., :, None] - g[..., None, :], -jnp.inf))
    kb = k * beta[..., None]
    lower = jnp.where(strict, jnp.einsum('bnhid,bnhjd->bnhij', kb, k) * decay, 0.0)
    rhs = jnp.concatenate([v * beta[..., None], kb * jnp.exp(g)[..., None]], axis=-1)
    sol = lax.linalg.triangular_solve(jnp.eye(C_CHUNK, dtype=F32) + lower, rhs, left_side=True, lower=True, unit_diagonal=True)
    u, w = sol[..., :dv], sol[..., dv:]
    attn = jnp.where(tri, jnp.einsum('bnhid,bnhjd->bnhij', q, k) * decay, 0.0)
    q_dec = q * jnp.exp(g)[..., None]
    k_dec = k * jnp.exp(g[..., -1:] - g)[..., None]
    g_last = jnp.exp(g[..., -1])

    def step(state, inp):
        u_c, w_c, q_c, k_c, a_c, gl = inp
        v_new = u_c - jnp.einsum('bhcd,bhde->bhce', w_c, state)
        o = jnp.einsum('bhcd,bhde->bhce', q_c, state) + jnp.einsum('bhij,bhje->bhie', a_c, v_new)
        state = state * gl[..., None, None] + jnp.einsum('bhcd,bhce->bhde', k_c, v_new)
        return state, o

    xs = tuple(jnp.moveaxis(t, 1, 0) for t in (u, w, q_dec, k_dec, attn, g_last))
    _, o = lax.scan(step, jnp.zeros((bn, h, dk, dv), F32), xs)
    return o.transpose(1, 0, 3, 2, 4).reshape(bn, s, h, dv)

def gated_deltanet_mixer(x, w_in, conv_w, a_log, dt_bias, norm_g, w_out):
    bn, s, _ = x.shape
    p = x @ w_in
    qkv, z, b, a = jnp.split(p, C_SPLITS, axis=-1)
    qkv = jax.nn.silu(causal_depthwise_conv(qkv, conv_w))
    q, k, v = jnp.split(qkv, (C_QK_W, 2 * C_QK_W), axis=-1)
    rep = C_VHEADS // C_KHEADS
    q = jnp.repeat(l2_normalize(q.reshape(bn, s, C_KHEADS, C_DK)) * (C_DK ** -0.5), rep, axis=2)
    k = jnp.repeat(l2_normalize(k.reshape(bn, s, C_KHEADS, C_DK)), rep, axis=2)
    v = v.reshape(bn, s, C_VHEADS, C_DV)
    beta = jax.nn.sigmoid(b.astype(F32))
    g = -jnp.exp(a_log.astype(F32)) * jax.nn.softplus(a.astype(F32) + dt_bias)
    o = chunk_gated_delta_rule(q, k, v, g, beta)
    o = rms_norm(o, norm_g, C_NORM_EPS) * jax.nn.silu(z.reshape(bn, s, C_VHEADS, C_DV).astype(F32))
    return o.reshape(bn, s, C_V_W).astype(x.dtype) @ w_out

def moe_ffn(x, router_w, router_b, exp_gate, exp_up, exp_down, sh_gate, sh_up, sh_down):
    bn, s, d = x.shape
    t = bn * s
    h = x.reshape(t, d)
    scores = jax.nn.sigmoid((h @ router_w).astype(F32))
    choice = scores + router_b
    per_group = N_EXPERTS // N_GROUPS
    grp_score = jnp.sum(lax.top_k(choice.reshape(t, N_GROUPS, per_group), 2)[0], axis=-1)
    _, gidx = lax.top_k(grp_score, TOPK_GROUPS)
    gmask = jnp.any(gidx[..., None] == jnp.arange(N_GROUPS), axis=1)
    choice = jnp.where(jnp.repeat(gmask, per_group, axis=1), choice, -jnp.inf)
    _, eidx = lax.top_k(choice, TOP_K)
    gate = jnp.take_along_axis(scores, eidx, axis=1)
    gate = gate / jnp.sum(gate, -1, keepdims=True) * ROUTE_SCALE

    tk = t * TOP_K
    flat_e = eidx.reshape(tk)
    flat_tok = jnp.repeat(jnp.arange(t, dtype=jnp.int32), TOP_K)
    flat_g = gate.reshape(tk)
    order = jnp.argsort(flat_e)
    e_sorted = flat_e[order]
    counts = jnp.bincount(flat_e, length=N_EXPERTS)
    start = jnp.cumsum(counts) - counts
    padded = (counts + MOE_BLOCK - 1) // MOE_BLOCK * MOE_BLOCK
    pend = jnp.cumsum(padded)
    pstart = pend - padded
    dest = pstart[e_sorted] + jnp.arange(tk, dtype=jnp.int32) - start[e_sorted]
    n_blocks = (tk + N_EXPERTS * (MOE_BLOCK - 1) + MOE_BLOCK - 1) // MOE_BLOCK
    npad = n_blocks * MOE_BLOCK
    slot_tok = jnp.full((npad,), t, jnp.int32).at[dest].set(flat_tok[order])
    slot_gate = jnp.zeros((npad,), F32).at[dest].set(flat_g[order])
    block_e = jnp.minimum(jnp.searchsorted(pend, jnp.arange(n_blocks) * MOE_BLOCK, side='right'), N_EXPERTS - 1)
    h_pad = jnp.concatenate([h, jnp.zeros((1, d), h.dtype)], axis=0)

    def expert_block(args):
        tok, e = args
        return swiglu(h_pad[tok], exp_gate[e], exp_up[e], exp_down[e])

    yb = lax.map(expert_block, (slot_tok.reshape(n_blocks, MOE_BLOCK), block_e)).reshape(npad, d)
    routed = jnp.zeros((t + 1, d), F32).at[slot_tok].add(yb.astype(F32) * slot_gate[:, None])[:t]
    shared = swiglu(h, sh_gate, sh_up, sh_down)
    return (routed.astype(x.dtype) + shared).reshape(bn, s, d)

def setup_inputs(seed: int = 0) -> dict:
    key = jax.random.key(seed)
    ks = iter(jax.random.split(key, 96))

    def nrm(shape, scale):
        return jax.random.normal(next(ks), shape, F32) * scale

    def unif(shape, lo, hi):
        return jax.random.uniform(next(ks), shape, F32, lo, hi)

    def gain(n):
        return 1.0 + nrm((n,), 0.02)

    def bias(n):
        return nrm((n,), 0.02)

    def moe_params(pfx):
        out = {}
        out[pfx + 'router_w'] = nrm((D_MODEL, N_EXPERTS), D_MODEL ** -0.5)
        out[pfx + 'router_b'] = nrm((N_EXPERTS,), 0.01)
        out[pfx + 'exp_gate'] = nrm((N_EXPERTS, D_MODEL, D_EXPERT), D_MODEL ** -0.5)
        out[pfx + 'exp_up'] = nrm((N_EXPERTS, D_MODEL, D_EXPERT), D_MODEL ** -0.5)
        out[pfx + 'exp_down'] = nrm((N_EXPERTS, D_EXPERT, D_MODEL), DN_BETA * D_EXPERT ** -0.5)
        out[pfx + 'sh_gate'] = nrm((D_MODEL, D_EXPERT), D_MODEL ** -0.5)
        out[pfx + 'sh_up'] = nrm((D_MODEL, D_EXPERT), D_MODEL ** -0.5)
        out[pfx + 'sh_down'] = nrm((D_EXPERT, D_MODEL), DN_BETA * D_EXPERT ** -0.5)
        return out

    inp = {}
    inp['x'] = nrm((BATCH, SEQ, D_MODEL), 1.0)
    inp['l0_w_in'] = nrm((D_MODEL, A_COLS + B_COLS), D_MODEL ** -0.5)
    inp['l0_a_lambda'] = nrm((4, A_QKDIM), 0.1)
    inp['l0_a_norm_g'] = gain(A_VDIM)
    inp['l0_b_mix'] = unif((B_COLS,), 0.0, 1.0)
    inp['l0_b_w0'] = unif((B_WIDTH,), -2.0, 1.0)
    inp['l0_b_w2'] = nrm((B_LORA_W, B_WIDTH), B_LORA_W ** -0.5)
    inp['l0_b_a0'] = unif((B_WIDTH,), -0.5, 0.5)
    inp['l0_b_a2'] = nrm((B_LORA_A, B_WIDTH), B_LORA_A ** -0.5)
    inp['l0_b_g2'] = nrm((B_LORA_G, B_WIDTH), B_LORA_G ** -0.5)
    inp['l0_b_k_k'] = 0.85 + nrm((B_WIDTH,), 0.05)
    inp['l0_b_k_a'] = 1.0 + nrm((B_WIDTH,), 0.05)
    inp['l0_b_r_k'] = nrm((B_WIDTH,), 0.1)
    inp['l0_b_lnx_g'] = gain(B_WIDTH)
    inp['l0_b_lnx_b'] = bias(B_WIDTH)
    inp['l0_w_out'] = nrm((A_WIDTH + B_WIDTH, D_MODEL), DN_BETA * (A_WIDTH + B_WIDTH) ** -0.5)
    inp['l0_ln1_g'] = gain(D_MODEL)
    inp['l0_ln1_b'] = bias(D_MODEL)
    inp.update(moe_params('l0_'))
    inp['l0_ln2_g'] = gain(D_MODEL)
    inp['l0_ln2_b'] = bias(D_MODEL)
    inp['l1_w_in'] = nrm((D_MODEL, C_COLS), D_MODEL ** -0.5)
    inp['l1_conv_w'] = nrm((C_CONV, C_QKV_W), C_CONV ** -0.5)
    inp['l1_a_log'] = jnp.log(unif((C_VHEADS,), 1.0, 16.0))
    dt = jnp.exp(unif((C_VHEADS,), math.log(1e-3), math.log(1e-1)))
    inp['l1_dt_bias'] = dt + jnp.log(-jnp.expm1(-dt))
    inp['l1_norm_g'] = gain(C_DV)
    inp['l1_w_out'] = nrm((C_V_W, D_MODEL), DN_BETA * C_V_W ** -0.5)
    inp['l1_ln1_g'] = gain(D_MODEL)
    inp['l1_ln1_b'] = bias(D_MODEL)
    inp.update(moe_params('l1_'))
    inp['l1_ln2_g'] = gain(D_MODEL)
    inp['l1_ln2_b'] = bias(D_MODEL)
    return inp

def reference(x, l0_w_in, l0_a_lambda, l0_a_norm_g, l0_b_mix, l0_b_w0, l0_b_w2, l0_b_a0, l0_b_a2, l0_b_g2, l0_b_k_k, l0_b_k_a, l0_b_r_k, l0_b_lnx_g, l0_b_lnx_b, l0_w_out, l0_ln1_g, l0_ln1_b, l0_router_w, l0_router_b, l0_exp_gate, l0_exp_up, l0_exp_down, l0_sh_gate, l0_sh_up, l0_sh_down, l0_ln2_g, l0_ln2_b, l1_w_in, l1_conv_w, l1_a_log, l1_dt_bias, l1_norm_g, l1_w_out, l1_ln1_g, l1_ln1_b, l1_router_w, l1_router_b, l1_exp_gate, l1_exp_up, l1_exp_down, l1_sh_gate, l1_sh_up, l1_sh_down, l1_ln2_g, l1_ln2_b):
    mix_params = (
        (l0_w_in, l0_a_lambda, l0_a_norm_g, l0_b_mix, l0_b_w0, l0_b_w2, l0_b_a0, l0_b_a2, l0_b_g2, l0_b_k_k, l0_b_k_a, l0_b_r_k, l0_b_lnx_g, l0_b_lnx_b, l0_w_out),
        (l1_w_in, l1_conv_w, l1_a_log, l1_dt_bias, l1_norm_g, l1_w_out),
    )
    norm_params = ((l0_ln1_g, l0_ln1_b, l0_ln2_g, l0_ln2_b), (l1_ln1_g, l1_ln1_b, l1_ln2_g, l1_ln2_b))
    moe_params = (
        (l0_router_w, l0_router_b, l0_exp_gate, l0_exp_up, l0_exp_down, l0_sh_gate, l0_sh_up, l0_sh_down),
        (l1_router_w, l1_router_b, l1_exp_gate, l1_exp_up, l1_exp_down, l1_sh_gate, l1_sh_up, l1_sh_down),
    )
    for layer in range(DEPTH):
        if layer % 2 == 0:
            m = attn_rwkv_mixer(x, *mix_params[layer], layer_idx=layer)
        else:
            m = gated_deltanet_mixer(x, *mix_params[layer])
        ln1_g, ln1_b, ln2_g, ln2_b = norm_params[layer]
        x = layer_norm(DN_ALPHA * x + m, ln1_g, ln1_b)
        x = layer_norm(DN_ALPHA * x + moe_ffn(x, *moe_params[layer]), ln2_g, ln2_b)
    return x


_drawn_inputs = setup_inputs


def setup_inputs(seed=0):
    import zlib

    import numpy as np

    out = dict(_drawn_inputs(seed))
    spreads = {}
    factors = {'l1_norm_g': 3.621, 'l1_ln2_g': 3.01, 'l1_ln2_b': 2.844}
    for name, (base, spread) in spreads.items():
        noise = np.random.default_rng([zlib.crc32(name.encode()), seed]).standard_normal(out[name].shape)
        drawn = base * np.exp(spread * noise) if base else spread * noise
        out[name] = jnp.asarray(drawn.astype(out[name].dtype))
    for name, factor in factors.items():
        out[name] = (out[name] * factor).astype(out[name].dtype)
    return out
```

```python
import math
from contextlib import ExitStack

import numpy as np

import concourse.bass as bass
from concourse import mybir

F32 = mybir.dt.float32
BF16 = mybir.dt.bfloat16
I32 = mybir.dt.int32
ALU = mybir.AluOpType
ACT = mybir.ActivationFunctionType
AX = mybir.AxisListType.X

P = 128
SEQ, D = 256, 1024
TT = SEQ // P
KT = D // P
ALPHA = 4.0 ** 0.25
LN_EPS = 1e-5

NE, NG, GE, TOPG = 64, 8, 8, 4
DE = D // 4
SLOTS = 64
ROUNDS = SEQ // SLOTS
ROUTE_SCALE = 2.5
EPI = 4
ITERS = NE // EPI
O_ITERS = (ROUNDS - 1) * ITERS
PCOLS = ROUNDS * NE + EPI
FAR = 1e30

RING = 4
WIDE = 4096
NARROW = 2048
CH = WIDE // KT

C_ID, C_STRICT, C_INCL, C_ONES, C_TRIU = 0, 128, 256, 384, 512
C_LVL = 640
LEVELS = 6
C_HALF = C_LVL + LEVELS * P
C_SEG = C_HALF + P
C_LOW = C_SEG + P
C_IOTA = C_LOW + P
C_G8 = C_IOTA + SLOTS
C_HEAD = C_G8 + NG * NG
C_END = C_HEAD + 32
SLOPES = [2.0 ** (-8.0 * (i + 1) / 4) for i in range(4)]
MIX_ARENA = 20000
N_M = {"M0": 9, "M1": 16}


def constants():
    p = np.arange(P)[:, None]
    f = np.arange(P)[None, :]
    same = (p // 64) == (f // 64)
    c = np.zeros((P, C_END), np.float32)
    c[:, C_ID:C_ID + P] = p == f
    c[:, C_STRICT:C_STRICT + P] = same & (p < f)
    c[:, C_INCL:C_INCL + P] = same & (p <= f)
    c[:, C_ONES:C_ONES + P] = 1.0
    c[:, C_TRIU:C_TRIU + P] = p < f
    for n in range(LEVELS):
        m = 1 << n
        c[:, C_LVL + n * P:C_LVL + (n + 1) * P] = (p // (2 * m) == f // (2 * m)) & (p % (2 * m) < m) & (f % (2 * m) >= m)
    c[:, C_HALF:C_HALF + P] = same
    c[:, C_SEG:C_SEG + P] = p > f
    c[:, C_LOW:C_LOW + P] = same & (f <= p)
    c[:, C_IOTA:C_IOTA + SLOTS] = np.arange(SLOTS)[None, :]
    c[:, C_G8:C_G8 + NG * NG] = (np.arange(NG)[None, :] < np.arange(NG)[:, None]).reshape(1, -1)
    for t in range(4):
        for h in range(8):
            c[:, C_HEAD + t * 8 + h] = (h // 2 == t) & ((np.arange(P) // 64) == h % 2)
    dist = P + p[:, :, None] - np.arange(2 * P)[None, None, :]
    bias = np.where(dist >= 0, -np.array(SLOPES)[None, :, None] * dist, -1e30)
    return c, bias.astype(np.float32).reshape(P, 4 * 2 * P)


OVER = ["onehot_ready", "gated_ready", "gathered", "gathered_lo", "gathered_hi", "gate_up_done", "silu_ready", "act_ready",
        "pair_turned", "turned_ready", "down_done", "y_lo", "y_hi", "pair_combined", "wide_used", "narrow_used"
        ] + [f"{ring}_loaded{n}" for ring in ("wide", "narrow") for n in range(RING)]


class Sems(dict):

    def __init__(self, nc, ctx):
        super().__init__()
        self.nc, self.ctx = nc, ctx

    def __missing__(self, name):
        self[name] = self.ctx.enter_context(self.nc.semaphore(name))
        return self[name]


def spread(ap, axis, shape):
    return ap.unsqueeze(axis).broadcast_to(shape)


def build_program(nc, a, out, stages=("M0", "E0", "M1", "E1")):
    with ExitStack() as ctx:
        S = Sems(nc, ctx)

        def sb(name, shape, dt=F32):
            return ctx.enter_context(nc.sbuf_tensor(name, shape, dt))

        wide = sb("wide_ring", [P, RING, WIDE])
        narrow = sb("narrow_ring", [P, RING, NARROW])
        x_tok = sb("x_tok", [P, TT, D])
        xT = sb("xT", [P, KT, SEQ])
        cst = sb("constants_sb", [P, C_END])
        lng = sb("ln_gain", [P, D])
        lnb = sb("ln_bias", [P, D])
        stats = sb("ln_stats", [P, TT, 2, 6])
        mv = sb("ln_mean_var", [P, TT, 2])
        rstd = sb("ln_rstd", [P, TT])
        arena = sb("arena", [P, MIX_ARENA])
        ps = ctx.enter_context(nc.psum_tensor("ps", [P, 8, 512], F32))
        ident = cst[:, C_ID:C_ID + P]

        def cm(col, n=P):
            return cst[:, col:col + n]

        def area(at, *dims, base=arena):
            n = int(np.prod(dims))
            v = base[:, at:at + n]
            names = "abcd"[:len(dims)]
            if len(dims) == 1:
                return v
            return v.rearrange(f"p ({' '.join(names)}) -> p {' '.join(names)}", **dict(zip(names, dims)))

        at = 0

        def take(*dims):
            nonlocal at
            v = area(at, *dims)
            at += int(np.prod(dims))
            return v

        h_rest = take(TT, KT, P)
        h_parts = take(TT * 3 * KT * P // 2).bitcast(BF16).rearrange("p (a b c d) -> p a b c d", a=TT, b=3, c=KT)
        scores = take(TT, NE)
        choice = take(TT, NE)
        choice_rep = take(TT, NE)
        sel = take(TT, NE)
        gate_one = take(TT, NE)
        grp_max = take(TT, NG, 8)
        grp = take(TT, NG)
        grp_gt = take(TT, NG, NG)
        grp_eq = take(TT, NG, NG)
        grp_rank = take(TT, NG)
        grp_off = take(TT, NG)
        top8 = take(TT, 8)
        gate_sum = take(TT)
        gate_inv = take(TT)
        pos_one = take(TT, NE)
        pos_r = take(TT, PCOLS)
        gate_r = take(TT, PCOLS)
        rb = take(NE)
        router_w = take(KT, NE)
        cnt = take(2)
        flag = take(2).bitcast(I32)
        oh = take(TT * EPI * SLOTS // 2).bitcast(BF16).rearrange("p (a b c) -> p a b c", a=TT, b=EPI)
        ohg = take(TT, EPI, SLOTS)
        hTe = take(2, KT, P)
        silu_g = take(2, DE)
        act_tok = take(2, DE)
        turned = take(2, 2 * 2 * P)
        y_sb = take(2, D)
        sh_silu = take(2, SEQ)
        shT = take(2, SEQ)
        assert at <= MIX_ARENA, at

        wide_at, narrow_at = {}, {}
        nw = nn = 0
        for st in stages:
            wide_at[st], narrow_at[st] = nw, nn
            if st[0] == "M":
                nw += N_M[st]
            else:
                nw += 1 + NE
                nn += 1 + NE
        SOLVE1 = 1 if "M0" in stages else 0
        moe_no = {st: n for n, st in enumerate(s for s in stages if s[0] == "E")}

        roots = {"M0": ["attn1", "attn0", "kk", "group_norm"], "M1": ["qk0", "qk1", "qk2", "qk3", "gdn0", "gdn1"]}
        ROOT = {name: n + 1 for n, name in enumerate(x for st in stages for x in roots.get(st, []) + ["ln_" + st])}

        def inv_root(act, t, name):
            act.wait_ge(S["square_ready"], ROOT[name])
            nc.scalar.activation(t, t, ACT.Ln).then_inc(S["root_ready"], 1)
            act.wait_ge(S["root_ready"], 2 * ROOT[name] - 1)
            nc.scalar.activation(t, t, ACT.Exp, scale=-0.5).then_inc(S["root_ready"], 1)

        def w_load(n):
            return S[f"wide_loaded{n % RING}"], 48 * (n // RING + 1)

        def n_load(n):
            return S[f"narrow_loaded{n % RING}"], 16 * (n // RING + 1)

        def gu_view(slot, kt):
            return wide[:, slot, :].rearrange("p (g k f) -> p k g f", g=2, k=KT)[:, kt, :, :]

        M0_UNITS = 13
        raw = area(0, 14, SEQ + 1)
        mixT = area(3600, 14, SEQ)
        at_ = area(0, 16, 2 * P)
        bt_ = area(4096, 16, 2 * P)
        KR = area(8192, 4, 2, SEQ)
        betaT = area(10240, 4, SEQ)
        gammaT = area(11264, 4, SEQ)
        tm4 = area(12288, 4, TT, 512)
        beta_tm, gamma_tm, V_tm, kappa_tm = (tm4[:, i] for i in range(4))
        y_tok = area(16384, TT, D)
        g_tm = area(18432, TT, 512)
        qkT = area(8192, 8, SEQ)
        vA = area(10240, TT, 512)
        alibi = area(11264, 4, SEQ)
        sc = area(12288, 2, 4, SEQ)
        attn = area(14336, 4, SEQ)
        attnT = area(15360, 4, 2, P)
        small = 19456
        cols = area(small, 34)
        al = area(small + 34, 4, 64)
        ang = area(small + 290, P)
        ncols = area(small + 418, 8)
        lam2 = area(small + 426, 2)
        lam = area(small + 428, 1)
        smax = area(small + 429, 2, 4)
        ssum = area(small + 437, 2, 4)
        arms = area(small + 445, 4)
        bonus = area(small + 449, TT, 8)
        gmu = area(small + 465, 16)
        gvar = area(small + 481, 16)
        lamC = area(small + 497, 4, 4)
        lora = lng[:, 0:512]
        g2_sb = lng[:, 512:1024]
        lnxg = lnb[:, 0:512]
        lnxb = lnb[:, 512:1024]
        nflat = narrow[:, :, :].rearrange("p a b -> p (a b)")
        N = [area(1024 * i, 4, SEQ, base=nflat) for i in range(8)]
        X, XT_, T1, QT = (area(2048 * i, 16, P, base=nflat) for i in range(4))
        w12 = wide[:, 1:3, :].rearrange("p a b -> p (a b)")
        G_ = area(0, TT, 512, base=w12)
        BV = area(1024, TT, 512, base=w12)
        U_ = area(2048, TT, 512, base=w12)
        Yr = area(3072, TT, 8, 64, base=w12)
        XKT = area(4096, TT, 4, P, base=w12)
        Sbd = area(5120, 4, P, base=w12)
        Ytmp = area(5632, TT, 8, 64, base=w12)
        EM = math.exp(-0.5)
        STEP = {name: n + 1 for names in (
            ("lam_exp", "tanh_ready", "xg_exp", "g_copied", "bonus_ready", "bv_ready", "xk_ready"),
            ("lam_sums", "ncols_ready", "kk_squared", "xg_ready", "cum_ready", "rk_ready", "factors_ready", "g_ready"),
            ("g_done", "kk_norm", "bonus_done", "bv_done", "xg2_done", "xk_done")) for n, name in enumerate(names)}

        def wv(n, w):
            return wide[:, n % RING, 0:KT * w].rearrange("p (k c) -> p k c", k=KT)

        def unit0(h):
            return (h % 2) * 4 + h // 2

        def m0_loads(sp, wide_chunk):
            w_in = a["l0_w_in"].rearrange("(p k) c -> p k c", k=KT)
            n = wide_at["M0"]
            for c in range(7):
                wide_chunk(n + c, w_in[:, :, c * CH:min((c + 1) * CH, 3328)])
            w_out = a["l0_w_out"].rearrange("(p k) c -> p k c", k=KT)
            for c in range(2):
                wide_chunk(n + 7 + c, w_out[:, :, c * CH:(c + 1) * CH])
            sp.wait_ge(S["rwkv_out"], 1)

        def m0_params(pool):
            pool.dma_start(cols, a["l0_b_cols"]).then_inc(S["mixer_in"], 16)
            pool.dma_start(alibi, a["alibi"].rearrange("p (h k) -> p h k", h=4)).then_inc(S["mixer_in"], 16)
            pool.dma_start(al, a["l0_a_lambda"].rearrange("a b -> (a b)").partition_broadcast(P).rearrange("p (a b) -> p a b", a=4)
                           ).then_inc(S["mixer_in"], 16)
            pool.dma_start(ang, a["l0_a_norm_g"].partition_broadcast(P)).then_inc(S["mixer_in"], 16)
            pool.dma_start(lora[0:64, :], a["l0_b_w2"]).then_inc(S["mixer_in"], 16)
            pool.dma_start(lora[64:128, :], a["l0_b_a2"]).then_inc(S["mixer_in"], 16)
            pool.dma_start(g2_sb, a["l0_b_g2"]).then_inc(S["mixer_in"], 16)
            pool.dma_start(lnxg, a["l0_b_lnx_g"].partition_broadcast(P)).then_inc(S["mixer_in"], 16)
            pool.dma_start(lnxb, a["l0_b_lnx_b"].partition_broadcast(P)).then_inc(S["mixer_in"], 16)
            solve_pool(pool, 0, at_)
            pool.wait_ge(S["rwkv_out"], 1)

        M0_IN = 16 * 9

        def solve_pool(pool, s, AT):
            pool.wait_ge(S["AT_ready"], s + 1)
            for lv in range(LEVELS):
                for b in range(4):
                    if lv:
                        pool.wait_ge(S["T1_done"], 24 * s + 4 * (lv - 1) + b + 1)
                    if lv == 1:
                        pool.wait_ge(S["XT_ready"], 24 * s + b + 1)
                    nc.gpsimd.tensor_tensor(QT_of(s)[:, 4 * b:4 * b + 4, :], AT[:, 4 * b:4 * b + 4, 0:P],
                                            spread(cm(C_LVL + lv * P), 1, [P, 4, P]), ALU.mult).then_inc(S["QT_ready"], 1)

        def QT_of(s):
            return QT if s < SOLVE1 else QT1

        def X_of(s):
            return (X, XT_, T1) if s < SOLVE1 else (X1, XT1, T11)

        def solve_pe(pe, s):
            mm = nc.tensor.matmul
            X, XT, T1 = X_of(s)
            Q = QT_of(s)
            for b in range(4):
                pe.wait_ge(S["QT_ready"], 24 * s + b + 1)
                for u in range(4):
                    last = mm(ps[:, b, u * P:(u + 1) * P], Q[:, 4 * b + u, :], ident, start=True, stop=True)
                last.then_inc(S["T1_done"], 1)
            for lv in range(1, LEVELS):
                for b in range(4):
                    pe.wait_ge(S["QT_ready"], 24 * s + 4 * lv + b + 1)
                    pe.wait_ge(S["X_ready"], 20 * s + 4 * (lv - 1) + b + 1)
                    for u in range(4):
                        last = mm(ps[:, b, u * P:(u + 1) * P], Q[:, 4 * b + u, :], X[:, 4 * b + u, :], start=True, stop=True)
                    last.then_inc(S["T1_done"], 1)
                for b in range(4):
                    n = 4 * (lv - 1) + b
                    pe.wait_ge(S["T1_ready"], 20 * s + n + 1)
                    pe.wait_ge(S["XT_ready"], 24 * s + 4 * lv + max(b - 1, 0) if b >= 2 else 24 * s + 4 * (lv - 1) + 4)
                    if lv < LEVELS - 1:
                        for u in range(4):
                            last = mm(ps[:, 4 + 2 * (b % 2), u * P:(u + 1) * P], XT[:, 4 * b + u, :], T1[:, 4 * b + u, :],
                                      start=True, stop=True)
                        last.then_inc(S["XQX_done"], 1)
                    for u in range(4):
                        last = mm(ps[:, 5 + 2 * (b % 2), u * P:(u + 1) * P], T1[:, 4 * b + u, :], XT[:, 4 * b + u, :],
                                  start=True, stop=True)
                    last.then_inc(S["XQXT_done"], 1)

        def solve_act(act, s):
            T1 = X_of(s)[2]
            for lv in range(1, LEVELS):
                for b in range(4):
                    act.wait_ge(S["T1_done"], 24 * s + 4 * lv + b + 1)
                    nc.scalar.copy(T1[:, 4 * b:4 * b + 4, :], ps[:, b, :].rearrange("p (u c) -> p u c", u=4)
                                   ).then_inc(S["T1_ready"], 1)

        def solve_dve(dve, v, s):
            X, XT, T1 = X_of(s)
            Q = QT_of(s)
            for b in range(4):
                dve.wait_ge(S["QT_ready"], 24 * s + b + 1)
                v.scalar_tensor_tensor(out=XT[:, 4 * b:4 * b + 4, :], in0=Q[:, 4 * b:4 * b + 4, :], scalar=-1.0,
                                       in1=spread(ident, 1, [P, 4, P]), op0=ALU.mult, op1=ALU.add).then_inc(S["XT_ready"], 1)
                dve.wait_ge(S["T1_done"], 24 * s + b + 1)
                v.scalar_tensor_tensor(out=X[:, 4 * b:4 * b + 4, :], in0=ps[:, b, :].rearrange("p (u c) -> p u c", u=4), scalar=-1.0,
                                       in1=spread(ident, 1, [P, 4, P]), op0=ALU.mult, op1=ALU.add).then_inc(S["X_ready"], 1)
            for lv in range(1, LEVELS):
                for b in range(4):
                    blk = slice(4 * b, 4 * b + 4)
                    if lv < LEVELS - 1:
                        dve.wait_ge(S["XQX_done"], 16 * s + 4 * (lv - 1) + b + 1)
                        dve.wait_ge(S["X_ready"], 20 * s + 4 * (lv - 1) + b + 1)
                        v.tensor_tensor(X[:, blk, :], X[:, blk, :], ps[:, 4 + 2 * (b % 2), :].rearrange("p (u c) -> p u c", u=4),
                                        ALU.subtract).then_inc(S["X_ready"], 1)
                    dve.wait_ge(S["XQXT_done"], 20 * s + 4 * (lv - 1) + b + 1)
                    dve.wait_ge(S["XT_ready"], 24 * s + 4 * (lv - 1) + b + 1)
                    v.tensor_tensor(XT[:, blk, :], XT[:, blk, :], ps[:, 5 + 2 * (b % 2), :].rearrange("p (u c) -> p u c", u=4),
                                    ALU.subtract).then_inc(S["XT_ready"], 1)

        def m0_pe(pe):
            mm = nc.tensor.matmul
            base = wide_at["M0"]

            def unit(u):
                n = base + u // 2
                w = CH if n < base + 6 else 256
                if u % 2 == 0:
                    pe.wait_ge(*w_load(n))
                if u >= 4:
                    pe.wait_ge(S["unit_out"], u - 3)
                wc = wv(n, w)
                off = (u % 2) * 256
                for half in range(2):
                    for kt in range(KT):
                        if u in (4, 5):
                            last = mm(ps[:, u % 4, half * 256:(half + 1) * 256], xT[:, kt, half * P:(half + 1) * P],
                                      wc[:, kt, off:off + 256], start=(kt == 0), stop=(kt == KT - 1))
                        else:
                            last = mm(ps[:, u % 4, half * 256:(half + 1) * 256], wc[:, kt, off + half * P:off + (half + 1) * P],
                                      xT[:, kt, :], start=(kt == 0), stop=(kt == KT - 1))
                last.then_inc(S["unit_done"], 1)

            def scores(qb):
                kw = (qb + 1) * P
                for h in range(4):
                    for c in range(2):
                        r = slice(64 * c, 64 * c + 64)
                        bank, col = (4 + 2 * c + h // 2, (h % 2) * kw) if qb else (4 + c, h * kw)
                        last = mm(ps[:, bank, col:col + kw], qkT[r, h, qb * P:(qb + 1) * P], qkT[r, 4 + h, 0:kw],
                                  start=True, stop=True)
                        if (h, c) == (3, 0):
                            last.then_inc(S["scores_done"], 1)
                last.then_inc(S["scores_done"], 1)

            def turn_attn(qb):
                pe.wait_ge(S["attn_ready"], 2 - qb)
                for h in range(4):
                    for kb in range(qb + 1):
                        bank, col = (6 + h // 2, (h % 2) * 2 * P + kb * P) if qb else (5, h * P)
                        last = nc.tensor.transpose(ps[:, bank, col:col + P], attn[:, h, kb * P:(kb + 1) * P], ident)
                last.then_inc(S["attn_turned"], 1)

            def attend(qb):
                pe.wait_ge(S["attnT_ready"], 2 - qb)
                bank = 4 if qb else 6
                for h in range(4):
                    for kb in range(qb + 1):
                        last = mm(ps[:, bank, h * P:(h + 1) * P], attnT[:, h, kb, :], vA[:, kb, h * P:(h + 1) * P],
                                  start=(kb == 0), stop=(kb == qb))
                last.then_inc(S["attended"], 1)

            for u in range(6):
                unit(u)
            pe.wait_ge(S["unit_out"], 6)
            scores(1)
            unit(6)
            unit(7)
            pe.wait_ge(S["scores_read"], 1)
            scores(0)
            unit(8)
            unit(9)
            turn_attn(1)
            unit(10)
            attend(1)
            turn_attn(0)
            unit(11)
            unit(12)
            attend(0)
            pe.wait_ge(S["mixer_in"], M0_IN)
            pe.wait_ge(S["scalar_step"], STEP["tanh_ready"])
            pe.wait_ge(S["attention_out"], 2)
            for t in range(4):
                for r in range(2):
                    rows = slice(64 * r, 64 * r + 64)
                    last = mm(ps[:, 4 + 2 * r + t // 2, (t % 2) * SEQ:(t % 2 + 1) * SEQ], lora[rows, t * P:(t + 1) * P],
                              mixT[rows, 12, :], start=True, stop=True)
                    if (t, r) == (3, 0):
                        last.then_inc(S["lora_done"], 1)
            last.then_inc(S["lora_done"], 1)
            pe.wait_ge(S["vector_step"], STEP["xg_ready"])
            for tt in range(TT):
                last = mm(ps[:, tt, :], mixT[:, 13, tt * P:(tt + 1) * P], g2_sb, start=True, stop=True)
            last.then_inc(S["tensor_step"], 1)
            pe.wait_ge(S["vector_step"], STEP["kk_squared"])
            for t in range(4):
                last = mm(ps[:, 2 + t // 2, (t % 2) * SEQ:(t % 2 + 1) * SEQ], cm(C_HALF), N[7][:, t, :], start=True, stop=True)
            last.then_inc(S["tensor_step"], 1)
            pe.wait_ge(S["vector_step"], STEP["rk_ready"])
            pe.wait_ge(S["decay_exp"], 8)
            for tt in range(TT):
                for t in range(4):
                    last = mm(ps[:, 4, tt * 8:(tt + 1) * 8], N[6][:, t, tt * P:(tt + 1) * P], cst[:, C_HEAD + 8 * t:C_HEAD + 8 * t + 8],
                              start=(t == 0), stop=(t == 3))
            last.then_inc(S["tensor_step"], 1)
            for q, src in enumerate((betaT, gammaT, mixT[:, 8:12, :], KR[:, :, 0, :])):
                if q == 0:
                    pe.wait_ge(S["vector_step"], STEP["factors_ready"])
                    pe.wait_ge(S["scalar_step"], STEP["g_copied"])
                    pe.wait_ge(S["scalar_step"], STEP["bonus_ready"])
                for tt in range(TT):
                    for t in range(4):
                        last = nc.tensor.transpose(ps[:, 2 * q + tt, t * P:(t + 1) * P], src[:, t, tt * P:(tt + 1) * P], ident)
                    last.then_inc(S["factors_turned"], 1)
            for i, src in enumerate((betaT, gammaT)):
                for tt in range(TT):
                    if i == 0:
                        pe.wait_ge(S["tm_ready"], 4 + 4 * tt)
                    else:
                        pe.wait_ge(S["pairs_out"], tt + 1)
                    for t in range(4):
                        for par in range(2):
                            rows = slice(64 * par, 64 * par + 64)
                            last = mm(ps[:, 4 * tt + 2 * par + t // 2, (t % 2) * 256:(t % 2 + 1) * 256],
                                      src[rows, t, tt * P:(tt + 1) * P], KR[rows, t, :, tt * P:(tt + 1) * P], start=True, stop=True)
                            if (t, par) == (3, 0):
                                last.then_inc(S["pairs_done"], 1)
                    last.then_inc(S["pairs_done"], 1)
            pe.wait_ge(S["pairs_out"], 4)
            for tt in range(TT):
                for h in range(8):
                    last = mm(ps[:, tt, h * 64:(h + 1) * 64], bt_[:, tt * 8 + unit0(h), 0:P], V_tm[:, tt, h * 64:(h + 1) * 64],
                              start=True, stop=True)
            last.then_inc(S["tensor_step"], 1)
            pe.wait_ge(S["scalar_step"], STEP["bv_ready"])
            solve_pe(pe, 0)
            pe.wait_ge(S["XT_ready"], 24)
            for tt in range(TT):
                for h in range(8):
                    last = mm(ps[:, tt, h * 64:(h + 1) * 64], XT_[:, tt * 8 + unit0(h), :], BV[:, tt, h * 64:(h + 1) * 64],
                              start=True, stop=True)
            last.then_inc(S["tensor_step"], 1)
            for tt in range(TT):
                for h in range(8):
                    p0 = 64 * (h % 2)
                    last = mm(ps[p0:p0 + 64, 2 + tt, (h // 2) * P:(h // 2 + 1) * P], kappa_tm[:, tt, h * 64:(h + 1) * 64],
                              XT_[:, tt * 8 + unit0(h), :], start=True, stop=True)
            last.then_inc(S["tensor_step"], 1)
            pe.wait_ge(S["vector_step"], STEP["g_ready"])
            for c in range(4):
                tt, r0 = c // 2, 64 * (c % 2)
                pe.wait_ge(S["state_ready"], c + 1)
                for t in range(4):
                    last = mm(ps[r0:r0 + 64, 4, t * P:(t + 1) * P], XKT[:, tt, t, r0:r0 + 64], Sbd[:, t, :], start=True, stop=True)
                last.then_inc(S["u_done"], 1)
                for t in range(4):
                    last = mm(ps[r0:r0 + 64, 6 + tt, t * P:(t + 1) * P], KR[:, t, 1, c * 64:(c + 1) * 64], Sbd[:, t, :],
                              start=(t == 0), stop=False, skip_group_check=True)
                last.then_inc(S["state_used"], 1)
                for h in range(8):
                    mm(ps[r0:r0 + 64, 6 + tt, h * 64:(h + 1) * 64], bt_[:, tt * 8 + unit0(h), P + r0:P + r0 + 64],
                       V_tm[:, tt, h * 64:(h + 1) * 64], start=False, stop=False, skip_group_check=True)
                pe.wait_ge(S["u_ready"], c + 1)
                if c < 3:
                    rows = slice(r0, r0 + 64)
                    for h in range(8):
                        p0 = 64 * (h % 2)
                        o = ps[p0:p0 + 64, 5, (h // 2) * 64:(h // 2 + 1) * 64]
                        hc = slice(h * 64, (h + 1) * 64)
                        mm(o, gamma_tm[rows, tt, hc], V_tm[rows, tt, hc], start=True, stop=False)
                        last = mm(o, beta_tm[rows, tt, hc], U_[rows, tt, hc], start=False, stop=True)
                    last.then_inc(S["incr_done"], 1)
                for h in range(8):
                    last = mm(ps[r0:r0 + 64, 6 + tt, h * 64:(h + 1) * 64], at_[:, tt * 8 + unit0(h), P + r0:P + r0 + 64],
                              U_[:, tt, h * 64:(h + 1) * 64], start=False, stop=(h == 7), skip_group_check=True)
                last.then_inc(S["y_done"], 1)
            pe.wait_ge(S["rwkv_out"], 1)
            for b in range(4):
                tt, half = divmod(b, 2)
                for k in range(4):
                    last = nc.tensor.transpose(ps[:, 4 + b, k * P:(k + 1) * P], y_tok[:, tt, 4 * half + k::KT], ident)
                last.then_inc(S["outs_turned"], 1)
            pe.wait_ge(S["outsT_ready"], 4)
            for h in range(2):
                n = base + 7 + h
                pe.wait_ge(*w_load(n))
                for tt in range(TT):
                    for kt in range(KT):
                        last = mm(ps[:, 2 * tt + h, :], xT[:, kt, tt * P:(tt + 1) * P], wv(n, CH)[:, kt, :],
                                  start=(kt == 0), stop=(kt == KT - 1))
                last.then_inc(S["wide_used"], 1)
                if h == 0:
                    continue

        def m0_act(act):
            A_ = nc.scalar.activation

            def unit_out(u):
                act.wait_ge(S["unit_done"], u + 1)
                if u % 2 or u == M0_UNITS - 1:
                    act.sem_inc(S["wide_used"], 1)
                src = ps[:, u % 4, :].rearrange("p (t c) -> p t c", t=2)
                if u < 4:
                    nc.scalar.mul(qkT[:, 2 * u:2 * u + 2, :], src, 0.125 if u < 2 else 1.0).then_inc(S["unit_out"], 1)
                elif u < 6:
                    nc.scalar.copy(vA[:, :, (u - 4) * 256:(u - 3) * 256], src).then_inc(S["unit_out"], 1)
                else:
                    nc.scalar.copy(raw[:, 2 * (u - 6):2 * (u - 6) + 2, 1:SEQ + 1], src).then_inc(S["unit_out"], 1)

            def softmax_exp(qb):
                act.wait_ge(S["shifted"], 2 - qb)
                kw = (qb + 1) * P
                A_(sc[:, :, :, 0:kw], sc[:, :, :, 0:kw], ACT.Exp).then_inc(S["probs_ready"], 1)

            for u in range(6):
                unit_out(u)
            act.wait_ge(S["vector_step"], STEP["lam_sums"])
            A_(lam2, lam2, ACT.Exp).then_inc(S["scalar_step"], 1)
            softmax_exp(1)
            unit_out(6)
            unit_out(7)
            softmax_exp(0)
            for u in (8, 9, 10):
                unit_out(u)
            inv_root(act, arms, "attn1")
            unit_out(11)
            unit_out(12)
            inv_root(act, arms, "attn0")
            act.wait_ge(S["mixed_units"], 7)
            A_(mixT[0:64, 12, :], mixT[0:64, 12, :], ACT.Tanh).then_inc(S["scalar_step"], 1)
            A_(mixT[:, 13, :], mixT[:, 13, :], ACT.Exp, scale=-1.0).then_inc(S["scalar_step"], 1)
            act.wait_ge(S["vector_step"], STEP["ncols_ready"])
            for r in range(2):
                act.wait_ge(S["lora_done"], r + 1)
                for t in range(4):
                    A_(N[2 * r][:, t, :], ps[:, 4 + 2 * r + t // 2, (t % 2) * SEQ:(t % 2 + 1) * SEQ], ACT.Exp,
                       bias=ncols[:, 4 * r + t:4 * r + t + 1], scale=-1.0).then_inc(S["decay_exp"], 1)
            act.wait_ge(S["tensor_step"], STEP["g_done"])
            nc.scalar.copy(g_tm, ps[:, 0:2, :]).then_inc(S["scalar_step"], 1)
            inv_root(act, N[7], "kk")
            act.wait_ge(S["vector_step"], STEP["cum_ready"])
            A_(N[0], N[0], ACT.Exp, scale=-EM).then_inc(S["decays"], 1)
            A_(N[5], N[1], ACT.Exp, scale=-EM).then_inc(S["decays"], 1)
            act.wait_ge(S["decays"], 2)
            A_(N[1], N[1], ACT.Exp, scale=EM).then_inc(S["decays"], 1)
            act.wait_ge(S["tensor_step"], STEP["bonus_done"])
            nc.scalar.copy(bonus, ps[:, 4, 0:16].rearrange("p (t h) -> p t h", t=TT)).then_inc(S["scalar_step"], 1)
            for q in range(4):
                act.wait_ge(S["factors_turned"], 2 * q + 1)
                nc.scalar.copy(tm4[:, q, 0, :], ps[:, 2 * q, :]).then_inc(S["tm_a"], 1)
            act.wait_ge(S["tensor_step"], STEP["bv_done"])
            nc.scalar.copy(BV, ps[:, 0:2, :]).then_inc(S["scalar_step"], 1)
            solve_act(act, 0)
            act.wait_ge(S["tensor_step"], STEP["xk_done"])
            nc.scalar.copy(XKT, ps[:, 2:4, :].rearrange("p a (t c) -> p a t c", t=4)).then_inc(S["scalar_step"], 1)
            inv_root(act, gvar, "group_norm")
            for b in (0, 2):
                act.wait_ge(S["outs_turned"], b + 1)
                nc.scalar.copy(xT[:, 4 * (b % 2):4 * (b % 2) + 4, (b // 2) * P:(b // 2 + 1) * P],
                               ps[:, 4 + b, :].rearrange("p (k t) -> p k t", k=4)).then_inc(S["outsT_ready"], 1)

        def m0_dve(dve, v, link):
            ts_, tt_, stt = v.tensor_scalar, v.tensor_tensor, v.scalar_tensor_tensor

            def bc(c0, n=4):
                return spread(cols[:, c0:c0 + n], 2, [P, n, SEQ])

            def mix_unit(u):
                i = 2 * (u - 6)
                dve.wait_ge(S["unit_out"], u + 1)
                link(tt_(mixT[:, i:i + 2, :], raw[:, i:i + 2, 0:SEQ], raw[:, i:i + 2, 1:SEQ + 1], ALU.subtract))
                for t in (i, i + 1):
                    last = stt(out=mixT[:, t, :], in0=mixT[:, t, :], scalar=cols[:, t:t + 1], in1=raw[:, t, 1:SEQ + 1],
                               op0=ALU.mult, op1=ALU.add)
                    if t == i:
                        link(last)
                last.then_inc(S["mixed_units"], 1)

            def softmax_a(qb):
                kw = (qb + 1) * P
                k0 = (1 - qb) * P
                dve.wait_ge(S["scores_done"], 4 - 2 * qb)
                if qb == 0:
                    dve.wait_ge(S["attn_ready"], 1)
                for c in range(2):
                    if qb:
                        src = ps[:, 4 + 2 * c:6 + 2 * c, :].rearrange("p b (h k) -> p (b h) k", h=2)
                    else:
                        src = ps[:, 4 + c, :].rearrange("p (h k) -> p h k", h=4)
                    last = tt_(sc[:, c, :, 0:kw], src, alibi[:, :, k0:k0 + kw], ALU.add)
                    if c == 0:
                        link(last)
                last.then_inc(S["scores_read"], 1)
                dve.wait_ge(S["scores_read"], 2 - qb)
                link(v.tensor_reduce(smax, sc[:, :, :, 0:kw], AX, ALU.max))
                for c in range(2):
                    last = tt_(sc[:, c, :, 0:kw], sc[:, c, :, 0:kw], spread(smax[:, c, :], 2, [P, 4, kw]), ALU.subtract)
                    if c == 0:
                        link(last)
                last.then_inc(S["shifted"], 1)

            def softmax_b(qb):
                kw = (qb + 1) * P
                dve.wait_ge(S["probs_ready"], 2 - qb)
                link(v.tensor_reduce(ssum, sc[:, :, :, 0:kw], AX, ALU.add))
                link(v.reciprocal(ssum, ssum))
                link(ts_(ssum[:, 1, :], ssum[:, 1, :], lam[:, 0:1], None, ALU.mult))
                for c in range(2):
                    link(tt_(sc[:, c, :, 0:kw], sc[:, c, :, 0:kw], spread(ssum[:, c, :], 2, [P, 4, kw]), ALU.mult))
                if qb == 0:
                    dve.wait_ge(S["attn_turned"], 1)
                tt_(attn[:, :, 0:kw], sc[:, 0, :, 0:kw], sc[:, 1, :, 0:kw], ALU.subtract).then_inc(S["attn_ready"], 1)

            def attnT_out(qb):
                dve.wait_ge(S["attn_turned"], 2 - qb)
                if qb:
                    v.tensor_copy(attnT, ps[:, 6:8, :].rearrange("p b (h k c) -> p (b h) k c", h=2, k=2)).then_inc(S["attnT_ready"], 1)
                else:
                    dve.wait_ge(S["attended"], 1)
                    v.tensor_copy(attnT[:, :, 0, :], ps[:, 5, :].rearrange("p (h c) -> p h c", h=4)).then_inc(S["attnT_ready"], 1)

            def head_norm(qb):
                dve.wait_ge(S["attended"], 2 - qb)
                o = y_tok[:, qb, 0:512]
                o3 = o.rearrange("p (h c) -> p h c", h=4)
                sq = y_tok[:, qb, 512:1024]
                link(v.tensor_copy(o, ps[:, 4 if qb else 6, :]))
                link(tt_(sq, o, o, ALU.mult))
                link(v.tensor_reduce(arms, sq.rearrange("p (h c) -> p h c", h=4), AX, ALU.add))
                ts_(arms, arms, 1.0 / P, 1e-5, ALU.mult, ALU.add).then_inc(S["square_ready"], 1)
                dve.wait_ge(S["root_ready"], 2 * ROOT[f"attn{qb}"])
                link(tt_(o3, o3, spread(arms, 2, [P, 4, P]), ALU.mult))
                tt_(o3, o3, spread(ang, 1, [P, 4, P]), ALU.mult).then_inc(S["attention_out"], 1)
                dve.wait_ge(S["attention_out"], 2 - qb)

            link(v.memset(raw[:, :, 0:1], 0.0))
            dve.wait_ge(S["mixer_in"], M0_IN)
            link(tt_(al[:, 0::2, :], al[:, 0::2, :], al[:, 1::2, :], ALU.mult))
            v.tensor_reduce(lam2, al[:, 0::2, :], AX, ALU.add).then_inc(S["vector_step"], 1)
            dve.wait_ge(S["scalar_step"], STEP["lam_exp"])
            LAM0 = 0.8 - 0.6 * math.exp(-0.3 * 0)
            link(ts_(lam, lam2[:, 0:1], lam2[:, 1:2], LAM0, ALU.subtract, ALU.add))
            link(ts_(ang, ang, 1.0 - LAM0, None, ALU.mult))
            ts_(ncols, cols[:, 14:22], -1.0, None, ALU.mult).then_inc(S["vector_step"], 1)
            softmax_a(1)
            softmax_b(1)
            softmax_a(0)
            mix_unit(6)
            mix_unit(7)
            attnT_out(1)
            softmax_b(0)
            mix_unit(8)
            mix_unit(9)
            attnT_out(0)
            head_norm(1)
            mix_unit(10)
            head_norm(0)
            mix_unit(11)
            mix_unit(12)
            dve.wait_ge(S["mixed_units"], 7)
            rT, kT = mixT[:, 0:4, :], mixT[:, 4:8, :]
            link(tt_(N[3], kT, bc(22), ALU.mult))
            tt_(N[7], N[3], N[3], ALU.mult).then_inc(S["vector_step"], 1)
            dve.wait_ge(S["scalar_step"], STEP["xg_exp"])
            link(ts_(mixT[:, 13, :], mixT[:, 13, :], 1.0, None, ALU.add))
            v.reciprocal(mixT[:, 13, :], mixT[:, 13, :]).then_inc(S["vector_step"], 1)
            dve.wait_ge(S["decay_exp"], 4)
            link(ts_(N[0], N[0], 1.0, None, ALU.add))
            link(v.reciprocal(N[0], N[0]))
            for t in range(4):
                for c in range(4):
                    cc = slice(64 * c, 64 * c + 64)
                    link(v.tensor_tensor_scan(N[1][:, t, cc], cst[:, C_ONES:C_ONES + 64], N[0][:, t, cc], 0.0, ALU.mult, ALU.add))
            tt_(N[0], N[1], N[0], ALU.subtract).then_inc(S["vector_step"], 1)
            dve.wait_ge(S["tensor_step"], STEP["kk_norm"])
            ts_(N[7], ps[:, 2:4, :].rearrange("p b (t c) -> p (b t) c", t=2), 1e-6, None, ALU.add).then_inc(S["square_ready"], 1)
            dve.wait_ge(S["decay_exp"], 8)
            link(ts_(N[2], N[2], 1.0, None, ALU.add))
            link(v.reciprocal(N[2], N[2]))
            for t in range(4):
                link(ts_(N[4][:, t, :], N[2][:, t, :], 1.0, cols[:, 26 + t:27 + t], ALU.subtract, ALU.mult))
            link(stt(out=N[4], in0=N[4], scalar=1.0, in1=kT, op0=ALU.add, op1=ALU.mult))
            link(tt_(N[6], rT, N[4], ALU.mult))
            tt_(N[6], N[6], bc(30), ALU.mult).then_inc(S["vector_step"], 1)
            dve.wait_ge(S["root_ready"], 2 * ROOT["kk"])
            link(tt_(N[3], N[3], N[7], ALU.mult))
            dve.wait_ge(S["decays"], 3)
            link(tt_(KR[:, :, 0, :], N[0], N[3], ALU.mult))
            link(tt_(KR[:, :, 1, :], N[5], rT, ALU.mult))
            link(tt_(N[3], N[3], N[2], ALU.mult))
            link(tt_(betaT, N[3], N[1], ALU.mult))
            link(v.tensor_copy(lamC, N[5][:, :, 63::64]))
            tt_(gammaT, N[4], N[1], ALU.mult).then_inc(S["vector_step"], 1)
            for q in range(4):
                dve.wait_ge(S["factors_turned"], 2 * q + 2)
                dve.wait_ge(S["tm_a"], q + 1)
                v.tensor_copy(tm4[:, q, 1, :], ps[:, 2 * q + 1, :]).then_inc(S["tm_ready"], 2)
            mask = spread(cst[:, C_STRICT:C_STRICT + 2 * P], 1, [P, 8, 2 * P])
            for i, dst in enumerate((at_, bt_)):
                for tt in range(TT):
                    dve.wait_ge(S["pairs_done"], 2 * (2 * i + tt) + 2)
                    tt_(dst[:, 8 * tt:8 * tt + 8, :], ps[:, 4 * tt:4 * tt + 4, :].rearrange("p b (u c) -> p (b u) c", u=2), mask, ALU.mult
                        ).then_inc(S["pairs_out"], 1)
                if i == 0:
                    dve.wait_ge(S["pairs_out"], 2)
                    v.engine_nop().then_inc(S["AT_ready"], 1)
            solve_dve(dve, v, 0)
            dve.wait_ge(S["tensor_step"], STEP["xg2_done"])
            v.tensor_copy(G_, ps[:, 0:2, :]).then_inc(S["vector_step"], 1)
            link(v.memset(U_, 0.0))
            dve.wait_ge(S["vector_step"], STEP["g_ready"])
            dve.wait_ge(S["scalar_step"], STEP["xk_ready"])
            v.memset(Sbd, 0.0).then_inc(S["state_ready"], 1)
            for c in range(4):
                tt, r0 = c // 2, 64 * (c % 2)
                rows = slice(r0, r0 + 64)
                dve.wait_ge(S["u_done"], c + 1)
                stt(out=U_[rows, tt, :], in0=ps[rows, 4, :], scalar=-1.0, in1=G_[rows, tt, :], op0=ALU.mult, op1=ALU.subtract
                    ).then_inc(S["u_ready"], 1)
                if c < 3:
                    dve.wait_ge(S["state_used"], c + 1)
                    dve.wait_ge(S["incr_done"], c + 1)
                    for par in range(2):
                        pr = slice(64 * par, 64 * par + 64)
                        s_ = Sbd[pr, :, 64 * par:64 * par + 64]
                        link(tt_(s_, s_, ps[pr, 5, 0:256].rearrange("p (t c) -> p t c", t=4), ALU.add))
                        last = tt_(s_, s_, spread(lamC[pr, :, c], 2, [64, 4, 64]), ALU.mult)
                        if par == 0:
                            link(last)
                    last.then_inc(S["state_ready"], 1)
                    dve.wait_ge(S["state_ready"], c + 2)
                if c % 2:
                    dve.wait_ge(S["y_done"], c + 1)
                    link(v.tensor_copy(Yr[:, tt], ps[:, 6 + tt, :].rearrange("p (h c) -> p h c", h=8)))
            Y = Yr.rearrange("p t h c -> p (t h) c")
            Yt = Ytmp.rearrange("p t h c -> p (t h) c")
            link(v.tensor_reduce(gmu, Y, AX, ALU.add))
            link(ts_(gmu, gmu, 1.0 / 64, None, ALU.mult))
            link(tt_(Y, Y, spread(gmu, 2, [P, 16, 64]), ALU.subtract))
            link(tt_(Yt, Y, Y, ALU.mult))
            link(v.tensor_reduce(gvar, Yt, AX, ALU.add))
            ts_(gvar, gvar, 1.0 / 64, 64e-5, ALU.mult, ALU.add).then_inc(S["square_ready"], 1)
            dve.wait_ge(S["scalar_step"], STEP["bonus_ready"])
            link(tt_(Yt, V_tm.rearrange("p t (h c) -> p (t h) c", h=8), spread(bonus.rearrange("p t h -> p (t h)"), 2, [P, 16, 64]), ALU.mult))
            dve.wait_ge(S["root_ready"], 2 * ROOT["group_norm"])
            link(tt_(Y, Y, spread(gvar, 2, [P, 16, 64]), ALU.mult))
            Y2, Yt2 = (z.rearrange("p t h c -> p t (h c)") for z in (Yr, Ytmp))
            link(tt_(Y2, Y2, spread(lnxg, 1, [P, TT, 512]), ALU.mult))
            link(tt_(Y2, Y2, spread(lnxb, 1, [P, TT, 512]), ALU.add))
            link(tt_(Y2, Y2, Yt2, ALU.add))
            dve.wait_ge(S["scalar_step"], STEP["g_copied"])
            tt_(y_tok[:, :, 512:1024], Y2, g_tm, ALU.mult).then_inc(S["rwkv_out"], 1)
            for b in (1, 3):
                dve.wait_ge(S["outs_turned"], b + 1)
                v.tensor_copy(xT[:, 4 * (b % 2):4 * (b % 2) + 4, (b // 2) * P:(b // 2 + 1) * P],
                              ps[:, 4 + b, :].rearrange("p (k t) -> p k t", k=4)).then_inc(S["outsT_ready"], 1)
            dve.wait_ge(S["wide_used"], RING + wide_at["M0"] + 9)

        M1_UNITS, VH, KH = 24, 16, 8
        qkF = area(0, 16, SEQ)
        yT16 = area(0, 16, SEQ)
        k_tm = area(4096, TT, KH, P)
        v_tm = area(6144, TT, VH, P)
        z_tm = area(10240, TT, VH, P)
        aT_ = area(14336, VH, P)
        St = area(16384, VH, P)
        craw = area(16384, 2, 2, SEQ + 4)
        cacc = area(17424, 2, 2, SEQ)
        ccols = area(18448, 32, 4)
        o_ms = area(18576, TT, VH)
        lngf = lng[:, :]
        w_ba = area(0, KT, 32, base=lngf)
        ong = area(256, P, base=lngf)
        alog = area(384, VH, base=lngf)
        dtb = area(400, VH, base=lngf)
        beta = area(416, TT, VH, base=lngf)
        xa = area(448, TT, VH, base=lngf)
        ab = area(480, TT, VH, base=lngf)
        gg = area(512, TT, VH, base=lngf)
        gcs = area(544, TT, VH, base=lngf)
        eg = area(576, TT, VH, base=lngf)
        kd = area(608, TT, VH, base=lngf)
        bg = area(640, TT, VH, base=lngf)
        glb = area(672, 4, VH, base=lngf)
        wflat = wide[:, :, :].rearrange("p a b -> p (a b)")
        X1, XT1, T11, QT1, AT1, vb, kbg, Ed = (area(2048 * i, VH, P, base=wflat) for i in range(8))
        Dr, A1, at1 = X1, XT1, T11
        u_, wT, kdec, vnew = (area(2048 * i, VH, P, base=nflat) for i in range(4))
        M1_IN = 16 * 5
        had = 1 if "M0" in stages else 0
        U0, P0, B3, B4 = 13 * had, M0_IN * had, 3 * had, 4 * had

        def m1_loads(sp, wide_chunk):
            w_in = a["l1_w_in"].rearrange("(p k) c -> p k c", k=KT)
            n = wide_at["M1"]
            for c in range(12):
                wide_chunk(n + c, w_in[:, :, c * CH:(c + 1) * CH])
            w_out = a["l1_w_out"].rearrange("(p k) c -> p k c", k=16)
            sp.wait_ge(S["uw_out"], 4)
            for c in range(4):
                wide_chunk(n + 12 + c, w_out[:, 4 * c:4 * c + 4, :])
            sp.wait_ge(S["gdn_out"], 2)

        def m1_params(pool):
            if len(stages) > 1 and stages[0] != "M1":
                pool.wait_ge(S["ln_done"], stages.index("M1"))
            pool.dma_start(w_ba, a["l1_w_in"].rearrange("(p k) c -> p k c", k=KT)[:, :, 6144:6176]).then_inc(S["mixer_in"], 16)
            pool.dma_start(ccols, a["l1_conv_cols"].rearrange("p (t j) -> p t j", j=4)).then_inc(S["mixer_in"], 16)
            pool.dma_start(ong, a["l1_norm_g"].partition_broadcast(P)).then_inc(S["mixer_in"], 16)
            pool.dma_start(alog, a["l1_a_log"].partition_broadcast(P)).then_inc(S["mixer_in"], 16)
            pool.dma_start(dtb, a["l1_dt_bias"].partition_broadcast(P)).then_inc(S["mixer_in"], 16)
            TTg = nc.gpsimd.tensor_tensor
            for r in range(2):
                pool.wait_ge(S["gates_ready"], 1)
                pool.wait_ge(S["unit_out"], U0 + M1_UNITS)
                if r:
                    pool.wait_ge(S["uw_out"], 2)
                for b in range(4):
                    TTg(Dr[:, 4 * b:4 * b + 4, :], spread(cm(C_SEG), 1, [P, 4, P]),
                        spread(gg[:, r, 4 * b:4 * b + 4], 2, [P, 4, P]), ALU.mult).then_inc(S["seg_ready"], 1)
                kk = spread(k_tm[:, r], 2, [P, KH, 2, P])
                pool.wait_ge(S["k_tm_ready"], 4)
                TTg(kbg.rearrange("p (h r) c -> p h r c", r=2), kk,
                    spread(bg[:, r, :].rearrange("p (h r) -> p h r", r=2), 3, [P, KH, 2, P]), ALU.mult).then_inc(S["kbg_ready"], 1)
                if r:
                    pool.wait_ge(S["incr_done"], B3 + 8)
                TTg(kdec.rearrange("p (h r) c -> p h r c", r=2), kk,
                    spread(kd[:, r, :].rearrange("p (h r) -> p h r", r=2), 3, [P, KH, 2, P]), ALU.mult).then_inc(S["kdec_ready"], 1)
                solve_pool(pool, SOLVE1 + r, AT1)
            pool.wait_ge(S["gdn_out"], 2)

        def m1_pe(pe):
            mm = nc.tensor.matmul
            tr = nc.tensor.transpose
            base = wide_at["M1"]
            pe.wait_ge(S["mixer_in"], P0 + M1_IN)
            for tt in range(TT):
                for kt in range(KT):
                    last = mm(ps[:, 5, tt * 32:(tt + 1) * 32], xT[:, kt, tt * P:(tt + 1) * P], w_ba[:, kt, :],
                              start=(kt == 0), stop=(kt == KT - 1))
            last.then_inc(S["ba_done"], 1)

            def unit(u):
                n = base + u // 2
                if u % 2 == 0:
                    pe.wait_ge(*w_load(n))
                if u >= 4:
                    pe.wait_ge(S["unit_out"], U0 + u - 3)
                wc = wv(n, CH)
                off = (u % 2) * 256
                for half in range(2):
                    for kt in range(KT):
                        if u >= 16:
                            last = mm(ps[:, u % 4, half * 256:(half + 1) * 256], xT[:, kt, half * P:(half + 1) * P],
                                      wc[:, kt, off:off + 256], start=(kt == 0), stop=(kt == KT - 1))
                        else:
                            last = mm(ps[:, u % 4, half * 256:(half + 1) * 256], wc[:, kt, off + half * P:off + (half + 1) * P],
                                      xT[:, kt, :], start=(kt == 0), stop=(kt == KT - 1))
                last.then_inc(S["unit_done"], 1)

            for u in range(M1_UNITS):
                unit(u)
                if u == 1:
                    pe.wait_ge(S["gates_ready"], 1)
                    for tt in range(TT):
                        mm(ps[:, 7, tt * VH:(tt + 1) * VH], cm(C_INCL), gg[:, tt, :], start=True, stop=True)
                        mm(ps[:, 7, (2 + tt) * VH:(3 + tt) * VH], cm(C_HALF), gg[:, tt, :], start=True, stop=True)
                        for hf in range(2):
                            for o in range(2):
                                c = 2 * tt + hf
                                last = mm(ps[64 * o:64 * o + 64, 7, (4 + c) * VH:(5 + c) * VH],
                                          cst[:, C_HALF + 64 * hf:C_HALF + 64 * hf + 64], gg[:, tt, :], start=True, stop=True)
                    last.then_inc(S["gsums_done"], 1)
                if 9 <= u <= 16:
                    w = u - 1
                    pe.wait_ge(S["conv_act"], w + 1)
                    if w >= 10:
                        pe.wait_ge(S["v_out"], w - 9)
                    for tt in range(TT):
                        for t in range(2):
                            last = tr(ps[:, 4 + w % 2, tt * 256 + t * P:tt * 256 + (t + 1) * P], cacc[:, w % 2, t, tt * P:(tt + 1) * P], ident)
                    last.then_inc(S["v_turned"], 1)
                if 10 <= u < 14:
                    b = u - 10
                    pe.wait_ge(S["sq_ready"], b + 1)
                    if b:
                        pe.wait_ge(S["square_ready"], ROOT[f"qk{b - 1}"])
                    else:
                        pe.wait_ge(S["gsums_out"], 3)
                    for t in range(4):
                        last = mm(ps[:, 6 + t // 2, (t % 2) * SEQ:(t % 2 + 1) * SEQ], cm(C_ONES), N[b][:, t, :], start=True, stop=True)
                    last.then_inc(S["ss_done"], 1)
                if u in (18, 20):
                    b = (u - 18) // 2
                    pe.wait_ge(S["qk_normed"], 3 + b)
                    if b:
                        pe.wait_ge(S["k_tm_ready"], 2)
                    for tt in range(TT):
                        for t in range(4):
                            last = tr(ps[:, 6 + tt, t * P:(t + 1) * P], qkF[:, 8 + 4 * b + t, tt * P:(tt + 1) * P], ident)
                        last.then_inc(S["k_turned"], 1)
            for r in range(2):
                tok = slice(r * P, (r + 1) * P)
                for b in range(4):
                    pe.wait_ge(S["seg_ready"], 4 * r + b + 1)
                    if r == 0:
                        pe.wait_ge(S["unit_out"], U0 + M1_UNITS)
                    else:
                        pe.wait_ge(S["state_ready"], B4 + 8 + b + 1)
                    mm(ps[:, b, :], cm(C_INCL), Dr[:, 4 * b:4 * b + 4, :].rearrange("p u c -> p (u c)"), start=True, stop=True
                       ).then_inc(S["dsum_done"], 1)
                if r == 0:
                    pe.wait_ge(S["k_tm_ready"], 4)
                    pe.wait_ge(S["v_out"], 8)
                else:
                    pe.wait_ge(S["o_out"], 8)
                for i, q0 in enumerate((8, 0)):
                    for h in range(KH):
                        last = mm(ps[:, 4 + 2 * i + h // 4, (h % 4) * P:(h % 4 + 1) * P], qkF[:, q0 + h, tok], qkF[:, 8 + h, tok],
                                  start=True, stop=True)
                    last.then_inc(S["kkqk_done"], 1)
                for b in range(4):
                    pe.wait_ge(S["A_ready"], 4 * r + b + 1)
                    for t in range(4):
                        last = tr(ps[:, b, t * P:(t + 1) * P], A1[:, 4 * b + t, :], ident)
                    last.then_inc(S["A_turned"], 1)
                for b in range(4):
                    pe.wait_ge(S["at_ready"], 4 * r + 4)
                    for t in range(4):
                        last = tr(ps[:, 4 + b, t * P:(t + 1) * P], at1[:, 4 * b + t, :], ident)
                    last.then_inc(S["at_turned"], 1)
                pe.wait_ge(S["aT_out"], 4 * r + 4)
                solve_pe(pe, SOLVE1 + r)
                pe.wait_ge(S["XT_ready"], 24 * (SOLVE1 + r) + 24)
                pe.wait_ge(S["vb_ready"], r + 1)
                pe.wait_ge(S["kbg_ready"], r + 1)
                for b in range(4):
                    for t in range(4):
                        last = mm(ps[:, b, t * P:(t + 1) * P], XT1[:, 4 * b + t, :], vb[:, 4 * b + t, :], start=True, stop=True)
                    last.then_inc(S["u1_done"], 1)
                for b in range(4):
                    for t in range(4):
                        last = mm(ps[:, 4 + b, t * P:(t + 1) * P], kbg[:, 4 * b + t, :], XT1[:, 4 * b + t, :], start=True, stop=True)
                    last.then_inc(S["w1_done"], 1)
                pe.wait_ge(S["uw_out"], 2 * r + 2)
                pe.wait_ge(S["kdec_ready"], r + 1)
                for hf in range(2):
                    c = 2 * r + hf
                    r0 = 64 * hf
                    rows = slice(r0, r0 + 64)
                    for b in range(4):
                        pe.wait_ge(S["state_ready"], B4 + 4 * c + b + 1)
                        for t in range(4):
                            last = mm(ps[rows, b, t * P:(t + 1) * P], wT[:, 4 * b + t, rows], St[:, 4 * b + t, :], start=True, stop=True)
                        last.then_inc(S["wS_done"], 1)
                        if hf:
                            pe.wait_ge(S["o_out"], 4 * (c - 1) + b + 1)
                        for t in range(2):
                            last = mm(ps[rows, 4 + b, t * 2 * P:(t + 1) * 2 * P], qkF[:, 2 * b + t, c * 64:(c + 1) * 64],
                                      St[:, 4 * b + 2 * t:4 * b + 2 * t + 2, :].rearrange("p u c -> p (u c)"), start=True, stop=True)
                        last.then_inc(S["qS_done"], 1)
                    for b in range(4):
                        pe.wait_ge(S["vnew_ready"], 4 * c + b + 1)
                        for t in range(4):
                            last = mm(ps[:, b, t * P:(t + 1) * P], kdec[rows, 4 * b + t, :], vnew[rows, 4 * b + t, :], start=True, stop=True)
                        last.then_inc(S["incr_done"], 1)
                    for b in range(4):
                        pe.wait_ge(S["qS_read"], 4 * c + b + 1)
                        for t in range(4):
                            last = mm(ps[rows, 4 + b, t * P:(t + 1) * P], aT_[:, 4 * b + t, rows], vnew[:, 4 * b + t, :], start=True, stop=True)
                        last.then_inc(S["av_done"], 1)
            for i in range(8):
                tt, q = divmod(i, 4)
                pe.wait_ge(S["gdn_out"], tt + 1)
                if i == 0:
                    pe.wait_ge(S["state_ready"], B4 + 20)
                o2 = v_tm[:, tt].rearrange("p h c -> p (h c)")
                for k in range(4):
                    last = tr(ps[:, i, k * P:(k + 1) * P], o2[:, 4 * q + k::16], ident)
                last.then_inc(S["outs_turned"], 1)
            pe.wait_ge(S["outsT_ready"], B4 + 8)
            for j in range(4):
                n = base + 12 + j
                pe.wait_ge(*w_load(n))
                w4 = wide[:, n % RING, :].rearrange("p (k c) -> p k c", k=4)
                for tt in range(TT):
                    for h in range(2):
                        for k in range(4):
                            last = mm(ps[:, 2 * tt + h, :], yT16[:, 4 * j + k, tt * P:(tt + 1) * P], w4[:, k, h * 512:(h + 1) * 512],
                                      start=(j == 0 and k == 0), stop=(j == 3 and k == 3))
                last.then_inc(S["wide_used"], 1)

        def m1_act(act):
            A_ = nc.scalar.activation
            act.wait_ge(S["ba_done"], 1)
            ba = ps[:, 5, 0:64].rearrange("p (t c) -> p t c", t=TT)
            A_(beta, ba[:, :, 0:VH], ACT.Exp, scale=-1.0).then_inc(S["beta_exp"], 1)
            A_(alog, alog, ACT.Exp).then_inc(S["beta_exp"], 1)
            act.wait_ge(S["abs_ready"], 1)
            A_(ab, ab, ACT.Exp, scale=-1.0).then_inc(S["abs_exp"], 1)
            act.wait_ge(S["abs_ready"], 2)
            A_(ab, ab, ACT.Ln).then_inc(S["abs_exp"], 1)

            def silu_unit(u):
                act.wait_ge(S["conv_done"], u + 1)
                dst = qkF[:, 2 * u:2 * u + 2, :] if u < 8 else cacc[:, u % 2]
                A_(dst, cacc[:, u % 2], ACT.Silu).then_inc(S["conv_act"], 1)

            def v_unit(u):
                act.wait_ge(S["v_turned"], u - 7)
                nc.scalar.copy(v_tm[:, :, 2 * (u - 8):2 * (u - 8) + 2, :],
                               ps[:, 4 + u % 2, :].rearrange("p (a b c) -> p a b c", a=TT, b=2)).then_inc(S["v_out"], 1)

            for u in range(M1_UNITS):
                act.wait_ge(S["unit_done"], U0 + u + 1)
                if u % 2:
                    act.sem_inc(S["wide_used"], 1)
                if u < 16:
                    if u >= 2:
                        act.wait_ge(S["conv_done"], u - 1)
                    else:
                        act.wait_ge(S["craw_zero"], 1)
                    nc.scalar.copy(craw[:, u % 2, :, 3:SEQ + 3], ps[:, u % 4, :].rearrange("p (t c) -> p t c", t=2)
                                   ).then_inc(S["unit_out"], 1)
                else:
                    A_(z_tm[:, :, 2 * (u - 16):2 * (u - 16) + 2, :], ps[:, u % 4, :].rearrange("p (a b c) -> p a b c", a=TT, b=2),
                       ACT.Silu).then_inc(S["unit_out"], 1)
                if 1 <= u <= 16:
                    silu_unit(u - 1)
                if 10 <= u <= 17:
                    v_unit(u - 2)
                if u == 2:
                    act.wait_ge(S["gsums_done"], 1)
                    A_(eg, ps[:, 7, 0:2 * VH].rearrange("p (t h) -> p t h", t=TT), ACT.Exp).then_inc(S["gsums_out"], 1)
                    A_(glb, ps[:, 7, 4 * VH:8 * VH].rearrange("p (t h) -> p t h", t=4), ACT.Exp).then_inc(S["gsums_out"], 1)
                    act.wait_ge(S["kd_ready"], 1)
                    A_(kd, kd, ACT.Exp).then_inc(S["kd_exp"], 1)
                if 12 <= u < 16:
                    b = u - 12
                    inv_root(act, N[4 + b], f"qk{b}")
            for r in range(2):
                for b in range(4):
                    act.wait_ge(S["dsum_done"], 4 * r + b + 1)
                    A_(Ed[:, 4 * b:4 * b + 4, :], ps[:, b, :].rearrange("p (u c) -> p u c", u=4), ACT.Exp).then_inc(S["seg_exp"], 1)
                for b in range(4):
                    act.wait_ge(S["at_turned"], 4 * r + b + 1)
                    if r:
                        act.wait_ge(S["av_done"], 8)
                    nc.scalar.copy(aT_[:, 4 * b:4 * b + 4, :], ps[:, 4 + b, :].rearrange("p (u c) -> p u c", u=4)).then_inc(S["aT_out"], 1)
                solve_act(act, SOLVE1 + r)
                act.wait_ge(S["w1_done"], 4 * r + 4)
                nc.scalar.copy(wT, ps[:, 4:8, :].rearrange("p b (u c) -> p (b u) c", u=4)).then_inc(S["uw_out"], 1)
                inv_root(act, o_ms[:, r, :], f"gdn{r}")
            for i in (0, 2, 4, 6):
                tt, q = divmod(i, 4)
                act.wait_ge(S["outs_turned"], B4 + i + 1)
                nc.scalar.copy(yT16[:, 4 * q:4 * q + 4, tt * P:(tt + 1) * P], ps[:, i, :].rearrange("p (k t) -> p k t", k=4)
                               ).then_inc(S["outsT_ready"], 1)

        def m1_dve(dve, v, link):
            ts_, tt_, stt = v.tensor_scalar, v.tensor_tensor, v.scalar_tensor_tensor
            v.memset(craw[:, :, :, 0:3], 0.0).then_inc(S["craw_zero"], 1)
            dve.wait_ge(S["mixer_in"], P0 + M1_IN)
            dve.wait_ge(S["ba_done"], 1)
            dve.wait_ge(S["beta_exp"], 2)
            link(tt_(xa, ps[:, 5, 0:64].rearrange("p (t c) -> p t c", t=TT)[:, :, VH:2 * VH], spread(dtb, 1, [P, TT, VH]), ALU.add))
            link(ts_(ab, xa, -1.0, None, ALU.mult))
            tt_(ab, ab, xa, ALU.max).then_inc(S["abs_ready"], 1)
            dve.wait_ge(S["abs_exp"], 1)
            ts_(ab, ab, 1.0, None, ALU.add).then_inc(S["abs_ready"], 1)
            link(ts_(beta, beta, 1.0, None, ALU.add))
            link(v.reciprocal(beta, beta))
            dve.wait_ge(S["abs_exp"], 2)
            link(stt(out=gg, in0=xa, scalar=0.0, in1=ab, op0=ALU.max, op1=ALU.add))
            stt(out=gg, in0=gg, scalar=-1.0, in1=spread(alog, 1, [P, TT, VH]), op0=ALU.mult, op1=ALU.mult).then_inc(S["gates_ready"], 1)

            def conv(u):
                dve.wait_ge(S["unit_out"], U0 + u + 1)
                if 2 <= u < 10:
                    dve.wait_ge(S["conv_act"], u - 1)
                elif u >= 10:
                    dve.wait_ge(S["v_turned"], u - 9)
                for j in range(4):
                    for t in range(2):
                        w = ccols[:, 2 * u + t, j:j + 1]
                        src = craw[:, u % 2, t, j:j + SEQ]
                        dst = cacc[:, u % 2, t, :]
                        if j == 0:
                            last = ts_(dst, src, w, None, ALU.mult)
                        else:
                            last = stt(out=dst, in0=src, scalar=w, in1=dst, op0=ALU.mult, op1=ALU.add)
                        if (j, t) != (3, 1):
                            link(last)
                last.then_inc(S["conv_done"], 1)

            for u in range(17):
                if u < 16:
                    conv(u)
                if u == 2:
                    dve.wait_ge(S["gsums_done"], 1)
                    dve.wait_ge(S["gsums_out"], 2)
                    link(v.tensor_copy(gcs, ps[:, 7, 0:2 * VH].rearrange("p (t h) -> p t h", t=TT)))
                    tt_(kd, ps[:, 7, 2 * VH:4 * VH].rearrange("p (t h) -> p t h", t=TT), gcs, ALU.subtract).then_inc(S["kd_ready"], 1)
                    link(tt_(bg, beta, eg, ALU.mult))
                    dve.wait_ge(S["kd_ready"], 1)
                    v.engine_nop().then_inc(S["gsums_out"], 1)
                if 9 <= u < 13:
                    b = u - 9
                    dve.wait_ge(S["conv_act"], 2 * b + 2)
                    q4 = qkF[:, 4 * b:4 * b + 4, :]
                    tt_(N[b], q4, q4, ALU.mult).then_inc(S["sq_ready"], 1)
                if 11 <= u < 15:
                    b = u - 11
                    dve.wait_ge(S["ss_done"], b + 1)
                    ts_(N[4 + b], ps[:, 6:8, :].rearrange("p b (t c) -> p (b t) c", t=2), 1e-6, float(P) if b < 2 else 1.0,
                        ALU.add, ALU.mult).then_inc(S["square_ready"], 1)
                if 12 < u < 17:
                    b = u - 13
                    dve.wait_ge(S["root_ready"], 2 * ROOT[f"qk{b}"])
                    q4 = qkF[:, 4 * b:4 * b + 4, :]
                    tt_(q4, q4, N[4 + b], ALU.mult).then_inc(S["qk_normed"], 1)
            for b in range(2):
                for tt in range(TT):
                    dve.wait_ge(S["k_turned"], 2 * b + tt + 1)
                    v.tensor_copy(k_tm[:, tt, 4 * b:4 * b + 4, :], ps[:, 6 + tt, :].rearrange("p (t c) -> p t c", t=4)
                                  ).then_inc(S["k_tm_ready"], 1)
            dve.wait_ge(S["qk_normed"], 4)
            dve.wait_ge(S["v_turned"], 8)
            dve.wait_ge(S["unit_out"], U0 + M1_UNITS)
            v.memset(St, 0.0).then_inc(S["state_ready"], 1)
            for _ in range(3):
                dve.wait_ge(S["state_ready"], B4 + 1)
                v.engine_nop().then_inc(S["state_ready"], 1)
            v.memset(vnew, 0.0).then_inc(S["vnew_zero"], 1)
            dve.wait_ge(S["vnew_zero"], 1)
            for r in range(2):
                for b in range(4):
                    blk = slice(4 * b, 4 * b + 4)
                    dve.wait_ge(S["seg_exp"], 4 * r + b + 1)
                    link(tt_(Ed[:, blk, :], Ed[:, blk, :], spread(cm(C_LOW), 1, [P, 4, P]), ALU.mult))
                dve.wait_ge(S["kkqk_done"], 2 * r + 2)
                for b in range(4):
                    blk = slice(4 * b, 4 * b + 4)
                    e4 = Ed[:, blk, :].rearrange("p (h r) c -> p h r c", r=2)

                    def pair(bank):
                        return spread(ps[:, bank + b // 2, (b % 2) * 2 * P:(b % 2 + 1) * 2 * P].rearrange("p (h c) -> p h c", h=2), 2, [P, 2, 2, P])
                    link(tt_(A1[:, blk, :].rearrange("p (h r) c -> p h r c", r=2), e4, pair(4), ALU.mult))
                    tt_(A1[:, blk, :], A1[:, blk, :], spread(beta[:, r, blk], 2, [P, 4, P]), ALU.mult).then_inc(S["A_ready"], 1)
                    tt_(at1[:, blk, :].rearrange("p (h r) c -> p h r c", r=2), e4, pair(6), ALU.mult).then_inc(S["at_ready"], 1)
                for b in range(4):
                    dve.wait_ge(S["A_turned"], 4 * r + b + 1)
                    last = v.tensor_copy(AT1[:, 4 * b:4 * b + 4, :], ps[:, b, :].rearrange("p (u c) -> p u c", u=4))
                    if b < 3:
                        link(last)
                last.then_inc(S["AT_ready"], 1)
                tt_(vb, v_tm[:, r], spread(beta[:, r, :], 2, [P, VH, P]), ALU.mult).then_inc(S["vb_ready"], 1)
                dve.wait_ge(S["A_turned"], 4 * r + 4)
                dve.wait_ge(S["at_turned"], 4 * r + 4)
                solve_dve(dve, v, SOLVE1 + r)
                dve.wait_ge(S["u1_done"], 4 * r + 4)
                v.tensor_copy(u_, ps[:, 0:4, :].rearrange("p b (u c) -> p (b u) c", u=4)).then_inc(S["uw_out"], 1)
                dve.wait_ge(S["uw_out"], 2 * r + 2)
                for hf in range(2):
                    c = 2 * r + hf
                    rows = slice(64 * hf, 64 * hf + 64)

                    def bank(n):
                        return ps[rows, n, :].rearrange("p (u c) -> p u c", u=4)
                    for b in range(4):
                        blk = slice(4 * b, 4 * b + 4)
                        dve.wait_ge(S["wS_done"], 4 * c + b + 1)
                        tt_(vnew[rows, blk, :], u_[rows, blk, :], bank(b), ALU.subtract).then_inc(S["vnew_ready"], 1)
                    for b in range(4):
                        blk = slice(4 * b, 4 * b + 4)
                        dve.wait_ge(S["qS_done"], 4 * c + b + 1)
                        tt_(v_tm[rows, r, blk, :], bank(4 + b), spread(eg[rows, r, blk], 2, [64, 4, P]), ALU.mult).then_inc(S["qS_read"], 1)
                        link(tt_(St[:, blk, :], St[:, blk, :], spread(glb[:, c, blk], 2, [P, 4, P]), ALU.mult))
                        dve.wait_ge(S["incr_done"], B3 + 4 * c + b + 1)
                        tt_(St[:, blk, :], St[:, blk, :], ps[:, b, :].rearrange("p (u c) -> p u c", u=4), ALU.add).then_inc(S["state_ready"], 1)
                    for b in range(4):
                        blk = slice(4 * b, 4 * b + 4)
                        dve.wait_ge(S["qS_read"], 4 * c + b + 1)
                        dve.wait_ge(S["av_done"], 4 * c + b + 1)
                        tt_(v_tm[rows, r, blk, :], v_tm[rows, r, blk, :], bank(4 + b), ALU.add).then_inc(S["o_out"], 1)
                    dve.wait_ge(S["state_ready"], B4 + 4 * c + 8)
                dve.wait_ge(S["o_out"], 8 * r + 8)
                o = v_tm[:, r]
                scratch = Ed if r == 0 else St
                link(tt_(scratch, o, o, ALU.mult))
                link(v.tensor_reduce(o_ms[:, r, :], scratch, AX, ALU.add))
                ts_(o_ms[:, r, :], o_ms[:, r, :], 1.0 / P, 1e-6, ALU.mult, ALU.add).then_inc(S["square_ready"], 1)
                link(tt_(o, o, spread(ong, 1, [P, VH, P]), ALU.mult))
                link(tt_(o, o, z_tm[:, r], ALU.mult))
                dve.wait_ge(S["root_ready"], 2 * ROOT[f"gdn{r}"])
                tt_(o, o, spread(o_ms[:, r, :], 2, [P, VH, P]), ALU.mult).then_inc(S["gdn_out"], 1)
            for i in (1, 3, 5, 7):
                tt, q = divmod(i, 4)
                dve.wait_ge(S["outs_turned"], B4 + i + 1)
                v.tensor_copy(yT16[:, 4 * q:4 * q + 4, tt * P:(tt + 1) * P], ps[:, i, :].rearrange("p (k t) -> p k t", k=4)
                              ).then_inc(S["outsT_ready"], 1)
            dve.wait_ge(S["wide_used"], RING + wide_at["M1"] + 16)


        mixer_loads, mixer_params, mixer_pe, mixer_act, mixer_dve = {}, {}, {}, {}, {}
        mixer_loads["M0"], mixer_params["M0"], mixer_pe["M0"], mixer_act["M0"], mixer_dve["M0"] = m0_loads, m0_params, m0_pe, m0_act, m0_dve
        mixer_loads["M1"], mixer_params["M1"], mixer_pe["M1"], mixer_act["M1"], mixer_dve["M1"] = m1_loads, m1_params, m1_pe, m1_act, m1_dve

        for name in OVER:
            S["over_" + name]

        block = ctx.enter_context(nc.Block())

        @block.sync
        def _(sp):
            sp.dma_start(x_tok[:, :, :], a["x"][0].rearrange("(t p) d -> p t d", p=P)).then_inc(S["x_in"], 16)
            sp.dma_start(cst[:, :], a["constants"]).then_inc(S["const_in"], 16)

            def wide_chunk(n, src):
                sp.wait_ge(S["wide_used"], n + 1)
                nk, w = src.shape[1:]
                dst = wide[:, n % RING, 0:nk * w].rearrange("p (k c) -> p k c", k=nk)
                for k0, k1 in ((0, nk // 4), (nk // 4, nk // 2), (nk // 2, nk)):
                    sp.dma_start(dst[:, k0:k1, :], src[:, k0:k1, :]).then_inc(w_load(n)[0], 16)

            def gate_up(slot, used, value, sem, g, u):
                sp.wait_ge(used, value)
                dst = wide[:, slot, :].rearrange("p (h n) -> p h n", h=2)
                sp.dma_start(dst[:, 0, :], g).then_inc(sem, 16)
                sp.dma_start(dst[:, 1, 0:NARROW // 2], u[:, 0:NARROW // 2]).then_inc(sem, 16)
                sp.dma_start(dst[:, 1, NARROW // 2:], u[:, NARROW // 2:]).then_inc(sem, 16)

            def down(slot, used, value, sem, d):
                sp.wait_ge(used, value)
                sp.dma_start(narrow[:, slot, :], d).then_inc(sem, 16)

            def moe_loads(st):
                pfx = f"l{st[1]}_"
                n, m = wide_at[st], narrow_at[st]
                sg = a[pfx + "sh_gate"].rearrange("(p k) f -> p (k f)", k=KT)
                su = a[pfx + "sh_up"].rearrange("(p k) f -> p (k f)", k=KT)
                sd = a[pfx + "sh_down"].rearrange("(p k) f -> p (k f)", k=2)
                gate_up(n % RING, S["wide_used"], n + 1, w_load(n)[0], sg, su)
                down(m % RING, S["narrow_used"], m + 1, n_load(m)[0], sd)
                eg = a[pfx + "exp_gate"].rearrange("e (p k) f -> p e (k f)", k=KT)
                eu = a[pfx + "exp_up"].rearrange("e (p k) f -> p e (k f)", k=KT)
                ed = a[pfx + "exp_down"].rearrange("e (p k) f -> p e (k f)", k=2)
                n, m = n + 1, m + 1
                with sp.Fori(0, ITERS) as it:
                    for j in range(EPI):
                        gate_up((n + j) % RING, S["wide_used"], it * EPI + (n + j + 1), w_load(n + j)[0],
                                eg[:, bass.ds(it * EPI + j, 1), :].rearrange("p e n -> p (e n)"),
                                eu[:, bass.ds(it * EPI + j, 1), :].rearrange("p e n -> p (e n)"))
                    for j in range(EPI):
                        down((m + j) % RING, S["narrow_used"], it * EPI + (m + j + 1), n_load(m + j)[0],
                             ed[:, bass.ds(it * EPI + j, 1), :].rearrange("p e n -> p (e n)"))
                k = moe_no[st]
                sp.wait_ge(S["flag_ready"], k + 1)
                many = sp.value_load(flag[0:1, 0:1])
                with sp.If(many > SLOTS):
                    sp.wait_ge(S["pair_combined"], 2 * ITERS * (k + 1))
                    o = "over_"
                    with sp.Fori(0, ROUNDS - 1) as r:
                        with sp.Fori(0, ITERS) as it:
                            for j in range(EPI):
                                gate_up(j, S[o + "wide_used"], r * (ITERS * EPI) + it * EPI + (j + 1), S[f"{o}wide_loaded{j}"],
                                        eg[:, bass.ds(it * EPI + j, 1), :].rearrange("p e n -> p (e n)"),
                                        eu[:, bass.ds(it * EPI + j, 1), :].rearrange("p e n -> p (e n)"))
                            for j in range(EPI):
                                down(j, S[o + "narrow_used"], r * (ITERS * EPI) + it * EPI + (j + 1), S[f"{o}narrow_loaded{j}"],
                                     ed[:, bass.ds(it * EPI + j, 1), :].rearrange("p e n -> p (e n)"))
                    sp.wait_ge(S[o + "pair_combined"], 2 * O_ITERS)
                    sp.wait_ge(S["ln_done"], stages.index(st) + 1)
                    for name in sorted(S):
                        if name.startswith(o):
                            sp.sem_clear(S[name])

            for st in stages:
                if st[0] == "M":
                    mixer_loads[st](sp, wide_chunk)
                else:
                    moe_loads(st)
            sp.wait_ge(S["ln_done"], len(stages))
            sp.dma_start(out[0].rearrange("(t p) d -> p t d", p=P), x_tok[:, :, :]).then_inc(S["stored"], 16)
            sp.wait_ge(S["stored"], 16)

        @block.gpsimd
        def _(pool):
            for i, st in enumerate(stages):
                pfx = f"l{st[1]}_"
                if st[0] == "M":
                    mixer_params[st](pool)
                else:
                    if i:
                        pool.wait_ge(S["ln_done"], i)
                    pool.dma_start(router_w, a[pfx + "router_w"].rearrange("(p k) e -> p k e", k=KT)).then_inc(S["router_in"], 16)
                    pool.dma_start(rb, a[pfx + "router_b"].partition_broadcast(P)).then_inc(S["router_in"], 16)
                if i:
                    pool.wait_ge(S["ln_done"], i)
                ln = pfx + ("ln1_" if st[0] == "M" else "ln2_")
                pool.dma_start(lng[:, :], a[ln + "g"].partition_broadcast(P)).then_inc(S["ln_in"], 16)
                pool.dma_start(lnb[:, :], a[ln + "b"].partition_broadcast(P)).then_inc(S["ln_in"], 16)

        @block.tensor
        def _(pe):
            mm = nc.tensor.matmul

            def turn_x(i):
                if i == 0:
                    pe.wait_ge(S["const_in"], 16)
                    pe.wait_ge(S["x_in"], 16)
                else:
                    pe.wait_ge(S["ln_done"], i)
                for b in range(4):
                    tt, half = divmod(b, 2)
                    for k in range(4):
                        kt = 4 * half + k
                        last = nc.tensor.transpose(ps[:, 4 + b, k * P:(k + 1) * P], x_tok[:, tt, kt::KT], ident)
                    last.then_inc(S["x_turned"], 1)

            def gather(p, waits):
                for half in range(2):
                    for k in range(4):
                        kt = 4 * half + k
                        for tt in range(TT):
                            for part in range(3):
                                last = mm(ps[:, 4 + 2 * p + half, k * P:(k + 1) * P], h_parts[:, tt, part, kt, :],
                                          oh[:, tt, 2 * p:2 * p + 2, :].rearrange("p e s -> p (e s)"),
                                          start=(tt == 0 and part == 0), stop=(tt == 1 and part == 2))
                    last.then_inc(S[waits + "gathered"], 1)

            def expert_loop(o, iters, base, wide0, narrow0, k):
                q = S
                with pe.Fori(0, iters) as it:
                    pe.wait_ge(q[o + "onehot_ready"], it + (base + k + 1))
                    gather(0, o)
                    gather(1, o)
                    for p in range(2):
                        pe.wait_ge(q[o + "gathered_lo"], it * 2 + (2 * base + p + 1))
                        pe.wait_ge(q[o + "gathered_hi"], it * 2 + (2 * base + p + 1))
                        for e in range(2):
                            n = wide0 + 2 * p + e
                            pe.wait_ge(q[f"{o}wide_loaded{n % RING}"], it * 48 + 48 * (n // RING + 1))
                        for kt in range(KT):
                            for e in range(2):
                                last = mm(ps[64 * e:64 * e + 64, 4 + p, :], hTe[:, p, kt, 64 * e:64 * e + 64],
                                          gu_view((wide0 + 2 * p + e) % RING, kt), start=(kt == 0), stop=(kt == KT - 1))
                                if kt == KT - 1:
                                    last.then_inc(q[o + ("wide_used" if e == 0 else "gate_up_done")], 1)
                                if (p, kt, e) == (1, 0, 0):
                                    last.then_inc(q[o + "wide_used"], 1)
                    for p in range(2):
                        def turn_pair(p):
                            pe.wait_ge(q[o + "act_ready"], it * 2 + (2 * base + p + 1))
                            pe.wait_ge(q[o + "gated_ready"], it + (base + k + 1))
                            for tt in range(TT):
                                t = nc.tensor.transpose(ps[:, 4 + p, tt * P:(tt + 1) * P],
                                                        ohg[:, tt, 2 * p:2 * p + 2, :].rearrange("p e s -> p (e s)"), ident)
                                if (p, tt) == (0, 0):
                                    t.then_inc(q[o + "wide_used"], 1)
                            for j in range(2):
                                last = nc.tensor.transpose(ps[:, 4 + p, (2 + j) * P:(3 + j) * P], act_tok[:, p, j::2], ident)
                            last.then_inc(q[o + "pair_turned"], 1)
                        if p == 0:
                            turn_pair(0)
                        pe.wait_ge(q[o + "turned_ready"], it * 2 + (2 * base + p + 1))
                        for e in range(2):
                            n = narrow0 + 2 * p + e
                            pe.wait_ge(q[f"{o}narrow_loaded{n % RING}"], it * 16 + 16 * (n // RING + 1))
                        for h in range(2):
                            for j in range(2):
                                for e in range(2):
                                    slot = (narrow0 + 2 * p + e) % RING
                                    last = mm(ps[64 * e:64 * e + 64, 6 + h, :],
                                              turned[:, p, (2 + j) * P + 64 * e:(2 + j) * P + 64 * e + 64],
                                              narrow[:, slot, j * D + h * 512:j * D + h * 512 + 512],
                                              start=(j == 0), stop=(j == 1))
                                    if j == 1 and e == 0 and h == 1:
                                        last.then_inc(q[o + "narrow_used"], 1)
                            last.then_inc(q[o + "down_done"], 1)
                        if p == 0:
                            turn_pair(1)
                        for h in range(2):
                            pe.wait_ge(q[o + ("y_lo" if h == 0 else "y_hi")], it * 2 + (2 * base + p + 1))
                            for tt in range(TT):
                                last = mm(ps[:, 2 * tt + h, :], turned[:, p, tt * P:(tt + 1) * P],
                                          y_sb[:, p, h * 512:(h + 1) * 512], start=False, stop=False, skip_group_check=True)
                                if (h, tt) == (0, 0):
                                    last.then_inc(q[o + "narrow_used"], 1)
                        last.then_inc(q[o + "pair_combined"], 1)

            pe.sem_inc(S["wide_used"], RING)
            pe.sem_inc(S["narrow_used"], RING)
            for i, st in enumerate(stages):
                turn_x(i)
                pe.wait_ge(S["xT_ready"], 4 * (i + 1))
                if st[0] == "M":
                    mixer_pe[st](pe)
                    continue
                k = moe_no[st]
                n, m = wide_at[st], narrow_at[st]
                pe.wait_ge(S["router_in"], 32 * (k + 1))
                for tt in range(TT):
                    for kt in range(KT):
                        last = mm(ps[:, 4, tt * NE:(tt + 1) * NE], xT[:, kt, tt * P:(tt + 1) * P], router_w[:, kt, :],
                                  start=(kt == 0), stop=(kt == KT - 1))
                last.then_inc(S["logits_done"], 1)
                pe.wait_ge(*w_load(n))
                for g in range(2):
                    for j in range(2):
                        for kt in range(KT):
                            last = mm(ps[:, 6 + g, j * SEQ:(j + 1) * SEQ], gu_view(n % RING, kt)[:, g, j::2], xT[:, kt, :],
                                      start=(kt == 0), stop=(kt == KT - 1))
                last.then_inc(S["shared_up"], 1)
                pe.wait_ge(S["sel_ready"], k + 1)
                mm(ps[:, 5, 0:NE], cm(C_TRIU), sel[:, 0, :], start=True, stop=True)
                mm(ps[:, 5, NE:2 * NE], cm(C_ONES), sel[:, 0, :], start=True, stop=False)
                mm(ps[:, 5, NE:2 * NE], cm(C_TRIU), sel[:, 1, :], start=False, stop=True)
                mm(ps[:, 5, 2 * NE:3 * NE], cm(C_ONES), sel[:, 0, :], start=True, stop=False)
                mm(ps[:, 5, 2 * NE:3 * NE], cm(C_ONES), sel[:, 1, :], start=False, stop=True).then_inc(S["ranks_done"], 1)
                pe.wait_ge(S["shared_act"], k + 1)
                pe.wait_ge(*n_load(m))
                for tt in range(TT):
                    for h in range(2):
                        for j in range(2):
                            last = mm(ps[:, 2 * tt + h, :], shT[:, j, tt * P:(tt + 1) * P],
                                      narrow[:, m % RING, j * D + h * 512:j * D + h * 512 + 512],
                                      start=(j == 0), stop=False, skip_group_check=True)
                            if (tt, h, j) == (1, 1, 0):
                                last.then_inc(S["wide_used"], 1)
                last.then_inc(S["narrow_used"], 1)
                pe.wait_ge(S["parts_ready"], k + 1)
                expert_loop("", ITERS, k * ITERS, n + 1, m + 1, k)
                pe.wait_ge(S["flag_ready"], k + 1)
                many = pe.value_load(flag[0:1, 0:1])
                with pe.If(many > SLOTS):
                    o = "over_"
                    pe.sem_inc(S[o + "wide_used"], RING)
                    pe.sem_inc(S[o + "narrow_used"], RING)
                    expert_loop(o, O_ITERS, 0, 0, 0, 0)

        @block.scalar
        def _(act):
            def turn_x(i):
                for b in (0, 2):
                    act.wait_ge(S["x_turned"], 4 * i + b + 1)
                    tt, half = divmod(b, 2)
                    nc.scalar.copy(xT[:, 4 * half:4 * half + 4, tt * P:(tt + 1) * P],
                                   ps[:, 4 + b, :].rearrange("p (k t) -> p k t", k=4)).then_inc(S["xT_ready"], 1)

            def expert_loop(o, iters, base):
                with act.Fori(0, iters) as it:
                    for p in range(2):
                        act.wait_ge(S[o + "gathered"], it * 4 + (4 * base + 2 * p + 1))
                        nc.scalar.copy(hTe[:, p, 0:4, :], ps[:, 4 + 2 * p, :].rearrange("p (k s) -> p k s", k=4)
                                       ).then_inc(S[o + "gathered_lo"], 1)
                    for p in range(2):
                        act.wait_ge(S[o + "gate_up_done"], it * 2 + (2 * base + p + 1))
                        nc.scalar.activation(silu_g[:, p, :], ps[:, 4 + p, 0:DE], ACT.Silu).then_inc(S[o + "silu_ready"], 1)
                    for p in range(2):
                        act.wait_ge(S[o + "down_done"], it * 4 + (4 * base + 2 * p + 1))
                        nc.scalar.copy(y_sb[:, p, 0:512], ps[:, 6, :]).then_inc(S[o + "y_lo"], 1)

            for i, st in enumerate(stages):
                turn_x(i)
                if st[0] == "M":
                    mixer_act[st](act)
                    inv_root(act, rstd[:, :], "ln_" + st)
                    continue
                k = moe_no[st]
                act.wait_ge(S["logits_done"], k + 1)
                nc.scalar.activation(scores, ps[:, 4, 0:TT * NE].rearrange("p (t e) -> p t e", t=TT), ACT.Exp, scale=-1.0
                                     ).then_inc(S["exp_scores"], 1)
                act.wait_ge(S["shared_up"], k + 1)
                nc.scalar.activation(sh_silu, ps[:, 6, :].rearrange("p (j t) -> p j t", j=2), ACT.Silu).then_inc(S["shared_silu"], 1)
                expert_loop("", ITERS, k * ITERS)
                act.wait_ge(S["flag_ready"], k + 1)
                many = act.value_load(flag[0:1, 0:1])
                with act.If(many > SLOTS):
                    expert_loop("over_", O_ITERS, 0)
                inv_root(act, rstd[:, :], "ln_" + st)

        @block.vector
        def _(dve):
            v = nc.vector
            order = [0]

            def link(ins):
                order[0] += 1
                ins.then_inc(S["dve_order"], 1)
                dve.wait_ge(S["dve_order"], order[0])

            def turn_x(i):
                for b in (1, 3):
                    dve.wait_ge(S["x_turned"], 4 * i + b + 1)
                    tt, half = divmod(b, 2)
                    v.tensor_copy(xT[:, 4 * half:4 * half + 4, tt * P:(tt + 1) * P],
                                  ps[:, 4 + b, :].rearrange("p (k t) -> p k t", k=4)).then_inc(S["xT_ready"], 1)

            def layer_norm(i):
                for tt in range(TT):
                    link(v.scalar_tensor_tensor(out=x_tok[:, tt, :], in0=x_tok[:, tt, :], scalar=ALPHA,
                                                in1=ps[:, 2 * tt:2 * tt + 2, :].rearrange("p b c -> p (b c)"),
                                                op0=ALU.mult, op1=ALU.add))
                for tt in range(TT):
                    for h in range(2):
                        last = v.bn_stats(out=stats[:, tt, h, :], in_=x_tok[:, tt, h * 512:(h + 1) * 512])
                        link(last)
                for tt in range(TT):
                    link(v.bn_aggr(out=mv[:, tt, :], in_=stats[:, tt, :, :]))
                v.tensor_scalar(rstd[:, :], mv[:, :, 1], LN_EPS, None, ALU.add).then_inc(S["square_ready"], 1)
                dve.wait_ge(S["root_ready"], 2 * ROOT["ln_" + stages[i]])
                for tt in range(TT):
                    link(v.tensor_scalar(x_tok[:, tt, :], x_tok[:, tt, :], mv[:, tt, 0:1], rstd[:, tt:tt + 1],
                                         ALU.subtract, ALU.mult))
                dve.wait_ge(S["ln_in"], 32 * (i + 1))
                link(v.tensor_tensor(x_tok[:, :, :], x_tok[:, :, :], spread(lng[:, :], 1, [P, TT, D]), ALU.mult))
                v.tensor_tensor(x_tok[:, :, :], x_tok[:, :, :], spread(lnb[:, :], 1, [P, TT, D]), ALU.add
                                ).then_inc(S["ln_done"], 1)
                dve.wait_ge(S["ln_done"], i + 1)

            def one_hots(o, col):
                v.tensor_tensor(oh, spread(spread(cm(C_IOTA, SLOTS), 1, [P, EPI, SLOTS]), 1, [P, TT, EPI, SLOTS]),
                                spread(pos_r[:, :, bass.ds(col, EPI)], 3, [P, TT, EPI, SLOTS]), ALU.is_equal
                                ).then_inc(S[o + "onehot_ready"], 1)

            def gated(o, col, value):
                dve.wait_ge(S[o + "onehot_ready"], value)
                v.tensor_tensor(ohg, oh, spread(gate_r[:, :, bass.ds(col, EPI)], 3, [P, TT, EPI, SLOTS]), ALU.mult
                                ).then_inc(S[o + "gated_ready"], 1)

            def expert_loop(o, iters, base, col0, k):
                one_hots(o, col0)
                gated(o, col0, base + k + 1)
                with dve.Fori(0, iters) as it:
                    for p in range(2):
                        dve.wait_ge(S[o + "gathered"], it * 4 + (4 * base + 2 * p + 2))
                        v.tensor_copy(hTe[:, p, 4:8, :], ps[:, 5 + 2 * p, :].rearrange("p (k s) -> p k s", k=4)
                                      ).then_inc(S[o + "gathered_hi"], 1)

                    def times_up(p):
                        dve.wait_ge(S[o + "silu_ready"], it * 2 + (2 * base + p + 1))
                        v.tensor_tensor(act_tok[:, p, :], silu_g[:, p, :], ps[:, 4 + p, DE:2 * DE], ALU.mult
                                        ).then_inc(S[o + "act_ready"], 1)

                    def turned_out(p):
                        dve.wait_ge(S[o + "pair_turned"], it * 2 + (2 * base + p + 1))
                        v.tensor_copy(turned[:, p, :], ps[:, 4 + p, :]).then_inc(S[o + "turned_ready"], 1)

                    def y_out(p):
                        dve.wait_ge(S[o + "down_done"], it * 4 + (4 * base + 2 * p + 2))
                        v.tensor_copy(y_sb[:, p, 512:1024], ps[:, 7, :]).then_inc(S[o + "y_hi"], 1)

                    times_up(0)
                    times_up(1)
                    turned_out(0)
                    y_out(0)
                    turned_out(1)
                    one_hots(o, it * EPI + (col0 + EPI))
                    gated(o, it * EPI + (col0 + EPI), it + (base + k + 2))
                    y_out(1)

            for i, st in enumerate(stages):
                turn_x(i)
                if st[0] == "M":
                    mixer_dve[st](dve, v, link)
                    layer_norm(i)
                    continue
                k = moe_no[st]
                dve.wait_ge(S["exp_scores"], k + 1)
                link(v.tensor_scalar(scores, scores, 1.0, None, ALU.add))
                link(v.reciprocal(scores, scores))
                dve.wait_ge(S["router_in"], 32 * (k + 1))
                link(v.tensor_tensor(choice, scores, spread(rb, 1, [P, TT, NE]), ALU.add))
                for tt in range(TT):
                    for g in range(NG):
                        last = v.max(out=grp_max[:, tt, g, :], in_=choice[:, tt, g * GE:(g + 1) * GE])
                        link(last)
                link(v.tensor_tensor(grp, grp_max[:, :, :, 0], grp_max[:, :, :, 1], ALU.add))
                left = spread(grp, 2, [P, TT, NG, NG])
                right = spread(grp, 3, [P, TT, NG, NG])
                link(v.tensor_tensor(grp_gt, left, right, ALU.is_gt))
                link(v.tensor_tensor(grp_eq, left, right, ALU.is_equal))
                link(v.tensor_tensor(grp_eq, grp_eq, spread(cm(C_G8, NG * NG).rearrange("p (a b) -> p a b", a=NG), 1, [P, TT, NG, NG]), ALU.mult))
                link(v.tensor_tensor(grp_gt, grp_gt, grp_eq, ALU.add))
                link(v.tensor_reduce(grp_rank, grp_gt, AX, ALU.add))
                link(v.tensor_scalar(grp_off, grp_rank, float(TOPG), -FAR, ALU.is_ge, ALU.mult))
                c4 = choice.rearrange("p t (g e) -> p t g e", g=NG)
                link(v.tensor_tensor(c4, c4, spread(grp_off, 3, [P, TT, NG, GE]), ALU.add))
                for tt in range(TT):
                    link(v.max(out=top8[:, tt, :], in_=choice[:, tt, :]))
                    link(v.match_replace(out=choice_rep[:, tt, :], in_to_replace=top8[:, tt, :], in_values=choice[:, tt, :],
                                         imm_value=-3.0 * FAR))
                v.tensor_tensor(sel, choice, choice_rep, ALU.is_gt).then_inc(S["sel_ready"], 1)
                dve.wait_ge(S["sel_ready"], k + 1)
                link(v.tensor_tensor(gate_one, sel, scores, ALU.mult))
                link(v.tensor_reduce(gate_sum, gate_one, AX, ALU.add))
                link(v.reciprocal(gate_inv, gate_sum))
                link(v.tensor_tensor(gate_one, gate_one, spread(gate_inv, 2, [P, TT, NE]), ALU.mult))
                for r in range(ROUNDS):
                    link(v.tensor_scalar(gate_r[:, :, r * NE:(r + 1) * NE], gate_one, ROUTE_SCALE, None, ALU.mult))
                link(v.memset(gate_r[:, :, ROUNDS * NE:], 0.0))
                dve.wait_ge(S["shared_silu"], k + 1)
                v.tensor_tensor(shT, sh_silu, ps[:, 7, :].rearrange("p (j t) -> p j t", j=2), ALU.mult).then_inc(S["shared_act"], 1)
                dve.wait_ge(S["ranks_done"], k + 1)
                link(v.scalar_tensor_tensor(out=pos_one, in0=ps[:, 5, 0:TT * NE].rearrange("p (t e) -> p t e", t=TT), scalar=1.0,
                                            in1=sel, op0=ALU.add, op1=ALU.mult))
                for r in range(ROUNDS):
                    link(v.tensor_scalar(pos_r[:, :, r * NE:(r + 1) * NE], pos_one, -1.0 - r * SLOTS, None, ALU.add))
                link(v.memset(pos_r[:, :, ROUNDS * NE:], -1.0))
                link(v.tensor_reduce(cnt[:, 0:1], ps[:, 5, 2 * NE:3 * NE], AX, ALU.max))
                v.tensor_copy(flag[:, 0:1], cnt[:, 0:1]).then_inc(S["flag_ready"], 1)
                xk = x_tok[:, :, :].rearrange("p t (q k) -> p t k q", k=KT)
                link(v.tensor_copy(h_parts[:, :, 0, :, :], xk))
                link(v.tensor_tensor(h_rest, xk, h_parts[:, :, 0, :, :], ALU.subtract))
                link(v.tensor_copy(h_parts[:, :, 1, :, :], h_rest))
                v.tensor_tensor(h_parts[:, :, 2, :, :], h_rest, h_parts[:, :, 1, :, :], ALU.subtract).then_inc(S["parts_ready"], 1)
                expert_loop("", ITERS, k * ITERS, 0, k)
                dve.wait_ge(S["flag_ready"], k + 1)
                many = dve.value_load(flag[0:1, 0:1])
                with dve.If(many > SLOTS):
                    dve.wait_ge(S["gated_ready"], (ITERS + 1) * (k + 1))
                    dve.wait_ge(S["pair_combined"], 2 * ITERS * (k + 1))
                    expert_loop("over_", O_ITERS, 0, NE, 0)
                    dve.wait_ge(S["over_pair_combined"], 2 * O_ITERS)
                dve.wait_ge(S["pair_combined"], 2 * ITERS * (k + 1))
                layer_norm(i)


def host_layout(a):
    a = dict(a)
    if "l0_b_mix" in a:
        names = ("l0_b_mix", "l0_b_w0", "l0_b_a0", "l0_b_k_k", "l0_b_k_a", "l0_b_r_k")
        a["l0_b_cols"] = np.ascontiguousarray(np.concatenate([np.asarray(a.pop(n)).reshape(-1, P) for n in names]).T)
    if "l1_conv_w" in a:
        a["l1_conv_cols"] = np.ascontiguousarray(np.asarray(a.pop("l1_conv_w")).reshape(4, 32, P).transpose(2, 1, 0).reshape(P, 128))
    return a


def kernel(**inputs):
    import concourse.bacc as bacc
    from concourse.bass_utils import run_bass_kernel_spmd

    arrays = host_layout({n: np.asarray(v) for n, v in inputs.items()})
    arrays["constants"], arrays["alibi"] = constants()
    nc = bacc.Bacc("TRN2", target_bir_lowering=False, num_devices=1)
    dram, a = {}, {}
    for name, value in arrays.items():
        value = np.ascontiguousarray(value)
        dram[f"in_{name}"] = value
        a[name] = nc.dram_tensor(f"in_{name}", value.shape, mybir.dt.from_np(value.dtype), kind="ExternalInput").ap()
    out = nc.dram_tensor("out_dram", (1, SEQ, D), F32, kind="ExternalOutput").ap()
    build_program(nc, a, out)
    return run_bass_kernel_spmd(nc, [dram], core_ids=[0]).results[0]["out_dram"]
```

```python
import math
from contextlib import ExitStack, contextmanager

import numpy as np

import concourse.bass as bass
from concourse import mybir

F32 = mybir.dt.float32
F32R = mybir.dt.float32r
I32 = mybir.dt.int32
ALU = mybir.AluOpType
ACT = mybir.ActivationFunctionType
AX = mybir.AxisListType.X

P = 128
SEQ, D = 256, 1024
TT = SEQ // P
KT = D // P
ALPHA = 4.0 ** 0.25
LN_EPS = 1e-5

NE, NG, GE, TOPG = 64, 8, 8, 4
DE = D // 4
SLOTS = 64
ROUNDS = SEQ // SLOTS
ROUTE_SCALE = 2.5
EPI = 4
ITERS = NE // EPI
O_ITERS = (ROUNDS - 1) * ITERS
PCOLS = ROUNDS * NE + EPI
FAR = 1e30

RING = 4
WIDE = 4096
NARROW = 2048
CH = WIDE // KT

C_ID, C_STRICT, C_INCL, C_ONES, C_TRIU = 0, 128, 256, 384, 512
C_LVL = 640
LEVELS = 6
C_HALF = C_LVL + LEVELS * P
C_SEG = C_HALF + P
C_LOW = C_SEG + P
C_IOTA = C_LOW + P
C_G8 = C_IOTA + SLOTS
C_HEAD = C_G8 + NG * NG
C_END = C_HEAD + 32
SLOPES = [2.0 ** (-8.0 * (i + 1) / 4) for i in range(4)]
MIX_ARENA = 20016
XL1_AT = 14336
XL0_AT, XL0B_AT = 7184, 18448
N_M = {"M0": 9, "M1": 16}


def constants():
    p = np.arange(P)[:, None]
    f = np.arange(P)[None, :]
    same = (p // 64) == (f // 64)
    c = np.zeros((P, C_END), np.float32)
    c[:, C_ID:C_ID + P] = p == f
    c[:, C_STRICT:C_STRICT + P] = same & (p < f)
    c[:, C_INCL:C_INCL + P] = same & (p <= f)
    c[:, C_ONES:C_ONES + P] = 1.0
    c[:, C_TRIU:C_TRIU + P] = p < f
    for n in range(LEVELS):
        m = 1 << n
        c[:, C_LVL + n * P:C_LVL + (n + 1) * P] = (p // (2 * m) == f // (2 * m)) & (p % (2 * m) < m) & (f % (2 * m) >= m)
    c[:, C_HALF:C_HALF + P] = same
    c[:, C_SEG:C_SEG + P] = p > f
    c[:, C_LOW:C_LOW + P] = same & (f <= p)
    c[:, C_IOTA:C_IOTA + SLOTS] = np.arange(SLOTS)[None, :]
    c[:, C_G8:C_G8 + NG * NG] = (np.arange(NG)[None, :] < np.arange(NG)[:, None]).reshape(1, -1)
    for t in range(4):
        for h in range(8):
            c[:, C_HEAD + t * 8 + h] = (h // 2 == t) & ((np.arange(P) // 64) == h % 2)
    dist = P + p[:, :, None] - np.arange(2 * P)[None, None, :]
    bias = np.where(dist >= 0, -np.array(SLOPES)[None, :, None] * dist, -1e30)
    return c, bias.astype(np.float32).reshape(P, 4 * 2 * P)


OVER = ["onehot_ready", "gated_ready", "gathered", "gathered_lo", "gathered_hi", "gate_up_done", "silu_ready", "act_ready", "gates_turned", "gates_out",
        "pair_turned", "turned_ready", "down_done", "y_lo", "y_hi", "pair_combined", "wide_used", "narrow_used"
        ] + [f"{ring}_loaded{n}" for ring in ("wide", "narrow") for n in range(RING)]


class Sems(dict):

    def __init__(self, nc, ctx):
        super().__init__()
        self.nc, self.ctx = nc, ctx

    def __missing__(self, name):
        self[name] = self.ctx.enter_context(self.nc.semaphore(name))
        return self[name]


def spread(ap, axis, shape):
    return ap.unsqueeze(axis).broadcast_to(shape)


def build_program(nc, a, out, stages=("M0", "E0", "M1", "E1")):
    with ExitStack() as ctx:
        S = Sems(nc, ctx)

        def sb(name, shape, dt=F32):
            return ctx.enter_context(nc.sbuf_tensor(name, shape, dt))

        under = []

        @contextmanager
        def aliases():
            with ExitStack() as stack:
                under.append(stack)
                yield
                under.pop()

        def rounded(name, *dims, dt=F32R):
            return under[-1].enter_context(nc.sbuf_tensor(name, [P, *dims], dt))

        wide = sb("wide_ring", [P, RING, WIDE])
        with aliases():
            w_parts = rounded("w_parts", 2, 2, KT, 256)
        narrow = sb("narrow_ring", [P, RING, NARROW])
        x_tok = sb("x_tok", [P, TT, D])
        with aliases():
            xT_hi = rounded("xT_high", KT, SEQ)
        xT = sb("xT", [P, KT, SEQ])
        cst = sb("constants_sb", [P, C_END])
        lng = sb("ln_gain", [P, D])
        lnb = sb("ln_bias", [P, D])
        stats = sb("ln_stats", [P, TT, 2, 6])
        mv = sb("ln_mean_var", [P, TT, 2])
        rstd = sb("ln_rstd", [P, TT])
        with aliases():
            h_parts = rounded("h_parts", TT, 2, KT, P)
            oh = rounded("one_hots", TT, EPI, SLOTS)
            ohT = rounded("one_hots_turned", 2, SEQ)
            y_parts = rounded("y_parts", 2, 2, D)
        with aliases():
            rounded("below_xT_low_1", XL1_AT, dt=F32)
            xT_lo1 = rounded("xT_low_1", KT, SEQ)
        with aliases():
            rounded("below_xT_low_0a", XL0_AT, dt=F32)
            xT_lo0a = rounded("xT_low_0a", KT // 2, SEQ)
            rounded("below_xT_low_0b", XL0B_AT - XL0_AT - KT // 2 * SEQ, dt=F32)
            xT_lo0b = rounded("xT_low_0b", KT // 2, SEQ)
        arena = sb("arena", [P, MIX_ARENA])
        ps = ctx.enter_context(nc.psum_tensor("ps", [P, 8, 512], F32))
        ident = cst[:, C_ID:C_ID + P]

        def cm(col, n=P):
            return cst[:, col:col + n]

        def area(at, *dims, base=arena):
            n = int(np.prod(dims))
            v = base[:, at:at + n]
            names = "abcd"[:len(dims)]
            if len(dims) == 1:
                return v
            return v.rearrange(f"p ({' '.join(names)}) -> p {' '.join(names)}", **dict(zip(names, dims)))

        at = TT * 2 * KT * P + TT * EPI * SLOTS + 2 * SEQ + 4 * D

        def take(*dims):
            nonlocal at
            v = area(at, *dims)
            at += int(np.prod(dims))
            return v

        scores = take(TT, NE)
        choice = take(TT, NE)
        choice_rep = take(TT, NE)
        sel = take(TT, NE)
        gate_one = take(TT, NE)
        grp_max = take(TT, NG, 8)
        grp = take(TT, NG)
        grp_gt = take(TT, NG, NG)
        grp_eq = take(TT, NG, NG)
        grp_rank = take(TT, NG)
        grp_off = take(TT, NG)
        top8 = take(TT, 8)
        gate_sum = take(TT)
        gate_inv = take(TT)
        pos_one = take(TT, NE)
        pos_r = take(TT, PCOLS)
        gate_r = take(TT, PCOLS)
        rb = take(NE)
        router_w = take(KT, NE)
        cnt = take(2)
        flag = take(2).bitcast(I32)
        ohg = take(TT, EPI, SLOTS)
        slot_gate = take(2)
        hTe = take(2, KT, P)
        silu_g = take(2, DE)
        act_tok = take(2, DE)
        turned = take(2, 2 * P)
        sh_silu = take(2, SEQ)
        shT = take(2, SEQ)
        assert at <= MIX_ARENA, at

        wide_at, narrow_at = {}, {}
        nw = nn = 0
        for st in stages:
            wide_at[st], narrow_at[st] = nw, nn
            if st[0] == "M":
                nw += N_M[st]
            else:
                nw += 1 + NE
                nn += 1 + NE
        SOLVE1 = 1 if "M0" in stages else 0
        moe_no = {st: n for n, st in enumerate(s for s in stages if s[0] == "E")}

        roots = {"M0": ["attn1", "attn0", "kk", "group_norm"], "M1": ["qk0", "qk1", "qk2", "qk3", "gdn0", "gdn1"]}
        ROOT = {name: n + 1 for n, name in enumerate(x for st in stages for x in roots.get(st, []) + ["ln_" + st])}

        def inv_root(act, t, name, requests=1):
            act.wait_ge(S["square_ready"], ROOT[name])
            nc.scalar.activation(t, t, ACT.Ln).then_inc(S["root_ready"], requests)
            act.wait_ge(S["root_ready"], 2 * ROOT[name] - requests)
            nc.scalar.activation(t, t, ACT.Exp, scale=-0.5).then_inc(S["root_ready"], requests)

        def w_load(n):
            return S[f"wide_loaded{n % RING}"], 48 * (n // RING + 1)

        def n_load(n):
            return S[f"narrow_loaded{n % RING}"], 16 * (n // RING + 1)

        mixers = [st for st in stages if st[0] == "M"]
        W0 = {st: 13 * mixers.index(st) for st in mixers}
        X0 = {st: 4 * mixers.index(st) for st in mixers}
        UNITS = {"M0": 13, "M1": 24}

        def x_low(st, kt):
            if st == "M1":
                return xT_lo1[:, kt]
            return (xT_lo0a if kt < 4 else xT_lo0b)[:, kt % 4]

        def x_low4(st, half):
            if st == "M1":
                return xT_lo1[:, 4 * half:4 * half + 4]
            return (xT_lo0b if half else xT_lo0a)[:, :]

        def unit_weights(st, u):
            n = wide_at[st] + u // 2
            w = 256 if (st, u) == ("M0", 12) else CH
            return n, wide[:, n % RING, 0:KT * w].rearrange("p (k c) -> p k c", k=KT)[:, :, (u % 2) * 256:(u % 2) * 256 + 256]

        def split_high(act, st, u):
            n, w = unit_weights(st, u)
            act.wait_ge(*w_load(n))
            if u >= 2:
                act.wait_ge(S["unit_done"], W0[st] + u - 1)
            nc.scalar.copy(w_parts[:, u % 2, 0], w).then_inc(S["w_high"], 1)

        def split_low(eng, ns, st, u):
            n, w = unit_weights(st, u)
            eng.wait_ge(S["w_high"], W0[st] + u + 1)
            ns.tensor_tensor(w_parts[:, u % 2, 1], w, w_parts[:, u % 2, 0].bitcast(F32), ALU.subtract).then_inc(S[f"w_low{u % 2}"], 1)

        def project(pe, st, u, token_major):
            pe.wait_ge(S["w_high"], W0[st] + u + 1)
            if u >= 4:
                pe.wait_ge(S["unit_out"], W0[st] + u - 3)
            wp = w_parts[:, u % 2]
            for half in range(2):
                tok = slice(half * P, (half + 1) * P)
                for n in range(3 * KT):
                    kt, part = (n // 2, n % 2) if n < 2 * KT else (n - 2 * KT, 0)
                    wt = wp[:, 0 if n < 2 * KT else 1, kt]
                    xt = x_low(st, kt) if part else xT_hi[:, kt]
                    if (half, n) == (0, 2 * KT):
                        before = (W0[st] + 1 - u % 2) // 2
                        pe.wait_ge(S[f"w_low{u % 2}"], before + u // 2 + 1)
                    lhsT, rhs = (xt[:, tok], wt) if token_major else (wt[:, tok], xt)
                    last = nc.tensor.matmul(ps[:, u % 4, half * 256:(half + 1) * 256], lhsT, rhs, start=(n == 0), stop=(n == 3 * KT - 1))
                    if (half, n) == (0, 2 * KT) and (u % 2 or u == UNITS[st] - 1):
                        last.then_inc(S["wide_used"], 1)
            last.then_inc(S["unit_done"], 1)

        def gu_view(slot, kt):
            return wide[:, slot, :].rearrange("p (g k f) -> p k g f", g=2, k=KT)[:, kt, :, :]

        M0_UNITS = 13
        raw = area(0, 14, SEQ + 1)
        mixT = area(3600, 14, SEQ)
        at_ = area(0, 16, 2 * P)
        bt_ = area(4096, 16, 2 * P)
        KR = area(8208, 4, 2, SEQ)
        betaT = area(10256, 4, SEQ)
        gammaT = area(11280, 4, SEQ)
        tm4 = area(12304, 4, TT, 512)
        beta_tm, gamma_tm, V_tm, kappa_tm = (tm4[:, i] for i in range(4))
        y_tok = area(16400, TT, D)
        g_tm = area(18448, TT, 512)
        qkT = area(8208, 8, SEQ)
        vA = area(10256, TT, 512)
        alibi = area(11280, 4, SEQ)
        sc = area(12304, 2, 4, SEQ)
        attn = area(14352, 4, SEQ)
        attnT = area(15376, 4, 2, P)
        small = 19472
        cols = area(small, 34)
        al = area(small + 34, 4, 64)
        ang = area(small + 290, P)
        ncols = area(small + 418, 8)
        lam2 = area(small + 426, 2)
        lam = area(small + 428, 1)
        smax = area(small + 429, 2, 4)
        ssum = area(small + 437, 2, 4)
        arms = area(small + 445, 4)
        bonus = area(small + 449, TT, 8)
        gmu = area(small + 465, 16)
        gvar = area(small + 481, 16)
        lamC = area(small + 497, 4, 4)
        lora = lng[:, 0:512]
        g2_sb = lng[:, 512:1024]
        lnxg = lnb[:, 0:512]
        lnxb = lnb[:, 512:1024]
        nflat = narrow[:, :, :].rearrange("p a b -> p (a b)")
        N = [area(1024 * i, 4, SEQ, base=nflat) for i in range(8)]
        X, XT_, T1, QT = (area(2048 * i, 16, P, base=nflat) for i in range(4))
        w12 = wide[:, 1:3, :].rearrange("p a b -> p (a b)")
        G_ = area(0, TT, 512, base=w12)
        BV = area(1024, TT, 512, base=w12)
        U_ = area(2048, TT, 512, base=w12)
        Yr = area(3072, TT, 8, 64, base=w12)
        XKT = area(4096, TT, 4, P, base=w12)
        Sbd = area(5120, 4, P, base=w12)
        Ytmp = area(5632, TT, 8, 64, base=w12)
        EM = math.exp(-0.5)
        STEP = {name: n + 1 for names in (
            ("lam_exp", "tanh_ready", "xg_exp", "g_copied", "bonus_ready", "bv_ready", "xk_ready"),
            ("lam_sums", "ncols_ready", "kk_squared", "xg_ready", "cum_ready", "rk_ready", "factors_ready", "g_ready"),
            ("g_done", "kk_norm", "bonus_done", "bv_done", "xg2_done", "xk_done")) for n, name in enumerate(names)}

        def wv(n, w):
            return wide[:, n % RING, 0:KT * w].rearrange("p (k c) -> p k c", k=KT)

        def unit0(h):
            return (h % 2) * 4 + h // 2

        def m0_loads(sp, wide_chunk):
            w_in = a["l0_w_in"].rearrange("(p k) c -> p k c", k=KT)
            n = wide_at["M0"]
            for c in range(7):
                wide_chunk(n + c, w_in[:, :, c * CH:min((c + 1) * CH, 3328)])
            w_out = a["l0_w_out"].rearrange("(p k) c -> p k c", k=KT)
            for c in range(2):
                wide_chunk(n + 7 + c, w_out[:, :, c * CH:(c + 1) * CH])
            sp.wait_ge(S["rwkv_out"], 1)

        def m0_params(pool):
            split_low(pool, nc.gpsimd, "M0", 0)
            pool.dma_start(cols, a["l0_b_cols"]).then_inc(S["mixer_in"], 16)
            pool.dma_start(alibi, a["alibi"].rearrange("p (h k) -> p h k", h=4)).then_inc(S["mixer_in"], 16)
            pool.dma_start(al, a["l0_a_lambda"].rearrange("a b -> (a b)").partition_broadcast(P).rearrange("p (a b) -> p a b", a=4)
                           ).then_inc(S["mixer_in"], 16)
            pool.dma_start(ang, a["l0_a_norm_g"].partition_broadcast(P)).then_inc(S["mixer_in"], 16)
            pool.dma_start(lora[0:64, :], a["l0_b_w2"]).then_inc(S["mixer_in"], 16)
            pool.dma_start(lora[64:128, :], a["l0_b_a2"]).then_inc(S["mixer_in"], 16)
            pool.dma_start(g2_sb, a["l0_b_g2"]).then_inc(S["mixer_in"], 16)
            pool.dma_start(lnxg, a["l0_b_lnx_g"].partition_broadcast(P)).then_inc(S["mixer_in"], 16)
            pool.dma_start(lnxb, a["l0_b_lnx_b"].partition_broadcast(P)).then_inc(S["mixer_in"], 16)
            for u in range(1, M0_UNITS):
                split_low(pool, nc.gpsimd, "M0", u)
            solve_pool(pool, 0, at_)
            pool.wait_ge(S["rwkv_out"], 1)

        M0_IN = 16 * 9

        def solve_pool(pool, s, AT):
            pool.wait_ge(S["AT_ready"], s + 1)
            for lv in range(LEVELS):
                for b in range(4):
                    if lv:
                        pool.wait_ge(S["T1_done"], 24 * s + 4 * (lv - 1) + b + 1)
                    if lv == 1:
                        pool.wait_ge(S["XT_ready"], 24 * s + b + 1)
                    nc.gpsimd.tensor_tensor(QT_of(s)[:, 4 * b:4 * b + 4, :], AT[:, 4 * b:4 * b + 4, 0:P],
                                            spread(cm(C_LVL + lv * P), 1, [P, 4, P]), ALU.mult).then_inc(S["QT_ready"], 1)

        def QT_of(s):
            return QT if s < SOLVE1 else QT1

        def X_of(s):
            return (X, XT_, T1) if s < SOLVE1 else (X1, XT1, T11)

        def solve_pe(pe, s):
            mm = nc.tensor.matmul
            X, XT, T1 = X_of(s)
            Q = QT_of(s)
            for b in range(4):
                pe.wait_ge(S["QT_ready"], 24 * s + b + 1)
                for u in range(4):
                    last = mm(ps[:, b, u * P:(u + 1) * P], Q[:, 4 * b + u, :], ident, start=True, stop=True)
                last.then_inc(S["T1_done"], 1)
            for lv in range(1, LEVELS):
                for b in range(4):
                    pe.wait_ge(S["QT_ready"], 24 * s + 4 * lv + b + 1)
                    pe.wait_ge(S["X_ready"], 20 * s + 4 * (lv - 1) + b + 1)
                    for u in range(4):
                        last = mm(ps[:, b, u * P:(u + 1) * P], Q[:, 4 * b + u, :], X[:, 4 * b + u, :], start=True, stop=True)
                    last.then_inc(S["T1_done"], 1)
                for b in range(4):
                    n = 4 * (lv - 1) + b
                    pe.wait_ge(S["T1_ready"], 20 * s + n + 1)
                    pe.wait_ge(S["XT_ready"], 24 * s + 4 * lv + max(b - 1, 0) if b >= 2 else 24 * s + 4 * (lv - 1) + 4)
                    if lv < LEVELS - 1:
                        for u in range(4):
                            last = mm(ps[:, 4 + 2 * (b % 2), u * P:(u + 1) * P], XT[:, 4 * b + u, :], T1[:, 4 * b + u, :],
                                      start=True, stop=True)
                        last.then_inc(S["XQX_done"], 1)
                    for u in range(4):
                        last = mm(ps[:, 5 + 2 * (b % 2), u * P:(u + 1) * P], T1[:, 4 * b + u, :], XT[:, 4 * b + u, :],
                                  start=True, stop=True)
                    last.then_inc(S["XQXT_done"], 1)

        def solve_act(act, s):
            T1 = X_of(s)[2]
            for lv in range(1, LEVELS):
                for b in range(4):
                    act.wait_ge(S["T1_done"], 24 * s + 4 * lv + b + 1)
                    nc.scalar.copy(T1[:, 4 * b:4 * b + 4, :], ps[:, b, :].rearrange("p (u c) -> p u c", u=4)
                                   ).then_inc(S["T1_ready"], 1)

        def solve_dve(dve, v, s, beside=None):
            X, XT, T1 = X_of(s)
            Q = QT_of(s)
            for b in range(4):
                dve.wait_ge(S["QT_ready"], 24 * s + b + 1)
                v.scalar_tensor_tensor(out=XT[:, 4 * b:4 * b + 4, :], in0=Q[:, 4 * b:4 * b + 4, :], scalar=-1.0,
                                       in1=spread(ident, 1, [P, 4, P]), op0=ALU.mult, op1=ALU.add).then_inc(S["XT_ready"], 1)
                dve.wait_ge(S["T1_done"], 24 * s + b + 1)
                v.scalar_tensor_tensor(out=X[:, 4 * b:4 * b + 4, :], in0=ps[:, b, :].rearrange("p (u c) -> p u c", u=4), scalar=-1.0,
                                       in1=spread(ident, 1, [P, 4, P]), op0=ALU.mult, op1=ALU.add).then_inc(S["X_ready"], 1)
            for lv in range(1, LEVELS):
                for b in range(4):
                    blk = slice(4 * b, 4 * b + 4)
                    if lv < LEVELS - 1:
                        dve.wait_ge(S["XQX_done"], 16 * s + 4 * (lv - 1) + b + 1)
                        dve.wait_ge(S["X_ready"], 20 * s + 4 * (lv - 1) + b + 1)
                        v.tensor_tensor(X[:, blk, :], X[:, blk, :], ps[:, 4 + 2 * (b % 2), :].rearrange("p (u c) -> p u c", u=4),
                                        ALU.subtract).then_inc(S["X_ready"], 1)
                    dve.wait_ge(S["XQXT_done"], 20 * s + 4 * (lv - 1) + b + 1)
                    dve.wait_ge(S["XT_ready"], 24 * s + 4 * (lv - 1) + b + 1)
                    v.tensor_tensor(XT[:, blk, :], XT[:, blk, :], ps[:, 5 + 2 * (b % 2), :].rearrange("p (u c) -> p u c", u=4),
                                    ALU.subtract).then_inc(S["XT_ready"], 1)
                    if beside:
                        beside(4 * (lv - 1) + b)

        def m0_pe(pe):
            mm = nc.tensor.matmul
            base = wide_at["M0"]

            def unit(u):
                project(pe, "M0", u, u in (4, 5))

            def scores(qb):
                kw = (qb + 1) * P
                for h in range(4):
                    for c in range(2):
                        r = slice(64 * c, 64 * c + 64)
                        bank, col = (4 + 2 * c + h // 2, (h % 2) * kw) if qb else (4 + c, h * kw)
                        last = mm(ps[:, bank, col:col + kw], qkT[r, h, qb * P:(qb + 1) * P], qkT[r, 4 + h, 0:kw],
                                  start=True, stop=True)
                        if (h, c) == (3, 0):
                            last.then_inc(S["scores_done"], 1)
                last.then_inc(S["scores_done"], 1)

            def turn_attn(qb):
                pe.wait_ge(S["attn_ready"], 2 - qb)
                for h in range(4):
                    for kb in range(qb + 1):
                        bank, col = (6 + h // 2, (h % 2) * 2 * P + kb * P) if qb else (5, h * P)
                        last = nc.tensor.transpose(ps[:, bank, col:col + P], attn[:, h, kb * P:(kb + 1) * P], ident)
                last.then_inc(S["attn_turned"], 1)

            def attend(qb):
                pe.wait_ge(S["attnT_ready"], 2 - qb)
                bank = 4 if qb else 6
                for h in range(4):
                    for kb in range(qb + 1):
                        last = mm(ps[:, bank, h * P:(h + 1) * P], attnT[:, h, kb, :], vA[:, kb, h * P:(h + 1) * P],
                                  start=(kb == 0), stop=(kb == qb))
                last.then_inc(S["attended"], 1)

            for u in range(6):
                unit(u)
            pe.wait_ge(S["unit_out"], 6)
            scores(1)
            unit(6)
            unit(7)
            pe.wait_ge(S["scores_read"], 1)
            scores(0)
            unit(8)
            unit(9)
            turn_attn(1)
            unit(10)
            attend(1)
            turn_attn(0)
            unit(11)
            unit(12)
            attend(0)
            pe.wait_ge(S["mixer_in"], M0_IN)
            pe.wait_ge(S["scalar_step"], STEP["tanh_ready"])
            pe.wait_ge(S["attention_out"], 2)
            for t in range(4):
                for r in range(2):
                    rows = slice(64 * r, 64 * r + 64)
                    last = mm(ps[:, 4 + 2 * r + t // 2, (t % 2) * SEQ:(t % 2 + 1) * SEQ], lora[rows, t * P:(t + 1) * P],
                              mixT[rows, 12, :], start=True, stop=True)
                    if (t, r) == (3, 0):
                        last.then_inc(S["lora_done"], 1)
            last.then_inc(S["lora_done"], 1)
            pe.wait_ge(S["vector_step"], STEP["xg_ready"])
            for tt in range(TT):
                last = mm(ps[:, tt, :], mixT[:, 13, tt * P:(tt + 1) * P], g2_sb, start=True, stop=True)
            last.then_inc(S["tensor_step"], 1)
            pe.wait_ge(S["vector_step"], STEP["kk_squared"])
            for t in range(4):
                last = mm(ps[:, 2 + t // 2, (t % 2) * SEQ:(t % 2 + 1) * SEQ], cm(C_HALF), N[7][:, t, :], start=True, stop=True)
            last.then_inc(S["tensor_step"], 1)
            pe.wait_ge(S["vector_step"], STEP["rk_ready"])
            pe.wait_ge(S["decay_exp"], 8)
            for tt in range(TT):
                for t in range(4):
                    last = mm(ps[:, 4, tt * 8:(tt + 1) * 8], N[6][:, t, tt * P:(tt + 1) * P], cst[:, C_HEAD + 8 * t:C_HEAD + 8 * t + 8],
                              start=(t == 0), stop=(t == 3))
            last.then_inc(S["tensor_step"], 1)
            for q, src in enumerate((betaT, gammaT, mixT[:, 8:12, :], KR[:, :, 0, :])):
                if q == 0:
                    pe.wait_ge(S["vector_step"], STEP["factors_ready"])
                    pe.wait_ge(S["scalar_step"], STEP["g_copied"])
                    pe.wait_ge(S["scalar_step"], STEP["bonus_ready"])
                for tt in range(TT):
                    for t in range(4):
                        last = nc.tensor.transpose(ps[:, 2 * q + tt, t * P:(t + 1) * P], src[:, t, tt * P:(tt + 1) * P], ident)
                    last.then_inc(S["factors_turned"], 1)
            for i, src in enumerate((betaT, gammaT)):
                for tt in range(TT):
                    if i == 0:
                        pe.wait_ge(S["tm_ready"], 4 + 4 * tt)
                    else:
                        pe.wait_ge(S["pairs_out"], tt + 1)
                    for t in range(4):
                        for par in range(2):
                            rows = slice(64 * par, 64 * par + 64)
                            last = mm(ps[:, 4 * tt + 2 * par + t // 2, (t % 2) * 256:(t % 2 + 1) * 256],
                                      src[rows, t, tt * P:(tt + 1) * P], KR[rows, t, :, tt * P:(tt + 1) * P], start=True, stop=True)
                            if (t, par) == (3, 0):
                                last.then_inc(S["pairs_done"], 1)
                    last.then_inc(S["pairs_done"], 1)
            pe.wait_ge(S["pairs_out"], 4)
            for tt in range(TT):
                for h in range(8):
                    last = mm(ps[:, tt, h * 64:(h + 1) * 64], bt_[:, tt * 8 + unit0(h), 0:P], V_tm[:, tt, h * 64:(h + 1) * 64],
                              start=True, stop=True)
            last.then_inc(S["tensor_step"], 1)
            pe.wait_ge(S["scalar_step"], STEP["bv_ready"])
            solve_pe(pe, 0)
            pe.wait_ge(S["XT_ready"], 24)
            for tt in range(TT):
                for h in range(8):
                    last = mm(ps[:, tt, h * 64:(h + 1) * 64], XT_[:, tt * 8 + unit0(h), :], BV[:, tt, h * 64:(h + 1) * 64],
                              start=True, stop=True)
            last.then_inc(S["tensor_step"], 1)
            for tt in range(TT):
                for h in range(8):
                    p0 = 64 * (h % 2)
                    last = mm(ps[p0:p0 + 64, 2 + tt, (h // 2) * P:(h // 2 + 1) * P], kappa_tm[:, tt, h * 64:(h + 1) * 64],
                              XT_[:, tt * 8 + unit0(h), :], start=True, stop=True)
            last.then_inc(S["tensor_step"], 1)
            pe.wait_ge(S["vector_step"], STEP["g_ready"])
            for c in range(4):
                tt, r0 = c // 2, 64 * (c % 2)
                pe.wait_ge(S["state_ready"], c + 1)
                for t in range(4):
                    last = mm(ps[r0:r0 + 64, 4, t * P:(t + 1) * P], XKT[:, tt, t, r0:r0 + 64], Sbd[:, t, :], start=True, stop=True)
                last.then_inc(S["u_done"], 1)
                for t in range(4):
                    last = mm(ps[r0:r0 + 64, 6 + tt, t * P:(t + 1) * P], KR[:, t, 1, c * 64:(c + 1) * 64], Sbd[:, t, :],
                              start=(t == 0), stop=False, skip_group_check=True)
                last.then_inc(S["state_used"], 1)
                for h in range(8):
                    mm(ps[r0:r0 + 64, 6 + tt, h * 64:(h + 1) * 64], bt_[:, tt * 8 + unit0(h), P + r0:P + r0 + 64],
                       V_tm[:, tt, h * 64:(h + 1) * 64], start=False, stop=False, skip_group_check=True)
                pe.wait_ge(S["u_ready"], c + 1)
                if c < 3:
                    rows = slice(r0, r0 + 64)
                    for h in range(8):
                        p0 = 64 * (h % 2)
                        o = ps[p0:p0 + 64, 5, (h // 2) * 64:(h // 2 + 1) * 64]
                        hc = slice(h * 64, (h + 1) * 64)
                        mm(o, gamma_tm[rows, tt, hc], V_tm[rows, tt, hc], start=True, stop=False)
                        last = mm(o, beta_tm[rows, tt, hc], U_[rows, tt, hc], start=False, stop=True)
                    last.then_inc(S["incr_done"], 1)
                for h in range(8):
                    last = mm(ps[r0:r0 + 64, 6 + tt, h * 64:(h + 1) * 64], at_[:, tt * 8 + unit0(h), P + r0:P + r0 + 64],
                              U_[:, tt, h * 64:(h + 1) * 64], start=False, stop=(h == 7), skip_group_check=True)
                last.then_inc(S["y_done"], 1)
            pe.wait_ge(S["rwkv_out"], 1)
            for b in range(4):
                tt, half = divmod(b, 2)
                for k in range(4):
                    last = nc.tensor.transpose(ps[:, 4 + b, k * P:(k + 1) * P], y_tok[:, tt, 4 * half + k::KT], ident)
                last.then_inc(S["outs_turned"], 1)
            pe.wait_ge(S["outsT_ready"], 4)
            for h in range(2):
                n = base + 7 + h
                pe.wait_ge(*w_load(n))
                for tt in range(TT):
                    for kt in range(KT):
                        last = mm(ps[:, 2 * tt + h, :], xT[:, kt, tt * P:(tt + 1) * P], wv(n, CH)[:, kt, :],
                                  start=(kt == 0), stop=(kt == KT - 1))
                last.then_inc(S["wide_used"], 1)
                if h == 0:
                    continue

        def m0_act(act):
            A_ = nc.scalar.activation

            def unit_out(u):
                act.wait_ge(S["unit_done"], u + 1)
                if u + 2 < M0_UNITS:
                    split_high(act, "M0", u + 2)
                src = ps[:, u % 4, :].rearrange("p (t c) -> p t c", t=2)
                if u < 4:
                    nc.scalar.mul(qkT[:, 2 * u:2 * u + 2, :], src, 0.125 if u < 2 else 1.0).then_inc(S["unit_out"], 1)
                elif u < 6:
                    nc.scalar.copy(vA[:, :, (u - 4) * 256:(u - 3) * 256], src).then_inc(S["unit_out"], 1)
                else:
                    nc.scalar.copy(raw[:, 2 * (u - 6):2 * (u - 6) + 2, 1:SEQ + 1], src).then_inc(S["unit_out"], 1)

            def softmax_exp(qb):
                act.wait_ge(S["shifted"], 2 - qb)
                kw = (qb + 1) * P
                A_(sc[:, :, :, 0:kw], sc[:, :, :, 0:kw], ACT.Exp).then_inc(S["probs_ready"], 1)

            for u in range(6):
                unit_out(u)
            act.wait_ge(S["vector_step"], STEP["lam_sums"])
            A_(lam2, lam2, ACT.Exp).then_inc(S["scalar_step"], 1)
            softmax_exp(1)
            unit_out(6)
            unit_out(7)
            softmax_exp(0)
            for u in (8, 9, 10):
                unit_out(u)
            inv_root(act, arms, "attn1")
            unit_out(11)
            unit_out(12)
            inv_root(act, arms, "attn0")
            act.wait_ge(S["mixed_units"], 7)
            A_(mixT[0:64, 12, :], mixT[0:64, 12, :], ACT.Tanh).then_inc(S["scalar_step"], 1)
            A_(mixT[:, 13, :], mixT[:, 13, :], ACT.Exp, scale=-1.0).then_inc(S["scalar_step"], 1)
            act.wait_ge(S["vector_step"], STEP["ncols_ready"])
            for r in range(2):
                act.wait_ge(S["lora_done"], r + 1)
                for t in range(4):
                    A_(N[2 * r][:, t, :], ps[:, 4 + 2 * r + t // 2, (t % 2) * SEQ:(t % 2 + 1) * SEQ], ACT.Exp,
                       bias=ncols[:, 4 * r + t:4 * r + t + 1], scale=-1.0).then_inc(S["decay_exp"], 1)
            act.wait_ge(S["tensor_step"], STEP["g_done"])
            nc.scalar.copy(g_tm, ps[:, 0:2, :]).then_inc(S["scalar_step"], 1)
            inv_root(act, N[7], "kk")
            act.wait_ge(S["vector_step"], STEP["cum_ready"])
            A_(N[0], N[0], ACT.Exp, scale=-EM).then_inc(S["decays"], 1)
            A_(N[5], N[1], ACT.Exp, scale=-EM).then_inc(S["decays"], 1)
            act.wait_ge(S["decays"], 2)
            A_(N[1], N[1], ACT.Exp, scale=EM).then_inc(S["decays"], 1)
            act.wait_ge(S["tensor_step"], STEP["bonus_done"])
            nc.scalar.copy(bonus, ps[:, 4, 0:16].rearrange("p (t h) -> p t h", t=TT)).then_inc(S["scalar_step"], 1)
            for q in range(4):
                act.wait_ge(S["factors_turned"], 2 * q + 1)
                nc.scalar.copy(tm4[:, q, 0, :], ps[:, 2 * q, :]).then_inc(S["tm_a"], 1)
            act.wait_ge(S["tensor_step"], STEP["bv_done"])
            nc.scalar.copy(BV, ps[:, 0:2, :]).then_inc(S["scalar_step"], 1)
            solve_act(act, 0)
            act.wait_ge(S["tensor_step"], STEP["xk_done"])
            nc.scalar.copy(XKT, ps[:, 2:4, :].rearrange("p a (t c) -> p a t c", t=4)).then_inc(S["scalar_step"], 1)
            inv_root(act, gvar, "group_norm")
            for b in (0, 2):
                act.wait_ge(S["outs_turned"], b + 1)
                nc.scalar.copy(xT[:, 4 * (b % 2):4 * (b % 2) + 4, (b // 2) * P:(b // 2 + 1) * P],
                               ps[:, 4 + b, :].rearrange("p (k t) -> p k t", k=4)).then_inc(S["outsT_ready"], 1)

        def m0_dve(dve, v, link):
            ts_, tt_, stt = v.tensor_scalar, v.tensor_tensor, v.scalar_tensor_tensor

            def bc(c0, n=4):
                return spread(cols[:, c0:c0 + n], 2, [P, n, SEQ])

            def mix_unit(u):
                i = 2 * (u - 6)
                dve.wait_ge(S["unit_out"], u + 1)
                link(tt_(mixT[:, i:i + 2, :], raw[:, i:i + 2, 0:SEQ], raw[:, i:i + 2, 1:SEQ + 1], ALU.subtract))
                for t in (i, i + 1):
                    last = stt(out=mixT[:, t, :], in0=mixT[:, t, :], scalar=cols[:, t:t + 1], in1=raw[:, t, 1:SEQ + 1],
                               op0=ALU.mult, op1=ALU.add)
                    if t == i:
                        link(last)
                last.then_inc(S["mixed_units"], 1)

            def softmax_a(qb):
                kw = (qb + 1) * P
                k0 = (1 - qb) * P
                dve.wait_ge(S["scores_done"], 4 - 2 * qb)
                if qb == 0:
                    dve.wait_ge(S["attn_ready"], 1)
                for c in range(2):
                    if qb:
                        src = ps[:, 4 + 2 * c:6 + 2 * c, :].rearrange("p b (h k) -> p (b h) k", h=2)
                    else:
                        src = ps[:, 4 + c, :].rearrange("p (h k) -> p h k", h=4)
                    last = tt_(sc[:, c, :, 0:kw], src, alibi[:, :, k0:k0 + kw], ALU.add)
                    if c == 0:
                        link(last)
                last.then_inc(S["scores_read"], 1)
                dve.wait_ge(S["scores_read"], 2 - qb)
                link(v.tensor_reduce(smax, sc[:, :, :, 0:kw], AX, ALU.max))
                for c in range(2):
                    last = tt_(sc[:, c, :, 0:kw], sc[:, c, :, 0:kw], spread(smax[:, c, :], 2, [P, 4, kw]), ALU.subtract)
                    if c == 0:
                        link(last)
                last.then_inc(S["shifted"], 1)

            def softmax_b(qb):
                kw = (qb + 1) * P
                dve.wait_ge(S["probs_ready"], 2 - qb)
                link(v.tensor_reduce(ssum, sc[:, :, :, 0:kw], AX, ALU.add))
                link(v.reciprocal(ssum, ssum))
                link(ts_(ssum[:, 1, :], ssum[:, 1, :], lam[:, 0:1], None, ALU.mult))
                for c in range(2):
                    link(tt_(sc[:, c, :, 0:kw], sc[:, c, :, 0:kw], spread(ssum[:, c, :], 2, [P, 4, kw]), ALU.mult))
                if qb == 0:
                    dve.wait_ge(S["attn_turned"], 1)
                tt_(attn[:, :, 0:kw], sc[:, 0, :, 0:kw], sc[:, 1, :, 0:kw], ALU.subtract).then_inc(S["attn_ready"], 1)

            def attnT_out(qb):
                dve.wait_ge(S["attn_turned"], 2 - qb)
                if qb:
                    v.tensor_copy(attnT, ps[:, 6:8, :].rearrange("p b (h k c) -> p (b h) k c", h=2, k=2)).then_inc(S["attnT_ready"], 1)
                else:
                    dve.wait_ge(S["attended"], 1)
                    v.tensor_copy(attnT[:, :, 0, :], ps[:, 5, :].rearrange("p (h c) -> p h c", h=4)).then_inc(S["attnT_ready"], 1)

            def head_norm(qb):
                dve.wait_ge(S["attended"], 2 - qb)
                o = y_tok[:, qb, 0:512]
                o3 = o.rearrange("p (h c) -> p h c", h=4)
                sq = y_tok[:, qb, 512:1024]
                link(v.tensor_copy(o, ps[:, 4 if qb else 6, :]))
                link(tt_(sq, o, o, ALU.mult))
                link(v.tensor_reduce(arms, sq.rearrange("p (h c) -> p h c", h=4), AX, ALU.add))
                ts_(arms, arms, 1.0 / P, 1e-5, ALU.mult, ALU.add).then_inc(S["square_ready"], 1)
                dve.wait_ge(S["root_ready"], 2 * ROOT[f"attn{qb}"])
                link(tt_(o3, o3, spread(arms, 2, [P, 4, P]), ALU.mult))
                tt_(o3, o3, spread(ang, 1, [P, 4, P]), ALU.mult).then_inc(S["attention_out"], 1)
                dve.wait_ge(S["attention_out"], 2 - qb)

            link(v.memset(raw[:, :, 0:1], 0.0))
            dve.wait_ge(S["mixer_in"], M0_IN)
            link(tt_(al[:, 0::2, :], al[:, 0::2, :], al[:, 1::2, :], ALU.mult))
            v.tensor_reduce(lam2, al[:, 0::2, :], AX, ALU.add).then_inc(S["vector_step"], 1)
            dve.wait_ge(S["scalar_step"], STEP["lam_exp"])
            LAM0 = 0.8 - 0.6 * math.exp(-0.3 * 0)
            link(ts_(lam, lam2[:, 0:1], lam2[:, 1:2], LAM0, ALU.subtract, ALU.add))
            link(ts_(ang, ang, 1.0 - LAM0, None, ALU.mult))
            ts_(ncols, cols[:, 14:22], -1.0, None, ALU.mult).then_inc(S["vector_step"], 1)
            softmax_a(1)
            softmax_b(1)
            softmax_a(0)
            mix_unit(6)
            mix_unit(7)
            attnT_out(1)
            softmax_b(0)
            mix_unit(8)
            mix_unit(9)
            attnT_out(0)
            head_norm(1)
            mix_unit(10)
            head_norm(0)
            mix_unit(11)
            mix_unit(12)
            dve.wait_ge(S["mixed_units"], 7)
            rT, kT = mixT[:, 0:4, :], mixT[:, 4:8, :]
            link(tt_(N[3], kT, bc(22), ALU.mult))
            tt_(N[7], N[3], N[3], ALU.mult).then_inc(S["vector_step"], 1)
            dve.wait_ge(S["scalar_step"], STEP["xg_exp"])
            link(ts_(mixT[:, 13, :], mixT[:, 13, :], 1.0, None, ALU.add))
            v.reciprocal(mixT[:, 13, :], mixT[:, 13, :]).then_inc(S["vector_step"], 1)
            dve.wait_ge(S["decay_exp"], 4)
            link(ts_(N[0], N[0], 1.0, None, ALU.add))
            link(v.reciprocal(N[0], N[0]))
            for t in range(4):
                for c in range(4):
                    cc = slice(64 * c, 64 * c + 64)
                    link(v.tensor_tensor_scan(N[1][:, t, cc], cst[:, C_ONES:C_ONES + 64], N[0][:, t, cc], 0.0, ALU.mult, ALU.add))
            tt_(N[0], N[1], N[0], ALU.subtract).then_inc(S["vector_step"], 1)
            dve.wait_ge(S["tensor_step"], STEP["kk_norm"])
            ts_(N[7], ps[:, 2:4, :].rearrange("p b (t c) -> p (b t) c", t=2), 1e-6, None, ALU.add).then_inc(S["square_ready"], 1)
            dve.wait_ge(S["decay_exp"], 8)
            link(ts_(N[2], N[2], 1.0, None, ALU.add))
            link(v.reciprocal(N[2], N[2]))
            for t in range(4):
                link(ts_(N[4][:, t, :], N[2][:, t, :], 1.0, cols[:, 26 + t:27 + t], ALU.subtract, ALU.mult))
            link(stt(out=N[4], in0=N[4], scalar=1.0, in1=kT, op0=ALU.add, op1=ALU.mult))
            link(tt_(N[6], rT, N[4], ALU.mult))
            tt_(N[6], N[6], bc(30), ALU.mult).then_inc(S["vector_step"], 1)
            dve.wait_ge(S["root_ready"], 2 * ROOT["kk"])
            link(tt_(N[3], N[3], N[7], ALU.mult))
            dve.wait_ge(S["decays"], 3)
            link(tt_(KR[:, :, 0, :], N[0], N[3], ALU.mult))
            link(tt_(KR[:, :, 1, :], N[5], rT, ALU.mult))
            link(tt_(N[3], N[3], N[2], ALU.mult))
            link(tt_(betaT, N[3], N[1], ALU.mult))
            link(v.tensor_copy(lamC, N[5][:, :, 63::64]))
            tt_(gammaT, N[4], N[1], ALU.mult).then_inc(S["vector_step"], 1)
            for q in range(4):
                dve.wait_ge(S["factors_turned"], 2 * q + 2)
                dve.wait_ge(S["tm_a"], q + 1)
                v.tensor_copy(tm4[:, q, 1, :], ps[:, 2 * q + 1, :]).then_inc(S["tm_ready"], 2)
            mask = spread(cst[:, C_STRICT:C_STRICT + 2 * P], 1, [P, 8, 2 * P])
            for i, dst in enumerate((at_, bt_)):
                for tt in range(TT):
                    dve.wait_ge(S["pairs_done"], 2 * (2 * i + tt) + 2)
                    tt_(dst[:, 8 * tt:8 * tt + 8, :], ps[:, 4 * tt:4 * tt + 4, :].rearrange("p b (u c) -> p (b u) c", u=2), mask, ALU.mult
                        ).then_inc(S["pairs_out"], 1)
                if i == 0:
                    dve.wait_ge(S["pairs_out"], 2)
                    v.engine_nop().then_inc(S["AT_ready"], 1)
            solve_dve(dve, v, 0)
            dve.wait_ge(S["tensor_step"], STEP["xg2_done"])
            v.tensor_copy(G_, ps[:, 0:2, :]).then_inc(S["vector_step"], 1)
            link(v.memset(U_, 0.0))
            dve.wait_ge(S["vector_step"], STEP["g_ready"])
            dve.wait_ge(S["scalar_step"], STEP["xk_ready"])
            v.memset(Sbd, 0.0).then_inc(S["state_ready"], 1)
            for c in range(4):
                tt, r0 = c // 2, 64 * (c % 2)
                rows = slice(r0, r0 + 64)
                dve.wait_ge(S["u_done"], c + 1)
                stt(out=U_[rows, tt, :], in0=ps[rows, 4, :], scalar=-1.0, in1=G_[rows, tt, :], op0=ALU.mult, op1=ALU.subtract
                    ).then_inc(S["u_ready"], 1)
                if c < 3:
                    dve.wait_ge(S["state_used"], c + 1)
                    dve.wait_ge(S["incr_done"], c + 1)
                    for par in range(2):
                        pr = slice(64 * par, 64 * par + 64)
                        s_ = Sbd[pr, :, 64 * par:64 * par + 64]
                        link(tt_(s_, s_, ps[pr, 5, 0:256].rearrange("p (t c) -> p t c", t=4), ALU.add))
                        last = tt_(s_, s_, spread(lamC[pr, :, c], 2, [64, 4, 64]), ALU.mult)
                        if par == 0:
                            link(last)
                    last.then_inc(S["state_ready"], 1)
                    dve.wait_ge(S["state_ready"], c + 2)
                if c % 2:
                    dve.wait_ge(S["y_done"], c + 1)
                    link(v.tensor_copy(Yr[:, tt], ps[:, 6 + tt, :].rearrange("p (h c) -> p h c", h=8)))
            Y = Yr.rearrange("p t h c -> p (t h) c")
            Yt = Ytmp.rearrange("p t h c -> p (t h) c")
            link(v.tensor_reduce(gmu, Y, AX, ALU.add))
            link(ts_(gmu, gmu, 1.0 / 64, None, ALU.mult))
            link(tt_(Y, Y, spread(gmu, 2, [P, 16, 64]), ALU.subtract))
            link(tt_(Yt, Y, Y, ALU.mult))
            link(v.tensor_reduce(gvar, Yt, AX, ALU.add))
            ts_(gvar, gvar, 1.0 / 64, 64e-5, ALU.mult, ALU.add).then_inc(S["square_ready"], 1)
            dve.wait_ge(S["scalar_step"], STEP["bonus_ready"])
            link(tt_(Yt, V_tm.rearrange("p t (h c) -> p (t h) c", h=8), spread(bonus.rearrange("p t h -> p (t h)"), 2, [P, 16, 64]), ALU.mult))
            dve.wait_ge(S["root_ready"], 2 * ROOT["group_norm"])
            link(tt_(Y, Y, spread(gvar, 2, [P, 16, 64]), ALU.mult))
            Y2, Yt2 = (z.rearrange("p t h c -> p t (h c)") for z in (Yr, Ytmp))
            link(tt_(Y2, Y2, spread(lnxg, 1, [P, TT, 512]), ALU.mult))
            link(tt_(Y2, Y2, spread(lnxb, 1, [P, TT, 512]), ALU.add))
            link(tt_(Y2, Y2, Yt2, ALU.add))
            dve.wait_ge(S["scalar_step"], STEP["g_copied"])
            tt_(y_tok[:, :, 512:1024], Y2, g_tm, ALU.mult).then_inc(S["rwkv_out"], 1)
            for b in (1, 3):
                dve.wait_ge(S["outs_turned"], b + 1)
                v.tensor_copy(xT[:, 4 * (b % 2):4 * (b % 2) + 4, (b // 2) * P:(b // 2 + 1) * P],
                              ps[:, 4 + b, :].rearrange("p (k t) -> p k t", k=4)).then_inc(S["outsT_ready"], 1)
            dve.wait_ge(S["wide_used"], RING + wide_at["M0"] + 9)

        M1_UNITS, VH, KH = 24, 16, 8
        qkF = area(0, 16, SEQ)
        yT16 = area(0, 16, SEQ)
        k_tm = area(4096, TT, KH, P)
        v_tm = area(6144, TT, VH, P)
        z_tm = area(10240, TT, VH, P)
        aT_ = area(14336, VH, P)
        St = area(16384, VH, P)
        craw = area(16384, 2, 2, SEQ + 4)
        cacc = area(17424, 2, 2, SEQ)
        ccols = area(18448, 32, 4)
        o_ms = area(18576, TT, VH)
        lngf = lng[:, :]
        w_ba = area(0, KT, 32, base=lngf)
        ong = area(256, P, base=lngf)
        alog = area(384, VH, base=lngf)
        dtb = area(400, VH, base=lngf)
        beta = area(416, TT, VH, base=lngf)
        xa = area(448, TT, VH, base=lngf)
        ab = area(480, TT, VH, base=lngf)
        gg = area(512, TT, VH, base=lngf)
        gcs = area(544, TT, VH, base=lngf)
        eg = area(576, TT, VH, base=lngf)
        kd = area(608, TT, VH, base=lngf)
        bg = area(640, TT, VH, base=lngf)
        glb = area(672, 4, VH, base=lngf)
        wflat = wide[:, :, :].rearrange("p a b -> p (a b)")
        X1, XT1, T11, QT1, AT1, vb, kbg, Ed = (area(2048 * i, VH, P, base=wflat) for i in range(8))
        Dr, A1, at1 = X1, XT1, T11
        u_, wT, kdec, vnew = (area(2048 * i, VH, P, base=nflat) for i in range(4))
        M1_IN = 16 * 5
        xF = area(6144, KT, SEQ)
        SUMS_AT = (7, 9, 11, 13)

        def squares(b):
            return area(4096 + 1024 * (b % 2), 4, SEQ)

        def norms(b):
            return area(11264 + 2048 * (b % 2), 4, SEQ)

        norm_pair = area(10240, 2, 2048)[:, :, 1024:2048]

        GSTEP = {name: n + 1 for n, name in enumerate(("craw_zero", "gates_ready", "kd_ready", "vnew_zero"))}
        had = 1 if "M0" in stages else 0
        U0, P0, B3, B4 = 13 * had, M0_IN * had, 3 * had, 4 * had

        def m1_loads(sp, wide_chunk):
            w_in = a["l1_w_in"].rearrange("(p k) c -> p k c", k=KT)
            n = wide_at["M1"]
            for c in range(12):
                wide_chunk(n + c, w_in[:, :, c * CH:(c + 1) * CH])
            w_out = a["l1_w_out"].rearrange("(p k) c -> p k c", k=16)
            sp.wait_ge(S["uw_out"], 4)
            for c in range(4):
                wide_chunk(n + 12 + c, w_out[:, 4 * c:4 * c + 4, :])
            sp.wait_ge(S["gdn_out"], 2)

        def m1_params(pool):
            split_low(pool, nc.gpsimd, "M1", 0)
            split_low(pool, nc.gpsimd, "M1", 1)
            if len(stages) > 1 and stages[0] != "M1":
                pool.wait_ge(S["ln_done"], stages.index("M1"))
            pool.dma_start(w_ba, a["l1_w_in"].rearrange("(p k) c -> p k c", k=KT)[:, :, 6144:6176]).then_inc(S["mixer_in"], 16)
            pool.dma_start(ccols, a["l1_conv_cols"].rearrange("p (t j) -> p t j", j=4)).then_inc(S["mixer_in"], 16)
            pool.dma_start(ong, a["l1_norm_g"].partition_broadcast(P)).then_inc(S["mixer_in"], 16)
            pool.dma_start(alog, a["l1_a_log"].partition_broadcast(P)).then_inc(S["mixer_in"], 16)
            pool.dma_start(dtb, a["l1_dt_bias"].partition_broadcast(P)).then_inc(S["mixer_in"], 16)
            TTg = nc.gpsimd.tensor_tensor
            split_low(pool, nc.gpsimd, "M1", 2)
            pool.wait_ge(S["xT_ready"], 4 * (stages.index("M1") + 1))
            TTg(xF, xT_hi[:, :, :].bitcast(F32), xT_lo1[:, :, :].bitcast(F32), ALU.add).then_inc(S["x_high"], 1)
            for u in range(4, M1_UNITS, 2):
                split_low(pool, nc.gpsimd, "M1", u)
            for r in range(2):
                pool.wait_ge(S["gdn_step"], GSTEP["gates_ready"])
                pool.wait_ge(S["unit_out"], U0 + M1_UNITS)
                if r:
                    pool.wait_ge(S["uw_out"], 2)
                for b in range(4):
                    TTg(Dr[:, 4 * b:4 * b + 4, :], spread(cm(C_SEG), 1, [P, 4, P]),
                        spread(gg[:, r, 4 * b:4 * b + 4], 2, [P, 4, P]), ALU.mult).then_inc(S["seg_ready"], 1)
                kk = spread(k_tm[:, r], 2, [P, KH, 2, P])
                pool.wait_ge(S["k_tm_ready"], 4)
                TTg(kbg.rearrange("p (h r) c -> p h r c", r=2), kk,
                    spread(bg[:, r, :].rearrange("p (h r) -> p h r", r=2), 3, [P, KH, 2, P]), ALU.mult).then_inc(S["kbg_ready"], 1)
                if r:
                    pool.wait_ge(S["incr_done"], B3 + 8)
                TTg(kdec.rearrange("p (h r) c -> p h r c", r=2), kk,
                    spread(kd[:, r, :].rearrange("p (h r) -> p h r", r=2), 3, [P, KH, 2, P]), ALU.mult).then_inc(S["kdec_ready"], 1)
                solve_pool(pool, SOLVE1 + r, AT1)
            pool.wait_ge(S["gdn_out"], 2)

        def m1_pe(pe):
            mm = nc.tensor.matmul
            tr = nc.tensor.transpose
            base = wide_at["M1"]
            for u in range(M1_UNITS):
                project(pe, "M1", u, u >= 16)
                if u == 3:
                    pe.wait_ge(S["mixer_in"], P0 + M1_IN)
                    pe.wait_ge(S["x_high"], X0["M1"] + 5)
                    for tt in range(TT):
                        for kt in range(KT):
                            last = mm(ps[:, 5, tt * 32:(tt + 1) * 32], xF[:, kt, tt * P:(tt + 1) * P], w_ba[:, kt, :],
                                      start=(kt == 0), stop=(kt == KT - 1))
                    last.then_inc(S["ba_done"], 1)
                if u == 5:
                    pe.wait_ge(S["gdn_step"], GSTEP["gates_ready"])
                    for tt in range(TT):
                        mm(ps[:, 7, tt * VH:(tt + 1) * VH], cm(C_INCL), gg[:, tt, :], start=True, stop=True)
                        mm(ps[:, 7, (2 + tt) * VH:(3 + tt) * VH], cm(C_HALF), gg[:, tt, :], start=True, stop=True)
                        for hf in range(2):
                            for o in range(2):
                                c = 2 * tt + hf
                                last = mm(ps[64 * o:64 * o + 64, 7, (4 + c) * VH:(5 + c) * VH],
                                          cst[:, C_HALF + 64 * hf:C_HALF + 64 * hf + 64], gg[:, tt, :], start=True, stop=True)
                    last.then_inc(S["gsums_done"], 1)
                if 10 <= u <= 17:
                    w = u - 2
                    pe.wait_ge(S["conv_act"], w + 1)
                    if w >= 10:
                        pe.wait_ge(S["v_out"], w - 9)
                    for tt in range(TT):
                        for t in range(2):
                            last = tr(ps[:, 4 + w % 2, tt * 256 + t * P:tt * 256 + (t + 1) * P], cacc[:, w % 2, t, tt * P:(tt + 1) * P], ident)
                    last.then_inc(S["v_turned"], 1)
                if u in SUMS_AT:
                    b = SUMS_AT.index(u)
                    pe.wait_ge(S["sq_ready"], b + 1)
                    if b:
                        pe.wait_ge(S["square_ready"], ROOT[f"qk{b - 1}"])
                    else:
                        pe.wait_ge(S["gsums_out"], 3)
                    for t in range(4):
                        last = mm(ps[:, 6 + t // 2, (t % 2) * SEQ:(t % 2 + 1) * SEQ], cm(C_ONES), squares(b)[:, t, :], start=True, stop=True)
                    last.then_inc(S["ss_done"], 1)
                if u in (18, 20):
                    b = (u - 18) // 2
                    pe.wait_ge(S["qk_normed"], 3 + b)
                    if b:
                        pe.wait_ge(S["k_tm_ready"], 2)
                    for tt in range(TT):
                        for t in range(4):
                            last = tr(ps[:, 6 + tt, t * P:(t + 1) * P], qkF[:, 8 + 4 * b + t, tt * P:(tt + 1) * P], ident)
                        last.then_inc(S["k_turned"], 1)
            for r in range(2):
                tok = slice(r * P, (r + 1) * P)
                for b in range(4):
                    pe.wait_ge(S["seg_ready"], 4 * r + b + 1)
                    if r == 0:
                        pe.wait_ge(S["unit_out"], U0 + M1_UNITS)
                    else:
                        pe.wait_ge(S["state_ready"], B4 + 8 + b + 1)
                    mm(ps[:, b, :], cm(C_INCL), Dr[:, 4 * b:4 * b + 4, :].rearrange("p u c -> p (u c)"), start=True, stop=True
                       ).then_inc(S["dsum_done"], 1)
                if r == 0:
                    pe.wait_ge(S["k_tm_ready"], 4)
                    pe.wait_ge(S["v_out"], 8)
                else:
                    pe.wait_ge(S["o_out"], 8)
                for i, q0 in enumerate((8, 0)):
                    for h in range(KH):
                        last = mm(ps[:, 4 + 2 * i + h // 4, (h % 4) * P:(h % 4 + 1) * P], qkF[:, q0 + h, tok], qkF[:, 8 + h, tok],
                                  start=True, stop=True)
                    last.then_inc(S["kkqk_done"], 1)
                for b in range(4):
                    pe.wait_ge(S["A_ready"], 4 * r + b + 1)
                    for t in range(4):
                        last = tr(ps[:, b, t * P:(t + 1) * P], A1[:, 4 * b + t, :], ident)
                    last.then_inc(S["A_turned"], 1)
                for b in range(4):
                    pe.wait_ge(S["at_ready"], 4 * r + 4)
                    for t in range(4):
                        last = tr(ps[:, 4 + b, t * P:(t + 1) * P], at1[:, 4 * b + t, :], ident)
                    last.then_inc(S["at_turned"], 1)
                pe.wait_ge(S["aT_out"], 4 * r + 4)
                solve_pe(pe, SOLVE1 + r)
                pe.wait_ge(S["XT_ready"], 24 * (SOLVE1 + r) + 24)
                pe.wait_ge(S["vb_ready"], r + 1)
                pe.wait_ge(S["kbg_ready"], r + 1)
                for b in range(4):
                    for t in range(4):
                        last = mm(ps[:, b, t * P:(t + 1) * P], XT1[:, 4 * b + t, :], vb[:, 4 * b + t, :], start=True, stop=True)
                    last.then_inc(S["u1_done"], 1)
                for b in range(4):
                    for t in range(4):
                        last = mm(ps[:, 4 + b, t * P:(t + 1) * P], kbg[:, 4 * b + t, :], XT1[:, 4 * b + t, :], start=True, stop=True)
                    last.then_inc(S["w1_done"], 1)
                pe.wait_ge(S["uw_out"], 2 * r + 2)
                pe.wait_ge(S["kdec_ready"], r + 1)
                for hf in range(2):
                    c = 2 * r + hf
                    r0 = 64 * hf
                    rows = slice(r0, r0 + 64)
                    for b in range(4):
                        pe.wait_ge(S["state_ready"], B4 + 4 * c + b + 1)
                        for t in range(4):
                            last = mm(ps[rows, b, t * P:(t + 1) * P], wT[:, 4 * b + t, rows], St[:, 4 * b + t, :], start=True, stop=True)
                        last.then_inc(S["wS_done"], 1)
                        if hf:
                            pe.wait_ge(S["o_out"], 4 * (c - 1) + b + 1)
                        for t in range(2):
                            last = mm(ps[rows, 4 + b, t * 2 * P:(t + 1) * 2 * P], qkF[:, 2 * b + t, c * 64:(c + 1) * 64],
                                      St[:, 4 * b + 2 * t:4 * b + 2 * t + 2, :].rearrange("p u c -> p (u c)"), start=True, stop=True)
                        last.then_inc(S["qS_done"], 1)
                    for b in range(4):
                        pe.wait_ge(S["vnew_ready"], 4 * c + b + 1)
                        for t in range(4):
                            last = mm(ps[:, b, t * P:(t + 1) * P], kdec[rows, 4 * b + t, :], vnew[rows, 4 * b + t, :], start=True, stop=True)
                        last.then_inc(S["incr_done"], 1)
                    for b in range(4):
                        pe.wait_ge(S["qS_read"], 4 * c + b + 1)
                        for t in range(4):
                            last = mm(ps[rows, 4 + b, t * P:(t + 1) * P], aT_[:, 4 * b + t, rows], vnew[:, 4 * b + t, :], start=True, stop=True)
                        last.then_inc(S["av_done"], 1)
            for i in range(8):
                tt, q = divmod(i, 4)
                pe.wait_ge(S["gdn_out"], tt + 1)
                if i == 0:
                    pe.wait_ge(S["state_ready"], B4 + 20)
                o2 = v_tm[:, tt].rearrange("p h c -> p (h c)")
                for k in range(4):
                    last = tr(ps[:, i, k * P:(k + 1) * P], o2[:, 4 * q + k::16], ident)
                last.then_inc(S["outs_turned"], 1)
            pe.wait_ge(S["outsT_ready"], B4 + 8)
            for j in range(4):
                n = base + 12 + j
                pe.wait_ge(*w_load(n))
                w4 = wide[:, n % RING, :].rearrange("p (k c) -> p k c", k=4)
                for tt in range(TT):
                    for h in range(2):
                        for k in range(4):
                            last = mm(ps[:, 2 * tt + h, :], yT16[:, 4 * j + k, tt * P:(tt + 1) * P], w4[:, k, h * 512:(h + 1) * 512],
                                      start=(j == 0 and k == 0), stop=(j == 3 and k == 3))
                last.then_inc(S["wide_used"], 1)

        def m1_act(act):
            A_ = nc.scalar.activation
            def gates():
                act.wait_ge(S["ba_done"], 1)
                ba = ps[:, 5, 0:64].rearrange("p (t c) -> p t c", t=TT)
                A_(beta, ba[:, :, 0:VH], ACT.Exp, scale=-1.0).then_inc(S["beta_exp"], 1)
                A_(alog, alog, ACT.Exp).then_inc(S["beta_exp"], 1)
                act.wait_ge(S["abs_ready"], 1)
                A_(ab, ab, ACT.Exp, scale=-1.0).then_inc(S["abs_exp"], 1)
                act.wait_ge(S["abs_ready"], 2)
                A_(ab, ab, ACT.Ln).then_inc(S["abs_exp"], 1)

            def silu_unit(u):
                act.wait_ge(S["conv_done"], u + 1)
                dst = qkF[:, 2 * u:2 * u + 2, :] if u < 8 else cacc[:, u % 2]
                A_(dst, cacc[:, u % 2], ACT.Silu).then_inc(S["conv_act"], 1)

            def v_unit(u):
                act.wait_ge(S["v_turned"], u - 7)
                nc.scalar.copy(v_tm[:, :, 2 * (u - 8):2 * (u - 8) + 2, :],
                               ps[:, 4 + u % 2, :].rearrange("p (a b c) -> p a b c", a=TT, b=2)).then_inc(S["v_out"], 1)

            for u in range(M1_UNITS):
                if u == 4:
                    gates()
                act.wait_ge(S["unit_done"], U0 + u + 1)
                if u == 20:
                    act.wait_ge(S["qk_normed"], 4)
                if u < 16:
                    if u >= 2:
                        act.wait_ge(S["conv_done"], u - 1)
                    else:
                        act.wait_ge(S["gdn_step"], GSTEP["craw_zero"])
                    nc.scalar.copy(craw[:, u % 2, :, 3:SEQ + 3], ps[:, u % 4, :].rearrange("p (t c) -> p t c", t=2)
                                   ).then_inc(S["unit_out"], 1)
                else:
                    A_(z_tm[:, :, 2 * (u - 16):2 * (u - 16) + 2, :], ps[:, u % 4, :].rearrange("p (a b c) -> p a b c", a=TT, b=2),
                       ACT.Silu).then_inc(S["unit_out"], 1)
                if u + 2 < M1_UNITS:
                    split_high(act, "M1", u + 2)
                if 1 <= u <= 16:
                    silu_unit(u - 1)
                if 11 <= u <= 18:
                    v_unit(u - 3)
                if u == 6:
                    act.wait_ge(S["gsums_done"], 1)
                    A_(eg, ps[:, 7, 0:2 * VH].rearrange("p (t h) -> p t h", t=TT), ACT.Exp).then_inc(S["gsums_out"], 1)
                    A_(glb, ps[:, 7, 4 * VH:8 * VH].rearrange("p (t h) -> p t h", t=4), ACT.Exp).then_inc(S["gsums_out"], 1)
                    act.wait_ge(S["gdn_step"], GSTEP["kd_ready"])
                    A_(kd, kd, ACT.Exp).then_inc(S["kd_exp"], 1)
                if u in (11, 15):
                    inv_root(act, norm_pair, "qk1" if u == 11 else "qk3", 2)
            for r in range(2):
                for b in range(4):
                    act.wait_ge(S["dsum_done"], 4 * r + b + 1)
                    A_(Ed[:, 4 * b:4 * b + 4, :], ps[:, b, :].rearrange("p (u c) -> p u c", u=4), ACT.Exp).then_inc(S["seg_exp"], 1)
                for b in range(4):
                    act.wait_ge(S["at_turned"], 4 * r + b + 1)
                    if r:
                        act.wait_ge(S["av_done"], 8)
                    nc.scalar.copy(aT_[:, 4 * b:4 * b + 4, :], ps[:, 4 + b, :].rearrange("p (u c) -> p u c", u=4)).then_inc(S["aT_out"], 1)
                solve_act(act, SOLVE1 + r)
                if r:
                    inv_root(act, o_ms[:, 0, :], "gdn0")
                act.wait_ge(S["w1_done"], 4 * r + 4)
                nc.scalar.copy(wT, ps[:, 4:8, :].rearrange("p b (u c) -> p (b u) c", u=4)).then_inc(S["uw_out"], 1)
            inv_root(act, o_ms[:, 1, :], "gdn1")
            for i in (0, 2, 4, 6):
                tt, q = divmod(i, 4)
                act.wait_ge(S["outs_turned"], B4 + i + 1)
                nc.scalar.copy(yT16[:, 4 * q:4 * q + 4, tt * P:(tt + 1) * P], ps[:, i, :].rearrange("p (k t) -> p k t", k=4)
                               ).then_inc(S["outsT_ready"], 1)

        def m1_dve(dve, v, link):
            ts_, tt_, stt = v.tensor_scalar, v.tensor_tensor, v.scalar_tensor_tensor
            v.memset(craw[:, :, :, 0:3], 0.0).then_inc(S["gdn_step"], 1)
            def gates():
                dve.wait_ge(S["ba_done"], 1)
                dve.wait_ge(S["beta_exp"], 2)
                link(tt_(xa, ps[:, 5, 0:64].rearrange("p (t c) -> p t c", t=TT)[:, :, VH:2 * VH], spread(dtb, 1, [P, TT, VH]), ALU.add))
                link(ts_(ab, xa, -1.0, None, ALU.mult))
                tt_(ab, ab, xa, ALU.max).then_inc(S["abs_ready"], 1)
                dve.wait_ge(S["abs_exp"], 1)
                ts_(ab, ab, 1.0, None, ALU.add).then_inc(S["abs_ready"], 1)
                link(ts_(beta, beta, 1.0, None, ALU.add))
                link(v.reciprocal(beta, beta))
                dve.wait_ge(S["abs_exp"], 2)
                link(stt(out=gg, in0=xa, scalar=0.0, in1=ab, op0=ALU.max, op1=ALU.add))
                stt(out=gg, in0=gg, scalar=-1.0, in1=spread(alog, 1, [P, TT, VH]), op0=ALU.mult, op1=ALU.mult).then_inc(S["gdn_step"], 1)

            def conv(u):
                dve.wait_ge(S["unit_out"], U0 + u + 1)
                if 2 <= u < 10:
                    dve.wait_ge(S["conv_act"], u - 1)
                elif u >= 10:
                    dve.wait_ge(S["v_turned"], u - 9)
                for j in range(4):
                    for t in range(2):
                        w = ccols[:, 2 * u + t, j:j + 1]
                        src = craw[:, u % 2, t, j:j + SEQ]
                        dst = cacc[:, u % 2, t, :]
                        if j == 0:
                            last = ts_(dst, src, w, None, ALU.mult)
                        else:
                            last = stt(out=dst, in0=src, scalar=w, in1=dst, op0=ALU.mult, op1=ALU.add)
                        if (j, t) != (3, 1):
                            link(last)
                last.then_inc(S["conv_done"], 1)

            for u in range(22):
                if u == 0:
                    dve.wait_ge(S["mixer_in"], P0 + M1_IN)
                if u == 4:
                    gates()
                if u < 16:
                    conv(u)
                if u % 2:
                    split_low(dve, v, "M1", u + 2)
                if u == 6:
                    dve.wait_ge(S["gsums_done"], 1)
                    dve.wait_ge(S["gsums_out"], 2)
                    link(v.tensor_copy(gcs, ps[:, 7, 0:2 * VH].rearrange("p (t h) -> p t h", t=TT)))
                    tt_(kd, ps[:, 7, 2 * VH:4 * VH].rearrange("p (t h) -> p t h", t=TT), gcs, ALU.subtract).then_inc(S["gdn_step"], 1)
                    link(tt_(bg, beta, eg, ALU.mult))
                    dve.wait_ge(S["gdn_step"], GSTEP["kd_ready"])
                    v.engine_nop().then_inc(S["gsums_out"], 1)
                if u + 1 in SUMS_AT:
                    b = SUMS_AT.index(u + 1)
                    dve.wait_ge(S["conv_act"], 2 * b + 2)
                    if b >= 2:
                        dve.wait_ge(S["ss_done"], b - 1)
                    q4 = qkF[:, 4 * b:4 * b + 4, :]
                    tt_(squares(b), q4, q4, ALU.mult).then_inc(S["sq_ready"], 1)
                if u in (12, 16):
                    for b in ((0, 1) if u == 12 else (2, 3)):
                        dve.wait_ge(S["root_ready"], 2 * ROOT["qk1" if u == 12 else "qk3"])
                        q4 = qkF[:, 4 * b:4 * b + 4, :]
                        tt_(q4, q4, norms(b), ALU.mult).then_inc(S["qk_normed"], 1)
                if u - 1 in SUMS_AT:
                    b = SUMS_AT.index(u - 1)
                    dve.wait_ge(S["ss_done"], b + 1)
                    if b >= 2:
                        dve.wait_ge(S["qk_normed"], b - 1)
                    ts_(norms(b), ps[:, 6:8, :].rearrange("p b (t c) -> p (b t) c", t=2), 1e-6, float(P) if b < 2 else 1.0,
                        ALU.add, ALU.mult).then_inc(S["square_ready"], 1)
                if u in (19, 21):
                    b = (u - 19) // 2
                    for tt in range(TT):
                        dve.wait_ge(S["k_turned"], 2 * b + tt + 1)
                        v.tensor_copy(k_tm[:, tt, 4 * b:4 * b + 4, :], ps[:, 6 + tt, :].rearrange("p (t c) -> p t c", t=4)
                                      ).then_inc(S["k_tm_ready"], 1)
            dve.wait_ge(S["qk_normed"], 4)
            dve.wait_ge(S["v_turned"], 8)
            dve.wait_ge(S["unit_out"], U0 + M1_UNITS)
            v.memset(St, 0.0).then_inc(S["state_ready"], 1)
            for _ in range(3):
                dve.wait_ge(S["state_ready"], B4 + 1)
                v.engine_nop().then_inc(S["state_ready"], 1)
            v.memset(vnew, 0.0).then_inc(S["gdn_step"], 1)
            dve.wait_ge(S["gdn_step"], GSTEP["vnew_zero"])
            def head_norm(r, step):
                o = v_tm[:, r]
                scratch = St if r else Ed
                if step == 0:
                    dve.wait_ge(S["o_out"], 8 * r + 8)
                    link(tt_(scratch, o, o, ALU.mult))
                elif step == 1:
                    link(v.tensor_reduce(o_ms[:, r, :], scratch, AX, ALU.add))
                    ts_(o_ms[:, r, :], o_ms[:, r, :], 1.0 / P, 1e-6, ALU.mult, ALU.add).then_inc(S["square_ready"], 1)
                elif step == 2:
                    link(tt_(o, o, z_tm[:, r], ALU.mult))
                else:
                    dve.wait_ge(S["root_ready"], 2 * ROOT[f"gdn{r}"])
                    tt_(o, o, spread(o_ms[:, r, :], 2, [P, VH, P]), ALU.mult).then_inc(S["gdn_out"], 1)

            def beside_solve(r, n):
                if r == 0:
                    if n in (8, 12):
                        z = z_tm[:, n // 4 - 2]
                        link(tt_(z, z, spread(ong, 1, [P, VH, P]), ALU.mult))
                elif n in (4, 8, 12, 19):
                    head_norm(0, 3 if n == 19 else n // 4 - 1)

            for r in range(2):
                for b in range(4):
                    blk = slice(4 * b, 4 * b + 4)
                    dve.wait_ge(S["seg_exp"], 4 * r + b + 1)
                    link(tt_(Ed[:, blk, :], Ed[:, blk, :], spread(cm(C_LOW), 1, [P, 4, P]), ALU.mult))
                dve.wait_ge(S["kkqk_done"], 2 * r + 2)
                for b in range(4):
                    blk = slice(4 * b, 4 * b + 4)
                    e4 = Ed[:, blk, :].rearrange("p (h r) c -> p h r c", r=2)

                    def pair(bank):
                        return spread(ps[:, bank + b // 2, (b % 2) * 2 * P:(b % 2 + 1) * 2 * P].rearrange("p (h c) -> p h c", h=2), 2, [P, 2, 2, P])
                    link(tt_(A1[:, blk, :].rearrange("p (h r) c -> p h r c", r=2), e4, pair(4), ALU.mult))
                    tt_(A1[:, blk, :], A1[:, blk, :], spread(beta[:, r, blk], 2, [P, 4, P]), ALU.mult).then_inc(S["A_ready"], 1)
                    tt_(at1[:, blk, :].rearrange("p (h r) c -> p h r c", r=2), e4, pair(6), ALU.mult).then_inc(S["at_ready"], 1)
                for b in range(4):
                    dve.wait_ge(S["A_turned"], 4 * r + b + 1)
                    last = v.tensor_copy(AT1[:, 4 * b:4 * b + 4, :], ps[:, b, :].rearrange("p (u c) -> p u c", u=4))
                    if b < 3:
                        link(last)
                last.then_inc(S["AT_ready"], 1)
                tt_(vb, v_tm[:, r], spread(beta[:, r, :], 2, [P, VH, P]), ALU.mult).then_inc(S["vb_ready"], 1)
                dve.wait_ge(S["A_turned"], 4 * r + 4)
                dve.wait_ge(S["at_turned"], 4 * r + 4)
                solve_dve(dve, v, SOLVE1 + r, lambda n: beside_solve(r, n))
                dve.wait_ge(S["u1_done"], 4 * r + 4)
                v.tensor_copy(u_, ps[:, 0:4, :].rearrange("p b (u c) -> p (b u) c", u=4)).then_inc(S["uw_out"], 1)
                dve.wait_ge(S["uw_out"], 2 * r + 2)
                for hf in range(2):
                    c = 2 * r + hf
                    rows = slice(64 * hf, 64 * hf + 64)

                    def bank(n):
                        return ps[rows, n, :].rearrange("p (u c) -> p u c", u=4)
                    for b in range(4):
                        blk = slice(4 * b, 4 * b + 4)
                        dve.wait_ge(S["wS_done"], 4 * c + b + 1)
                        tt_(vnew[rows, blk, :], u_[rows, blk, :], bank(b), ALU.subtract).then_inc(S["vnew_ready"], 1)
                    for b in range(4):
                        blk = slice(4 * b, 4 * b + 4)
                        dve.wait_ge(S["qS_done"], 4 * c + b + 1)
                        tt_(v_tm[rows, r, blk, :], bank(4 + b), spread(eg[rows, r, blk], 2, [64, 4, P]), ALU.mult).then_inc(S["qS_read"], 1)
                        link(tt_(St[:, blk, :], St[:, blk, :], spread(glb[:, c, blk], 2, [P, 4, P]), ALU.mult))
                        dve.wait_ge(S["incr_done"], B3 + 4 * c + b + 1)
                        tt_(St[:, blk, :], St[:, blk, :], ps[:, b, :].rearrange("p (u c) -> p u c", u=4), ALU.add).then_inc(S["state_ready"], 1)
                    for b in range(4):
                        blk = slice(4 * b, 4 * b + 4)
                        dve.wait_ge(S["qS_read"], 4 * c + b + 1)
                        dve.wait_ge(S["av_done"], 4 * c + b + 1)
                        tt_(v_tm[rows, r, blk, :], v_tm[rows, r, blk, :], bank(4 + b), ALU.add).then_inc(S["o_out"], 1)
                    dve.wait_ge(S["state_ready"], B4 + 4 * c + 8)
                if r:
                    for n in range(4):
                        head_norm(r, n)
            for i in (1, 3, 5, 7):
                tt, q = divmod(i, 4)
                dve.wait_ge(S["outs_turned"], B4 + i + 1)
                v.tensor_copy(yT16[:, 4 * q:4 * q + 4, tt * P:(tt + 1) * P], ps[:, i, :].rearrange("p (k t) -> p k t", k=4)
                              ).then_inc(S["outsT_ready"], 1)
            dve.wait_ge(S["wide_used"], RING + wide_at["M1"] + 16)


        mixer_loads, mixer_params, mixer_pe, mixer_act, mixer_dve = {}, {}, {}, {}, {}
        mixer_loads["M0"], mixer_params["M0"], mixer_pe["M0"], mixer_act["M0"], mixer_dve["M0"] = m0_loads, m0_params, m0_pe, m0_act, m0_dve
        mixer_loads["M1"], mixer_params["M1"], mixer_pe["M1"], mixer_act["M1"], mixer_dve["M1"] = m1_loads, m1_params, m1_pe, m1_act, m1_dve

        for name in OVER:
            S["over_" + name]

        block = ctx.enter_context(nc.Block())

        @block.sync
        def _(sp):
            sp.dma_start(x_tok[:, :, :], a["x"][0].rearrange("(t p) d -> p t d", p=P)).then_inc(S["x_in"], 16)
            sp.dma_start(cst[:, :], a["constants"]).then_inc(S["const_in"], 16)

            def wide_chunk(n, src):
                sp.wait_ge(S["wide_used"], n + 1)
                nk, w = src.shape[1:]
                dst = wide[:, n % RING, 0:nk * w].rearrange("p (k c) -> p k c", k=nk)
                for k0, k1 in ((0, nk // 4), (nk // 4, nk // 2), (nk // 2, nk)):
                    sp.dma_start(dst[:, k0:k1, :], src[:, k0:k1, :]).then_inc(w_load(n)[0], 16)

            def gate_up(slot, used, value, sem, g, u):
                sp.wait_ge(used, value)
                dst = wide[:, slot, :].rearrange("p (h n) -> p h n", h=2)
                sp.dma_start(dst[:, 0, :], g).then_inc(sem, 16)
                sp.dma_start(dst[:, 1, 0:NARROW // 2], u[:, 0:NARROW // 2]).then_inc(sem, 16)
                sp.dma_start(dst[:, 1, NARROW // 2:], u[:, NARROW // 2:]).then_inc(sem, 16)

            def down(slot, used, value, sem, d):
                sp.wait_ge(used, value)
                sp.dma_start(narrow[:, slot, :], d).then_inc(sem, 16)

            def moe_loads(st):
                pfx = f"l{st[1]}_"
                n, m = wide_at[st], narrow_at[st]
                sg = a[pfx + "sh_gate"].rearrange("(p k) f -> p (k f)", k=KT)
                su = a[pfx + "sh_up"].rearrange("(p k) f -> p (k f)", k=KT)
                sd = a[pfx + "sh_down"].rearrange("(p k) f -> p (k f)", k=2)
                gate_up(n % RING, S["wide_used"], n + 1, w_load(n)[0], sg, su)
                down(m % RING, S["narrow_used"], m + 1, n_load(m)[0], sd)
                eg = a[pfx + "exp_gate"].rearrange("e (p k) f -> p e (k f)", k=KT)
                eu = a[pfx + "exp_up"].rearrange("e (p k) f -> p e (k f)", k=KT)
                ed = a[pfx + "exp_down"].rearrange("e (p k) f -> p e (k f)", k=2)
                n, m = n + 1, m + 1
                with sp.Fori(0, ITERS) as it:
                    for j in range(EPI):
                        gate_up((n + j) % RING, S["wide_used"], it * EPI + (n + j + 1), w_load(n + j)[0],
                                eg[:, bass.ds(it * EPI + j, 1), :].rearrange("p e n -> p (e n)"),
                                eu[:, bass.ds(it * EPI + j, 1), :].rearrange("p e n -> p (e n)"))
                    for j in range(EPI):
                        down((m + j) % RING, S["narrow_used"], it * EPI + (m + j + 1), n_load(m + j)[0],
                             ed[:, bass.ds(it * EPI + j, 1), :].rearrange("p e n -> p (e n)"))
                k = moe_no[st]
                sp.wait_ge(S["flag_ready"], k + 1)
                many = sp.value_load(flag[0:1, 0:1])
                with sp.If(many > SLOTS):
                    sp.wait_ge(S["pair_combined"], 2 * ITERS * (k + 1))
                    o = "over_"
                    with sp.Fori(0, ROUNDS - 1) as r:
                        with sp.Fori(0, ITERS) as it:
                            for j in range(EPI):
                                gate_up(j, S[o + "wide_used"], r * (ITERS * EPI) + it * EPI + (j + 1), S[f"{o}wide_loaded{j}"],
                                        eg[:, bass.ds(it * EPI + j, 1), :].rearrange("p e n -> p (e n)"),
                                        eu[:, bass.ds(it * EPI + j, 1), :].rearrange("p e n -> p (e n)"))
                            for j in range(EPI):
                                down(j, S[o + "narrow_used"], r * (ITERS * EPI) + it * EPI + (j + 1), S[f"{o}narrow_loaded{j}"],
                                     ed[:, bass.ds(it * EPI + j, 1), :].rearrange("p e n -> p (e n)"))
                    sp.wait_ge(S[o + "pair_combined"], 2 * O_ITERS)
                    sp.wait_ge(S["ln_done"], stages.index(st) + 1)
                    for name in sorted(S):
                        if name.startswith(o):
                            sp.sem_clear(S[name])

            for st in stages:
                if st[0] == "M":
                    mixer_loads[st](sp, wide_chunk)
                else:
                    moe_loads(st)
            sp.wait_ge(S["ln_done"], len(stages))
            sp.dma_start(out[0].rearrange("(t p) d -> p t d", p=P), x_tok[:, :, :]).then_inc(S["stored"], 16)
            sp.wait_ge(S["stored"], 16)

        @block.gpsimd
        def _(pool):
            for i, st in enumerate(stages):
                pfx = f"l{st[1]}_"
                if st[0] == "M":
                    mixer_params[st](pool)
                else:
                    if i:
                        pool.wait_ge(S["ln_done"], i)
                    pool.dma_start(router_w, a[pfx + "router_w"].rearrange("(p k) e -> p k e", k=KT)).then_inc(S["router_in"], 16)
                    pool.dma_start(rb, a[pfx + "router_b"].partition_broadcast(P)).then_inc(S["router_in"], 16)
                if i:
                    pool.wait_ge(S["ln_done"], i)
                ln = pfx + ("ln1_" if st[0] == "M" else "ln2_")
                pool.dma_start(lng[:, :], a[ln + "g"].partition_broadcast(P)).then_inc(S["ln_in"], 16)
                pool.dma_start(lnb[:, :], a[ln + "b"].partition_broadcast(P)).then_inc(S["ln_in"], 16)

        @block.tensor
        def _(pe):
            mm = nc.tensor.matmul

            def turn_x(i):
                if i == 0:
                    pe.wait_ge(S["const_in"], 16)
                    pe.wait_ge(S["x_in"], 16)
                else:
                    pe.wait_ge(S["ln_done"], i)
                for b in range(4):
                    tt, half = divmod(b, 2)
                    for k in range(4):
                        kt = 4 * half + k
                        last = nc.tensor.transpose(ps[:, 4 + b, k * P:(k + 1) * P], x_tok[:, tt, kt::KT], ident)
                    last.then_inc(S["x_turned"], 1)

            def gather(o):
                for kt in range(KT):
                    c = (kt % 2) * EPI * SLOTS
                    for tt in range(TT):
                        for part in range(2):
                            last = mm(ps[:, 4 + kt // 2, c:c + EPI * SLOTS], h_parts[:, tt, part, kt, :],
                                      oh[:, tt].rearrange("p e s -> p (e s)"),
                                      start=(tt == 0 and part == 0), stop=(tt == 1 and part == 1))
                    if kt % 2:
                        last.then_inc(S[o + "gathered"], 1)

            def expert_loop(o, iters, base, wide0, narrow0, k):
                q = S
                with pe.Fori(0, iters) as it:
                    pe.wait_ge(q[o + "onehot_ready"], it + (base + k + 1))
                    gather(o)
                    for p in range(2):
                        for e in range(2):
                            n = wide0 + 2 * p + e
                            pe.wait_ge(q[f"{o}wide_loaded{n % RING}"], it * 48 + 48 * (n // RING + 1))
                        for kt in range(KT):
                            if p == 0 and kt % 2 == 0:
                                pe.wait_ge(q[o + ("gathered_lo" if kt < 4 else "gathered_hi")], it * 2 + (2 * base + kt % 4 // 2 + 1))
                            for e in range(2):
                                last = mm(ps[64 * e:64 * e + 64, 4 + p, :], hTe[:, p, kt, 64 * e:64 * e + 64],
                                          gu_view((wide0 + 2 * p + e) % RING, kt), start=(kt == 0), stop=(kt == KT - 1))
                                if kt == KT - 1:
                                    last.then_inc(q[o + ("wide_used" if e == 0 else "gate_up_done")], 1)
                                if (p, kt, e) == (1, 0, 0):
                                    last.then_inc(q[o + "wide_used"], 1)
                        if p == 0:
                            pe.wait_ge(q[o + "gated_ready"], it + (base + k + 1))
                            for g in range(2):
                                for tt in range(TT):
                                    t = nc.tensor.transpose(ps[:, 7, g * SEQ + tt * P:g * SEQ + (tt + 1) * P],
                                                            ohg[:, tt, 2 * g:2 * g + 2, :].rearrange("p e s -> p (e s)"), ident)
                            t.then_inc(q[o + "gates_turned"], 1)
                    for p in range(2):
                        def turn_pair(p):
                            pe.wait_ge(q[o + "act_ready"], it * 2 + (2 * base + p + 1))
                            for j in range(2):
                                t = nc.tensor.transpose(ps[:, 4 + p, j * P:(1 + j) * P], act_tok[:, p, j::2], ident)
                                if (p, j) == (0, 0):
                                    t.then_inc(q[o + "wide_used"], 1)
                            t.then_inc(q[o + "pair_turned"], 1)
                        if p == 0:
                            turn_pair(0)
                        pe.wait_ge(q[o + "turned_ready"], it * 2 + (2 * base + p + 1))
                        for e in range(2):
                            n = narrow0 + 2 * p + e
                            pe.wait_ge(q[f"{o}narrow_loaded{n % RING}"], it * 16 + 16 * (n // RING + 1))
                        for h in range(2):
                            for j in range(2):
                                for e in range(2):
                                    slot = (narrow0 + 2 * p + e) % RING
                                    last = mm(ps[64 * e:64 * e + 64, 6 + h, :],
                                              turned[:, p, j * P + 64 * e:j * P + 64 * e + 64],
                                              narrow[:, slot, j * D + h * 512:j * D + h * 512 + 512],
                                              start=(j == 0), stop=(j == 1))
                                    if j == 1 and e == 0 and h == 1:
                                        last.then_inc(q[o + "narrow_used"], 1)
                            last.then_inc(q[o + "down_done"], 1)
                        if p == 0:
                            turn_pair(1)
                        for h in range(2):
                            pe.wait_ge(q[o + "y_lo"], it * 4 + (4 * base + 2 * p + h + 1))
                            pe.wait_ge(q[o + "y_hi"], it * 4 + (4 * base + 2 * p + h + 1))
                            for part in range(2):
                                for tt in range(TT):
                                    last = mm(ps[:, 2 * tt + h, :], ohT[:, p, tt * P:(tt + 1) * P],
                                              y_parts[:, p, part, h * 512:(h + 1) * 512],
                                              start=False, stop=False, skip_group_check=True)
                                    if (h, part, tt) == (0, 0, 0):
                                        last.then_inc(q[o + "narrow_used"], 1)
                        last.then_inc(q[o + "pair_combined"], 1)

            pe.sem_inc(S["wide_used"], RING)
            pe.sem_inc(S["narrow_used"], RING)
            for i, st in enumerate(stages):
                turn_x(i)
                pe.wait_ge(S["xT_ready"], 4 * (i + 1))
                if st[0] == "M":
                    mixer_pe[st](pe)
                    continue
                k = moe_no[st]
                n, m = wide_at[st], narrow_at[st]
                pe.wait_ge(S["router_in"], 32 * (k + 1))
                for tt in range(TT):
                    for kt in range(KT):
                        last = mm(ps[:, 4, tt * NE:(tt + 1) * NE], xT[:, kt, tt * P:(tt + 1) * P], router_w[:, kt, :],
                                  start=(kt == 0), stop=(kt == KT - 1))
                last.then_inc(S["logits_done"], 1)
                pe.wait_ge(*w_load(n))
                for g in range(2):
                    for j in range(2):
                        for kt in range(KT):
                            last = mm(ps[:, 6 + g, j * SEQ:(j + 1) * SEQ], gu_view(n % RING, kt)[:, g, j::2], xT[:, kt, :],
                                      start=(kt == 0), stop=(kt == KT - 1))
                last.then_inc(S["shared_up"], 1)
                pe.wait_ge(S["sel_ready"], k + 1)
                mm(ps[:, 5, 0:NE], cm(C_TRIU), sel[:, 0, :], start=True, stop=True)
                mm(ps[:, 5, NE:2 * NE], cm(C_ONES), sel[:, 0, :], start=True, stop=False)
                mm(ps[:, 5, NE:2 * NE], cm(C_TRIU), sel[:, 1, :], start=False, stop=True)
                mm(ps[:, 5, 2 * NE:3 * NE], cm(C_ONES), sel[:, 0, :], start=True, stop=False)
                mm(ps[:, 5, 2 * NE:3 * NE], cm(C_ONES), sel[:, 1, :], start=False, stop=True).then_inc(S["ranks_done"], 1)
                pe.wait_ge(S["shared_act"], k + 1)
                pe.wait_ge(*n_load(m))
                for tt in range(TT):
                    for h in range(2):
                        for j in range(2):
                            last = mm(ps[:, 2 * tt + h, :], shT[:, j, tt * P:(tt + 1) * P],
                                      narrow[:, m % RING, j * D + h * 512:j * D + h * 512 + 512],
                                      start=(j == 0), stop=False, skip_group_check=True)
                            if (tt, h, j) == (1, 1, 0):
                                last.then_inc(S["wide_used"], 1)
                last.then_inc(S["narrow_used"], 1)
                pe.wait_ge(S["parts_ready"], k + 1)
                expert_loop("", ITERS, k * ITERS, n + 1, m + 1, k)
                pe.wait_ge(S["flag_ready"], k + 1)
                many = pe.value_load(flag[0:1, 0:1])
                with pe.If(many > SLOTS):
                    o = "over_"
                    pe.sem_inc(S[o + "wide_used"], RING)
                    pe.sem_inc(S[o + "narrow_used"], RING)
                    expert_loop(o, O_ITERS, 0, 0, 0, 0)

        @block.scalar
        def _(act):
            def turn_x(i):
                st = stages[i]
                if st[0] == "M":
                    split_high(act, st, 0)
                    split_high(act, st, 1)
                    for b in range(4):
                        act.wait_ge(S["x_turned"], 4 * i + b + 1)
                        tt, half = divmod(b, 2)
                        nc.scalar.copy(xT_hi[:, 4 * half:4 * half + 4, tt * P:(tt + 1) * P],
                                       ps[:, 4 + b, :].rearrange("p (k t) -> p k t", k=4)).then_inc(S["x_high"], 1)
                    return
                for b in (0, 2):
                    act.wait_ge(S["x_turned"], 4 * i + b + 1)
                    tt, half = divmod(b, 2)
                    nc.scalar.copy(xT[:, 4 * half:4 * half + 4, tt * P:(tt + 1) * P],
                                   ps[:, 4 + b, :].rearrange("p (k t) -> p k t", k=4)).then_inc(S["xT_ready"], 1)

            def expert_loop(o, iters, base):
                with act.Fori(0, iters) as it:
                    for b in range(2):
                        act.wait_ge(S[o + "gathered"], it * 4 + (4 * base + b + 1))
                        nc.scalar.copy(hTe[:, :, 2 * b:2 * b + 2, :].rearrange("p q k s -> p k q s"),
                                       ps[:, 4 + b, :].rearrange("p (k q s) -> p k q s", k=2, q=2)).then_inc(S[o + "gathered_lo"], 1)
                    for p in range(2):
                        act.wait_ge(S[o + "gate_up_done"], it * 2 + (2 * base + p + 1))
                        nc.scalar.activation(silu_g[:, p, :], ps[:, 4 + p, 0:DE], ACT.Silu).then_inc(S[o + "silu_ready"], 1)
                    for p in range(2):
                        for h in range(2):
                            act.wait_ge(S[o + "down_done"], it * 4 + (4 * base + 2 * p + h + 1))
                            nc.scalar.copy(y_parts[:, p, 0, h * 512:(h + 1) * 512], ps[:, 6 + h, :]
                                           ).then_inc(S[o + "y_lo"], 1)

            for i, st in enumerate(stages):
                turn_x(i)
                if st[0] == "M":
                    mixer_act[st](act)
                    inv_root(act, rstd[:, :], "ln_" + st)
                    continue
                k = moe_no[st]
                act.wait_ge(S["logits_done"], k + 1)
                nc.scalar.activation(scores, ps[:, 4, 0:TT * NE].rearrange("p (t e) -> p t e", t=TT), ACT.Exp, scale=-1.0
                                     ).then_inc(S["exp_scores"], 1)
                act.wait_ge(S["shared_up"], k + 1)
                nc.scalar.activation(sh_silu, ps[:, 6, :].rearrange("p (j t) -> p j t", j=2), ACT.Silu).then_inc(S["shared_silu"], 1)
                expert_loop("", ITERS, k * ITERS)
                act.wait_ge(S["flag_ready"], k + 1)
                many = act.value_load(flag[0:1, 0:1])
                with act.If(many > SLOTS):
                    expert_loop("over_", O_ITERS, 0)
                inv_root(act, rstd[:, :], "ln_" + st)

        @block.vector
        def _(dve):
            v = nc.vector
            order = [0]

            def link(ins):
                order[0] += 1
                ins.then_inc(S["dve_order"], 1)
                dve.wait_ge(S["dve_order"], order[0])

            def turn_x(i):
                st = stages[i]
                if st[0] == "M":
                    for b in range(4):
                        dve.wait_ge(S["x_high"], X0[st] + b + 1)
                        tt, half = divmod(b, 2)
                        tok = slice(tt * P, (tt + 1) * P)
                        v.tensor_tensor(x_low4(st, half)[:, :, tok], ps[:, 4 + b, :].rearrange("p (k t) -> p k t", k=4),
                                        xT_hi[:, 4 * half:4 * half + 4, tok].bitcast(F32), ALU.subtract).then_inc(S["xT_ready"], 1)
                    return
                for b in (1, 3):
                    dve.wait_ge(S["x_turned"], 4 * i + b + 1)
                    tt, half = divmod(b, 2)
                    v.tensor_copy(xT[:, 4 * half:4 * half + 4, tt * P:(tt + 1) * P],
                                  ps[:, 4 + b, :].rearrange("p (k t) -> p k t", k=4)).then_inc(S["xT_ready"], 1)

            def layer_norm(i):
                for tt in range(TT):
                    link(v.scalar_tensor_tensor(out=x_tok[:, tt, :], in0=x_tok[:, tt, :], scalar=ALPHA,
                                                in1=ps[:, 2 * tt:2 * tt + 2, :].rearrange("p b c -> p (b c)"),
                                                op0=ALU.mult, op1=ALU.add))
                for tt in range(TT):
                    for h in range(2):
                        last = v.bn_stats(out=stats[:, tt, h, :], in_=x_tok[:, tt, h * 512:(h + 1) * 512])
                        link(last)
                for tt in range(TT):
                    link(v.bn_aggr(out=mv[:, tt, :], in_=stats[:, tt, :, :]))
                v.tensor_scalar(rstd[:, :], mv[:, :, 1], LN_EPS, None, ALU.add).then_inc(S["square_ready"], 1)
                dve.wait_ge(S["root_ready"], 2 * ROOT["ln_" + stages[i]])
                for tt in range(TT):
                    link(v.tensor_scalar(x_tok[:, tt, :], x_tok[:, tt, :], mv[:, tt, 0:1], rstd[:, tt:tt + 1],
                                         ALU.subtract, ALU.mult))
                dve.wait_ge(S["ln_in"], 32 * (i + 1))
                link(v.tensor_tensor(x_tok[:, :, :], x_tok[:, :, :], spread(lng[:, :], 1, [P, TT, D]), ALU.mult))
                v.tensor_tensor(x_tok[:, :, :], x_tok[:, :, :], spread(lnb[:, :], 1, [P, TT, D]), ALU.add
                                ).then_inc(S["ln_done"], 1)
                dve.wait_ge(S["ln_done"], i + 1)

            def one_hots(o, col):
                v.tensor_tensor(oh[:, :, :, :], spread(spread(cm(C_IOTA, SLOTS), 1, [P, EPI, SLOTS]), 1, [P, TT, EPI, SLOTS]),
                                spread(pos_r[:, :, bass.ds(col, EPI)], 3, [P, TT, EPI, SLOTS]), ALU.is_equal
                                ).then_inc(S[o + "onehot_ready"], 1)

            def gated(o, col, value):
                dve.wait_ge(S[o + "onehot_ready"], value)
                v.tensor_tensor(ohg, oh[:, :, :, :].bitcast(F32), spread(gate_r[:, :, bass.ds(col, EPI)], 3, [P, TT, EPI, SLOTS]), ALU.mult
                                ).then_inc(S[o + "gated_ready"], 1)

            def expert_loop(o, iters, base, col0, k):
                one_hots(o, col0)
                gated(o, col0, base + k + 1)
                with dve.Fori(0, iters) as it:
                    for b in range(2, 4):
                        dve.wait_ge(S[o + "gathered"], it * 4 + (4 * base + b + 1))
                        v.tensor_copy(hTe[:, :, 2 * b:2 * b + 2, :].rearrange("p q k s -> p k q s"),
                                      ps[:, 4 + b, :].rearrange("p (k q s) -> p k q s", k=2, q=2)).then_inc(S[o + "gathered_hi"], 1)
                    dve.wait_ge(S[o + "gates_turned"], it + (base + 1))
                    gT = ps[:, 7, :].rearrange("p (q t) -> p q t", q=2)
                    v.tensor_reduce(slot_gate, gT, AX, ALU.add).then_inc(S[o + "gates_out"], 1)
                    v.tensor_scalar(ohT[:, :, :], gT, 0.0, None, ALU.is_gt).then_inc(S[o + "gates_out"], 1)
                    dve.wait_ge(S[o + "gates_out"], it * 2 + (2 * base + 2))
                    one_hots(o, it * EPI + (col0 + EPI))
                    gated(o, it * EPI + (col0 + EPI), it + (base + k + 2))

                    def times_up(p):
                        dve.wait_ge(S[o + "silu_ready"], it * 2 + (2 * base + p + 1))
                        v.scalar_tensor_tensor(out=act_tok[:, p, :], in0=silu_g[:, p, :], scalar=slot_gate[:, p:p + 1],
                                               in1=ps[:, 4 + p, DE:2 * DE], op0=ALU.mult, op1=ALU.mult
                                               ).then_inc(S[o + "act_ready"], 1)

                    def turned_out(p):
                        dve.wait_ge(S[o + "pair_turned"], it * 2 + (2 * base + p + 1))
                        v.tensor_copy(turned[:, p, :], ps[:, 4 + p, 0:2 * P]).then_inc(S[o + "turned_ready"], 1)

                    def y_out(p, h):
                        dve.wait_ge(S[o + "y_lo"], it * 4 + (4 * base + 2 * p + h + 1))
                        v.tensor_tensor(y_parts[:, p, 1, h * 512:(h + 1) * 512], ps[:, 6 + h, :],
                                        y_parts[:, p, 0, h * 512:(h + 1) * 512].bitcast(F32), ALU.subtract).then_inc(S[o + "y_hi"], 1)

                    times_up(0)
                    turned_out(0)
                    times_up(1)
                    y_out(0, 0)
                    turned_out(1)
                    y_out(0, 1)
                    y_out(1, 0)
                    y_out(1, 1)

            for i, st in enumerate(stages):
                turn_x(i)
                if st[0] == "M":
                    mixer_dve[st](dve, v, link)
                    layer_norm(i)
                    continue
                k = moe_no[st]
                dve.wait_ge(S["exp_scores"], k + 1)
                link(v.tensor_scalar(scores, scores, 1.0, None, ALU.add))
                link(v.reciprocal(scores, scores))
                dve.wait_ge(S["router_in"], 32 * (k + 1))
                link(v.tensor_tensor(choice, scores, spread(rb, 1, [P, TT, NE]), ALU.add))
                for tt in range(TT):
                    for g in range(NG):
                        last = v.max(out=grp_max[:, tt, g, :], in_=choice[:, tt, g * GE:(g + 1) * GE])
                        link(last)
                link(v.tensor_tensor(grp, grp_max[:, :, :, 0], grp_max[:, :, :, 1], ALU.add))
                left = spread(grp, 2, [P, TT, NG, NG])
                right = spread(grp, 3, [P, TT, NG, NG])
                link(v.tensor_tensor(grp_gt, left, right, ALU.is_gt))
                link(v.tensor_tensor(grp_eq, left, right, ALU.is_equal))
                link(v.tensor_tensor(grp_eq, grp_eq, spread(cm(C_G8, NG * NG).rearrange("p (a b) -> p a b", a=NG), 1, [P, TT, NG, NG]), ALU.mult))
                link(v.tensor_tensor(grp_gt, grp_gt, grp_eq, ALU.add))
                link(v.tensor_reduce(grp_rank, grp_gt, AX, ALU.add))
                link(v.tensor_scalar(grp_off, grp_rank, float(TOPG), -FAR, ALU.is_ge, ALU.mult))
                c4 = choice.rearrange("p t (g e) -> p t g e", g=NG)
                link(v.tensor_tensor(c4, c4, spread(grp_off, 3, [P, TT, NG, GE]), ALU.add))
                for tt in range(TT):
                    link(v.max(out=top8[:, tt, :], in_=choice[:, tt, :]))
                    link(v.match_replace(out=choice_rep[:, tt, :], in_to_replace=top8[:, tt, :], in_values=choice[:, tt, :],
                                         imm_value=-3.0 * FAR))
                v.tensor_tensor(sel, choice, choice_rep, ALU.is_gt).then_inc(S["sel_ready"], 1)
                dve.wait_ge(S["sel_ready"], k + 1)
                link(v.tensor_tensor(gate_one, sel, scores, ALU.mult))
                link(v.tensor_reduce(gate_sum, gate_one, AX, ALU.add))
                link(v.reciprocal(gate_inv, gate_sum))
                link(v.tensor_tensor(gate_one, gate_one, spread(gate_inv, 2, [P, TT, NE]), ALU.mult))
                for r in range(ROUNDS):
                    link(v.tensor_scalar(gate_r[:, :, r * NE:(r + 1) * NE], gate_one, ROUTE_SCALE, None, ALU.mult))
                link(v.memset(gate_r[:, :, ROUNDS * NE:], 0.0))
                dve.wait_ge(S["shared_silu"], k + 1)
                v.tensor_tensor(shT, sh_silu, ps[:, 7, :].rearrange("p (j t) -> p j t", j=2), ALU.mult).then_inc(S["shared_act"], 1)
                dve.wait_ge(S["ranks_done"], k + 1)
                link(v.scalar_tensor_tensor(out=pos_one, in0=ps[:, 5, 0:TT * NE].rearrange("p (t e) -> p t e", t=TT), scalar=1.0,
                                            in1=sel, op0=ALU.add, op1=ALU.mult))
                for r in range(ROUNDS):
                    link(v.tensor_scalar(pos_r[:, :, r * NE:(r + 1) * NE], pos_one, -1.0 - r * SLOTS, None, ALU.add))
                link(v.memset(pos_r[:, :, ROUNDS * NE:], -1.0))
                link(v.tensor_reduce(cnt[:, 0:1], ps[:, 5, 2 * NE:3 * NE], AX, ALU.max))
                v.tensor_copy(flag[:, 0:1], cnt[:, 0:1]).then_inc(S["flag_ready"], 1)
                xk = x_tok[:, :, :].rearrange("p t (q k) -> p t k q", k=KT)
                for tt in range(TT):
                    link(v.tensor_copy(h_parts[:, tt, 0], xk[:, tt]))
                    last = v.tensor_tensor(h_parts[:, tt, 1], xk[:, tt], h_parts[:, tt, 0].bitcast(F32), ALU.subtract)
                last.then_inc(S["parts_ready"], 1)
                expert_loop("", ITERS, k * ITERS, 0, k)
                dve.wait_ge(S["flag_ready"], k + 1)
                many = dve.value_load(flag[0:1, 0:1])
                with dve.If(many > SLOTS):
                    dve.wait_ge(S["gated_ready"], (ITERS + 1) * (k + 1))
                    dve.wait_ge(S["pair_combined"], 2 * ITERS * (k + 1))
                    expert_loop("over_", O_ITERS, 0, NE, 0)
                    dve.wait_ge(S["over_pair_combined"], 2 * O_ITERS)
                dve.wait_ge(S["pair_combined"], 2 * ITERS * (k + 1))
                layer_norm(i)


def host_layout(a):
    a = dict(a)
    if "l0_b_mix" in a:
        names = ("l0_b_mix", "l0_b_w0", "l0_b_a0", "l0_b_k_k", "l0_b_k_a", "l0_b_r_k")
        a["l0_b_cols"] = np.ascontiguousarray(np.concatenate([np.asarray(a.pop(n)).reshape(-1, P) for n in names]).T)
    if "l1_conv_w" in a:
        a["l1_conv_cols"] = np.ascontiguousarray(np.asarray(a.pop("l1_conv_w")).reshape(4, 32, P).transpose(2, 1, 0).reshape(P, 128))
    return a


def kernel(**inputs):
    import concourse.bacc as bacc
    from concourse.bass_utils import run_bass_kernel_spmd

    arrays = host_layout({n: np.asarray(v) for n, v in inputs.items()})
    arrays["constants"], arrays["alibi"] = constants()
    nc = bacc.Bacc("TRN2", target_bir_lowering=False, num_devices=1)
    dram, a = {}, {}
    for name, value in arrays.items():
        value = np.ascontiguousarray(value)
        dram[f"in_{name}"] = value
        a[name] = nc.dram_tensor(f"in_{name}", value.shape, mybir.dt.from_np(value.dtype), kind="ExternalInput").ap()
    out = nc.dram_tensor("out_dram", (1, SEQ, D), F32, kind="ExternalOutput").ap()
    build_program(nc, a, out)
    return run_bass_kernel_spmd(nc, [dram], core_ids=[0]).results[0]["out_dram"]
```

```python
import math
from contextlib import ExitStack, contextmanager

import numpy as np

import concourse.bass as bass
from concourse import mybir

F32 = mybir.dt.float32
F32R = mybir.dt.float32r
I32 = mybir.dt.int32
ALU = mybir.AluOpType
ACT = mybir.ActivationFunctionType
AX = mybir.AxisListType.X

P = 128
SEQ, D = 256, 1024
TT = SEQ // P
KT = D // P
ALPHA = 4.0 ** 0.25
LN_EPS = 1e-5

NE, NG, GE, TOPG = 64, 8, 8, 4
DE = D // 4
SLOTS = 64
ROUNDS = SEQ // SLOTS
ROUTE_SCALE = 2.5
EPI = 4
ITERS = NE // EPI
O_ITERS = (ROUNDS - 1) * ITERS
PCOLS = ROUNDS * NE + EPI
FAR = 1e30

RING = 4
WIDE = 4096
NARROW = 2048
CH = WIDE // KT

C_ID, C_STRICT, C_INCL, C_ONES, C_TRIU = 0, 128, 256, 384, 512
C_LVL = 640
LEVELS = 6
C_HALF = C_LVL + LEVELS * P
C_SEG = C_HALF + P
C_LOW = C_SEG + P
C_IOTA = C_LOW + P
C_G8 = C_IOTA + SLOTS
C_HEAD = C_G8 + NG * NG
C_END = C_HEAD + 32
SLOPES = [2.0 ** (-8.0 * (i + 1) / 4) for i in range(4)]
MIX_ARENA = 20016
XL1_AT = 14336
XL0_AT, XL0B_AT = 7184, 18448
N_M = {"M0": 9, "M1": 16}


def constants():
    p = np.arange(P)[:, None]
    f = np.arange(P)[None, :]
    same = (p // 64) == (f // 64)
    c = np.zeros((P, C_END), np.float32)
    c[:, C_ID:C_ID + P] = p == f
    c[:, C_STRICT:C_STRICT + P] = same & (p < f)
    c[:, C_INCL:C_INCL + P] = same & (p <= f)
    c[:, C_ONES:C_ONES + P] = 1.0
    c[:, C_TRIU:C_TRIU + P] = p < f
    for n in range(LEVELS):
        m = 1 << n
        c[:, C_LVL + n * P:C_LVL + (n + 1) * P] = (p // (2 * m) == f // (2 * m)) & (p % (2 * m) < m) & (f % (2 * m) >= m)
    c[:, C_HALF:C_HALF + P] = same
    c[:, C_SEG:C_SEG + P] = p > f
    c[:, C_LOW:C_LOW + P] = same & (f <= p)
    c[:, C_IOTA:C_IOTA + SLOTS] = np.arange(SLOTS)[None, :]
    c[:, C_G8:C_G8 + NG * NG] = (np.arange(NG)[None, :] < np.arange(NG)[:, None]).reshape(1, -1)
    for t in range(4):
        for h in range(8):
            c[:, C_HEAD + t * 8 + h] = (h // 2 == t) & ((np.arange(P) // 64) == h % 2)
    dist = P + p[:, :, None] - np.arange(2 * P)[None, None, :]
    bias = np.where(dist >= 0, -np.array(SLOPES)[None, :, None] * dist, -1e30)
    return c, bias.astype(np.float32).reshape(P, 4 * 2 * P)


OVER = ["onehot_ready", "gated_ready", "gathered", "gathered_lo", "gathered_hi", "gate_up_done", "silu_ready", "act_ready", "gates_turned", "gates_out",
        "pair_turned", "turned_ready", "down_done", "y_lo", "y_hi", "pair_combined", "wide_used", "narrow_used"
        ] + [f"{ring}_loaded{n}" for ring in ("wide", "narrow") for n in range(RING)]


class Sems(dict):

    def __init__(self, nc, ctx):
        super().__init__()
        self.nc, self.ctx = nc, ctx

    def __missing__(self, name):
        self[name] = self.ctx.enter_context(self.nc.semaphore(name))
        return self[name]


def spread(ap, axis, shape):
    return ap.unsqueeze(axis).broadcast_to(shape)


def build_program(nc, a, out, stages=("M0", "E0", "M1", "E1")):
    with ExitStack() as ctx:
        S = Sems(nc, ctx)

        def sb(name, shape, dt=F32):
            return ctx.enter_context(nc.sbuf_tensor(name, shape, dt))

        under = []

        @contextmanager
        def aliases():
            with ExitStack() as stack:
                under.append(stack)
                yield
                under.pop()

        def rounded(name, *dims, dt=F32R):
            return under[-1].enter_context(nc.sbuf_tensor(name, [P, *dims], dt))

        wide = sb("wide_ring", [P, RING, WIDE])
        with aliases():
            w_parts = rounded("w_parts", 2, 2, KT, 256)
        narrow = sb("narrow_ring", [P, RING, NARROW])
        x_tok = sb("x_tok", [P, TT, D])
        with aliases():
            xT_hi = rounded("xT_high", KT, SEQ)
        xT = sb("xT", [P, KT, SEQ])
        cst = sb("constants_sb", [P, C_END])
        lng = sb("ln_gain", [P, D])
        lnb = sb("ln_bias", [P, D])
        stats = sb("ln_stats", [P, TT, 2, 6])
        mv = sb("ln_mean_var", [P, TT, 2])
        rstd = sb("ln_rstd", [P, TT])
        unused = sb("unused", [P, 1])
        with aliases():
            h_parts = rounded("h_parts", TT, 2, KT, P)
            oh = rounded("one_hots", TT, EPI, SLOTS)
            ohT = rounded("one_hots_turned", 2, SEQ)
            y_parts = rounded("y_parts", 2, 2, D)
        with aliases():
            yT_hi = rounded("outputs_high", 2 * KT, SEQ)
            yT_lo0 = rounded("outputs_low", KT, SEQ)
        with aliases():
            rounded("below_wo_parts", 6144, dt=F32)
            wo_low0 = rounded("wo_low_0", 4, 512)
            rounded("between_wo_parts_0", 2048, dt=F32)
            wo_high0 = rounded("wo_high_0", 4, 512)
            rounded("between_wo_parts_1", 2048, dt=F32)
            wo_low1 = rounded("wo_low_1", 4, 512)
            wo_high1 = rounded("wo_high_1", 4, 512)
            wo_parts = ((wo_high0, wo_low0), (wo_high1, wo_low1))
        with aliases():
            rounded("below_xT_low_1", XL1_AT, dt=F32)
            xT_lo1 = rounded("xT_low_1", KT, SEQ)
        with aliases():
            rounded("below_xT_low_0a", XL0_AT, dt=F32)
            xT_lo0a = rounded("xT_low_0a", KT // 2, SEQ)
            rounded("below_xT_low_0b", XL0B_AT - XL0_AT - KT // 2 * SEQ, dt=F32)
            xT_lo0b = rounded("xT_low_0b", KT // 2, SEQ)
        arena = sb("arena", [P, MIX_ARENA])
        ps = ctx.enter_context(nc.psum_tensor("ps", [P, 8, 512], F32))
        ident = cst[:, C_ID:C_ID + P]

        def cm(col, n=P):
            return cst[:, col:col + n]

        def area(at, *dims, base=arena):
            n = int(np.prod(dims))
            v = base[:, at:at + n]
            names = "abcd"[:len(dims)]
            if len(dims) == 1:
                return v
            return v.rearrange(f"p ({' '.join(names)}) -> p {' '.join(names)}", **dict(zip(names, dims)))

        at = TT * 2 * KT * P + TT * EPI * SLOTS + 2 * SEQ + 4 * D

        def take(*dims):
            nonlocal at
            v = area(at, *dims)
            at += int(np.prod(dims))
            return v

        scores = take(TT, NE)
        choice = take(TT, NE)
        choice_rep = take(TT, NE)
        sel = take(TT, NE)
        gate_one = take(TT, NE)
        grp_max = take(TT, NG, 8)
        grp = take(TT, NG)
        grp_gt = take(TT, NG, NG)
        grp_eq = take(TT, NG, NG)
        grp_rank = take(TT, NG)
        grp_off = take(TT, NG)
        top8 = take(TT, 8)
        gate_sum = take(TT)
        gate_inv = take(TT)
        pos_one = take(TT, NE)
        pos_r = take(TT, PCOLS)
        gate_r = take(TT, PCOLS)
        rb = take(NE)
        router_w = take(KT, NE)
        cnt = take(2)
        flag = take(2).bitcast(I32)
        ohg = take(TT, EPI, SLOTS)
        slot_gate = take(2)
        hTe = take(2, KT, P)
        silu_g = take(2, DE)
        act_tok = take(2, DE)
        turned = take(2, 2 * P)
        sh_silu = take(2, SEQ)
        shT = take(2, SEQ)
        assert at <= MIX_ARENA, at

        wide_at, narrow_at = {}, {}
        nw = nn = 0
        for st in stages:
            wide_at[st], narrow_at[st] = nw, nn
            if st[0] == "M":
                nw += N_M[st]
            else:
                nw += 1 + NE
                nn += 1 + NE
        SOLVE1 = 1 if "M0" in stages else 0
        moe_no = {st: n for n, st in enumerate(s for s in stages if s[0] == "E")}

        roots = {"M0": ["kk", "attention", "group_norm0", "group_norm1"], "M1": ["qk0", "qk1", "qk2", "qk3", "gdn0", "gdn1", "gdn2"]}
        ROOT = {name: n + 1 for n, name in enumerate(x for st in stages for x in roots.get(st, []) + ["ln_" + st])}

        def inv_root(act, t, name, requests=1):
            act.wait_ge(S["square_ready"], ROOT[name])
            nc.scalar.activation(t, t, ACT.Ln).then_inc(S["root_ready"], requests)
            act.wait_ge(S["root_ready"], 2 * ROOT[name] - requests)
            nc.scalar.activation(t, t, ACT.Exp, scale=-0.5).then_inc(S["root_ready"], requests)

        def w_load(n):
            return S[f"wide_loaded{n % RING}"], 48 * (n // RING + 1)

        def n_load(n):
            return S[f"narrow_loaded{n % RING}"], 16 * (n // RING + 1)

        mixers = [st for st in stages if st[0] == "M"]
        W0 = {st: 13 * mixers.index(st) for st in mixers}
        X0 = {st: 4 * mixers.index(st) for st in mixers}
        UNITS = {"M0": 13, "M1": 24}

        def x_low(st, kt):
            if st == "M1":
                return xT_lo1[:, kt]
            return (xT_lo0a if kt < 4 else xT_lo0b)[:, kt % 4]

        def x_low4(st, half):
            if st == "M1":
                return xT_lo1[:, 4 * half:4 * half + 4]
            return (xT_lo0b if half else xT_lo0a)[:, :]

        def parts(buf, part, u, st):
            if st == "M1" and u >= UNITS["M1"]:
                return wo_parts[buf][part][:, :, :]
            return w_parts[:, buf, part]

        def unit_weights(st, u):
            n = wide_at[st] + u // 2
            if st == "M1" and u >= UNITS["M1"]:
                return n, wide[:, n % RING, :].rearrange("p (k c) -> p k c", k=4)[:, :, (u % 2) * 512:(u % 2) * 512 + 512]
            w = 256 if (st, u) == ("M0", 12) else CH
            return n, wide[:, n % RING, 0:KT * w].rearrange("p (k c) -> p k c", k=KT)[:, :, (u % 2) * 256:(u % 2) * 256 + 256]

        def split_high(act, st, u):
            n, w = unit_weights(st, u)
            act.wait_ge(*w_load(n))
            if u >= 2:
                act.wait_ge(S["unit_done"], W0[st] + u - 1)
            nc.scalar.copy(parts(u % 2, 0, u, st), w).then_inc(S["w_high"], 1)

        def split_low(eng, ns, st, u):
            n, w = unit_weights(st, u)
            eng.wait_ge(S["w_high"], W0[st] + u + 1)
            ns.tensor_tensor(parts(u % 2, 1, u, st), w, parts(u % 2, 0, u, st).bitcast(F32), ALU.subtract).then_inc(S[f"w_low{u % 2}"], 1)

        def project(pe, st, u, token_major):
            pe.wait_ge(S["w_high"], W0[st] + u + 1)
            if u >= 4:
                pe.wait_ge(S["unit_out"], W0[st] + u - 3)
            wp = w_parts[:, u % 2]
            for half in range(2):
                tok = slice(half * P, (half + 1) * P)
                for n in range(3 * KT):
                    kt, part = (n // 2, n % 2) if n < 2 * KT else (n - 2 * KT, 0)
                    wt = wp[:, 0 if n < 2 * KT else 1, kt]
                    xt = x_low(st, kt) if part else xT_hi[:, kt]
                    if (half, n) == (0, 2 * KT):
                        before = (W0[st] + 1 - u % 2) // 2
                        pe.wait_ge(S[f"w_low{u % 2}"], before + u // 2 + 1)
                    lhsT, rhs = (xt[:, tok], wt) if token_major else (wt[:, tok], xt)
                    last = nc.tensor.matmul(ps[:, u % 4, half * 256:(half + 1) * 256], lhsT, rhs, start=(n == 0), stop=(n == 3 * KT - 1))
                    if (half, n) == (0, 2 * KT) and (u % 2 or u == UNITS[st] - 1):
                        last.then_inc(S["wide_used"], 1)
            last.then_inc(S["unit_done"], 1)

        def gu_view(slot, kt):
            return wide[:, slot, :].rearrange("p (g k f) -> p k g f", g=2, k=KT)[:, kt, :, :]

        M0_UNITS = 13
        raw = area(0, 14, SEQ + 1)
        mixT = area(3600, 14, SEQ)
        at_ = area(0, 16, 2 * P)
        bt_ = area(4096, 16, 2 * P)
        KR = area(8208, 4, 2, SEQ)
        betaT = area(10256, 4, SEQ)
        gammaT = area(11280, 4, SEQ)
        kk_ = area(11280, 4, SEQ)
        kk_norm = area(8208, 4, SEQ)
        rk = xT[:, 0:4, :]
        tm4 = area(12304, 4, TT, 512)
        V_tm, beta_tm, gamma_tm, kappa_tm = (tm4[:, i] for i in range(4))
        y_tok = area(16400, TT, D)
        g_tm = area(18448, TT, 512)
        qkT = area(8208, 8, SEQ)
        vA = area(10256, TT, 512)
        alibi = area(11280, 4, SEQ)
        sc = area(12304, 2, 4, SEQ)
        attn = area(14352, 4, SEQ)
        attnT = area(15376, 4, 2, P)
        small = 19472
        cols = area(small, 34)
        al = area(small + 34, 4, 64)
        ang = area(small + 290, P)
        chunk_start = area(small + 34, SEQ)
        lam2 = area(small + 426, 2)
        lam = area(small + 428, 1)
        smax = area(small + 429, 2, 4)
        ssum = area(small + 437, 2, 4)
        arms = area(small + 513, TT, 4)
        bonus = area(small + 449, TT, 8)
        gmu = area(small + 465, 16)
        gvar = area(small + 481, 16)
        lamC = area(small + 497, 4, 4)
        lora = lng[:, 0:512]
        g2_sb = lng[:, 512:1024]
        lnxg = lnb[:, 0:512]
        lnxb = lnb[:, 512:1024]
        nflat = narrow[:, :, :].rearrange("p a b -> p (a b)")
        N = [area(1024 * i, 4, SEQ, base=nflat) for i in range(8)]
        X, XT_, T1, QT = (area(2048 * i, 16, P, base=nflat) for i in range(4))
        w12 = wide[:, 1:3, :].rearrange("p a b -> p (a b)")
        G_ = area(0, TT, 512, base=w12)
        BV = area(1024, TT, 512, base=w12)
        U_ = area(2048, TT, 512, base=w12)
        Yr = area(3072, TT, 8, 64, base=w12)
        XKT = area(4096, TT, 4, P, base=w12)
        Sbd = area(5120, 4, P, base=w12)
        Ytmp = area(5632, TT, 8, 64, base=w12)
        bonus_v = area(6656, TT, 512, base=w12)
        EM = math.exp(-0.5)
        STEP = {name: n + 1 for names in (
            ("lam_exp", "tanh_ready", "xg_ready", "g_copied", "bv_ready", "xk_ready", "bonus_ready"),
            ("lam_sums", "kk_squared", "cum_ready", "k_ready", "beta_ready", "factors_ready", "g_ready"),
            ("rk_half", "rk_ready", "kr_ready", "bonus_v", "bonus_v_bias", "bonus_v_gated", "gain_gated"),
            ("kk_norm", "g_done", "bv_done", "xg2_done", "xk_done", "bonus_done")) for n, name in enumerate(names)}

        def wv(n, w):
            return wide[:, n % RING, 0:KT * w].rearrange("p (k c) -> p k c", k=KT)

        def unit0(h):
            return (h % 2) * 4 + h // 2

        def m0_loads(sp, wide_chunk):
            w_in = a["l0_w_in"].rearrange("(p k) c -> p k c", k=KT)
            n = wide_at["M0"]
            for c in range(7):
                wide_chunk(n + c, w_in[:, :, c * CH:min((c + 1) * CH, 3328)])
            w_out = a["l0_w_out"].rearrange("(p k) c -> p k c", k=KT)
            for c in range(2):
                wide_chunk(n + 7 + c, w_out[:, :, c * CH:(c + 1) * CH])
            sp.wait_ge(S["rwkv_out"], 2)

        LOW_BY_VECTOR = (0, 1, 3, 5)

        def m0_params(pool):
            pool.dma_start(cols, a["l0_b_cols"]).then_inc(S["mixer_in"], 16)
            pool.dma_start(alibi, a["alibi"].rearrange("p (h k) -> p h k", h=4)).then_inc(S["mixer_in"], 16)
            pool.dma_start(al, a["l0_a_lambda"].rearrange("a b -> (a b)").partition_broadcast(P).rearrange("p (a b) -> p a b", a=4)
                           ).then_inc(S["mixer_in"], 16)
            pool.dma_start(ang, a["l0_a_norm_g"].partition_broadcast(P)).then_inc(S["mixer_in"], 16)
            pool.dma_start(lora[0:64, :], a["l0_b_w2"]).then_inc(S["mixer_in"], 16)
            pool.dma_start(lora[64:128, :], a["l0_b_a2"]).then_inc(S["mixer_in"], 16)
            pool.dma_start(g2_sb, a["l0_b_g2"]).then_inc(S["mixer_in"], 16)
            pool.dma_start(lnxg, a["l0_b_lnx_g"].partition_broadcast(P)).then_inc(S["mixer_in"], 16)
            pool.dma_start(lnxb, a["l0_b_lnx_b"].partition_broadcast(P)).then_inc(S["mixer_in"], 16)
            for u in range(M0_UNITS):
                if u not in LOW_BY_VECTOR:
                    split_low(pool, nc.gpsimd, "M0", u)
            TTg = nc.gpsimd.tensor_tensor

            def step(ins, name):
                ins.then_inc(S["pool_step"], 1)
                pool.wait_ge(S["pool_step"], STEP[name])

            pool.wait_ge(S["vector_step"], STEP["k_ready"])
            rT = mixT[:, 0:4, :]
            step(TTg(rk, rT, N[4], ALU.mult), "rk_half")
            step(TTg(rk, rk, spread(cols[:, 30:34], 2, [P, 4, SEQ]), ALU.mult), "rk_ready")
            pool.wait_ge(S["vector_step"], STEP["beta_ready"])
            pool.wait_ge(S["decays"], 2)
            step(TTg(KR[:, :, 1, :], N[5], rT, ALU.mult), "kr_ready")
            solve_pool(pool, 0, at_)
            pool.wait_ge(S["scalar_step"], STEP["bonus_ready"])
            step(TTg(bonus_v.rearrange("p t (h c) -> p t h c", h=8), V_tm.rearrange("p t (h c) -> p t h c", h=8),
                     spread(bonus, 3, [P, TT, 8, 64]), ALU.mult), "bonus_v")
            step(TTg(bonus_v, bonus_v, spread(lnxb, 1, [P, TT, 512]), ALU.add), "bonus_v_bias")
            step(TTg(bonus_v, bonus_v, g_tm, ALU.mult), "bonus_v_gated")
            step(TTg(g_tm, g_tm, spread(lnxg, 1, [P, TT, 512]), ALU.mult), "gain_gated")
            pool.wait_ge(S["rwkv_out"], 2)

        M0_IN = 16 * 9

        def solve_pool(pool, s, AT):
            pool.wait_ge(S["AT_ready"], s + 1)
            for lv in range(LEVELS):
                for b in range(4):
                    if lv:
                        pool.wait_ge(S["T1_done"], 24 * s + 4 * (lv - 1) + b + 1)
                    if lv == 1:
                        pool.wait_ge(S["XT_ready"], 24 * s + b + 1)
                    nc.gpsimd.tensor_tensor(QT_of(s)[:, 4 * b:4 * b + 4, :], AT[:, 4 * b:4 * b + 4, 0:P],
                                            spread(cm(C_LVL + lv * P), 1, [P, 4, P]), ALU.mult).then_inc(S["QT_ready"], 1)

        def QT_of(s):
            return QT if s < SOLVE1 else QT1

        def X_of(s):
            return (X, XT_, T1) if s < SOLVE1 else (X1, XT1, T11)

        def solve_pe(pe, s):
            mm = nc.tensor.matmul
            X, XT, T1 = X_of(s)
            Q = QT_of(s)
            for b in range(4):
                pe.wait_ge(S["QT_ready"], 24 * s + b + 1)
                for u in range(4):
                    last = mm(ps[:, b, u * P:(u + 1) * P], Q[:, 4 * b + u, :], ident, start=True, stop=True)
                last.then_inc(S["T1_done"], 1)
            for lv in range(1, LEVELS):
                for b in range(4):
                    pe.wait_ge(S["QT_ready"], 24 * s + 4 * lv + b + 1)
                    pe.wait_ge(S["X_ready"], 20 * s + 4 * (lv - 1) + b + 1)
                    for u in range(4):
                        last = mm(ps[:, b, u * P:(u + 1) * P], Q[:, 4 * b + u, :], X[:, 4 * b + u, :], start=True, stop=True)
                    last.then_inc(S["T1_done"], 1)
                for b in range(4):
                    n = 4 * (lv - 1) + b
                    pe.wait_ge(S["T1_ready"], 20 * s + n + 1)
                    pe.wait_ge(S["XT_ready"], 24 * s + 4 * lv + max(b - 1, 0) if b >= 2 else 24 * s + 4 * (lv - 1) + 4)
                    if lv < LEVELS - 1:
                        for u in range(4):
                            last = mm(ps[:, 4 + 2 * (b % 2), u * P:(u + 1) * P], XT[:, 4 * b + u, :], T1[:, 4 * b + u, :],
                                      start=True, stop=True)
                        last.then_inc(S["XQX_done"], 1)
                    for u in range(4):
                        last = mm(ps[:, 5 + 2 * (b % 2), u * P:(u + 1) * P], T1[:, 4 * b + u, :], XT[:, 4 * b + u, :],
                                  start=True, stop=True)
                    last.then_inc(S["XQXT_done"], 1)

        def solve_act(act, s):
            T1 = X_of(s)[2]
            for lv in range(1, LEVELS):
                for b in range(4):
                    act.wait_ge(S["T1_done"], 24 * s + 4 * lv + b + 1)
                    nc.scalar.copy(T1[:, 4 * b:4 * b + 4, :], ps[:, b, :].rearrange("p (u c) -> p u c", u=4)
                                   ).then_inc(S["T1_ready"], 1)

        def solve_dve(dve, v, s, beside=None):
            X, XT, T1 = X_of(s)
            Q = QT_of(s)
            for b in range(4):
                dve.wait_ge(S["QT_ready"], 24 * s + b + 1)
                v.scalar_tensor_tensor(out=XT[:, 4 * b:4 * b + 4, :], in0=Q[:, 4 * b:4 * b + 4, :], scalar=-1.0,
                                       in1=spread(ident, 1, [P, 4, P]), op0=ALU.mult, op1=ALU.add).then_inc(S["XT_ready"], 1)
                dve.wait_ge(S["T1_done"], 24 * s + b + 1)
                v.scalar_tensor_tensor(out=X[:, 4 * b:4 * b + 4, :], in0=ps[:, b, :].rearrange("p (u c) -> p u c", u=4), scalar=-1.0,
                                       in1=spread(ident, 1, [P, 4, P]), op0=ALU.mult, op1=ALU.add).then_inc(S["X_ready"], 1)
            for lv in range(1, LEVELS):
                for b in range(4):
                    blk = slice(4 * b, 4 * b + 4)
                    if lv < LEVELS - 1:
                        dve.wait_ge(S["XQX_done"], 16 * s + 4 * (lv - 1) + b + 1)
                        dve.wait_ge(S["X_ready"], 20 * s + 4 * (lv - 1) + b + 1)
                        v.tensor_tensor(X[:, blk, :], X[:, blk, :], ps[:, 4 + 2 * (b % 2), :].rearrange("p (u c) -> p u c", u=4),
                                        ALU.subtract).then_inc(S["X_ready"], 1)
                    dve.wait_ge(S["XQXT_done"], 20 * s + 4 * (lv - 1) + b + 1)
                    dve.wait_ge(S["XT_ready"], 24 * s + 4 * (lv - 1) + b + 1)
                    v.tensor_tensor(XT[:, blk, :], XT[:, blk, :], ps[:, 5 + 2 * (b % 2), :].rearrange("p (u c) -> p u c", u=4),
                                    ALU.subtract).then_inc(S["XT_ready"], 1)
                    if beside:
                        beside(4 * (lv - 1) + b)

        def m0_pe(pe):
            mm = nc.tensor.matmul
            base = wide_at["M0"]

            def unit(u):
                project(pe, "M0", u, u in (4, 5))

            def scores(qb):
                kw = (qb + 1) * P
                for h in range(4):
                    for c in range(2):
                        r = slice(64 * c, 64 * c + 64)
                        bank, col = (4 + 2 * c + h // 2, (h % 2) * kw) if qb else (4 + c, h * kw)
                        last = mm(ps[:, bank, col:col + kw], qkT[r, h, qb * P:(qb + 1) * P], qkT[r, 4 + h, 0:kw],
                                  start=True, stop=True)
                        if (h, c) == (3, 0):
                            last.then_inc(S["scores_done"], 1)
                last.then_inc(S["scores_done"], 1)

            def turn_attn(qb):
                pe.wait_ge(S["attn_ready"], 2 - qb)
                for h in range(4):
                    for kb in range(qb + 1):
                        bank, col = (6 + h // 2, (h % 2) * 2 * P + kb * P) if qb else (5, h * P)
                        last = nc.tensor.transpose(ps[:, bank, col:col + P], attn[:, h, kb * P:(kb + 1) * P], ident)
                last.then_inc(S["attn_turned"], 1)

            def attend(qb):
                pe.wait_ge(S["attnT_ready"], 2 - qb)
                bank = 4 if qb else 6
                for h in range(4):
                    for kb in range(qb + 1):
                        last = mm(ps[:, bank, h * P:(h + 1) * P], attnT[:, h, kb, :], vA[:, kb, h * P:(h + 1) * P],
                                  start=(kb == 0), stop=(kb == qb))
                last.then_inc(S["attended"], 1)

            for u in range(6):
                unit(u)
            pe.wait_ge(S["unit_out"], 6)
            scores(1)
            unit(6)
            unit(7)
            pe.wait_ge(S["scores_read"], 1)
            scores(0)
            unit(8)
            unit(9)
            turn_attn(1)
            unit(10)
            attend(1)
            turn_attn(0)
            unit(11)
            unit(12)
            pe.wait_ge(S["vector_step"], STEP["kk_squared"])
            pe.wait_ge(S["unit_out"], 12)
            for t in range(4):
                last = mm(ps[:, 2 + t // 2, (t % 2) * SEQ:(t % 2 + 1) * SEQ], cm(C_HALF), kk_norm[:, t, :], start=True, stop=True)
            last.then_inc(S["tensor_step"], 1)
            attend(0)
            pe.wait_ge(S["mixer_in"], M0_IN)
            pe.wait_ge(S["scalar_step"], STEP["tanh_ready"])
            pe.wait_ge(S["attention_out"], 2)
            for t in range(4):
                for r in range(2):
                    rows = slice(64 * r, 64 * r + 64)
                    last = mm(ps[:, 4 + 2 * r + t // 2, (t % 2) * SEQ:(t % 2 + 1) * SEQ], lora[rows, t * P:(t + 1) * P],
                              mixT[rows, 12, :], start=True, stop=True)
                    if (t, r) == (3, 0):
                        last.then_inc(S["lora_done"], 1)
            last.then_inc(S["lora_done"], 1)
            pe.wait_ge(S["scalar_step"], STEP["xg_ready"])
            for tt in range(TT):
                last = mm(ps[:, tt, :], mixT[:, 13, tt * P:(tt + 1) * P], g2_sb, start=True, stop=True)
            last.then_inc(S["tensor_step"], 1)
            for q, src in enumerate((mixT[:, 8:12, :], betaT, gammaT, KR[:, :, 0, :])):
                if q == 0:
                    pe.wait_ge(S["scalar_step"], STEP["g_copied"])
                elif q == 1:
                    pe.wait_ge(S["vector_step"], STEP["beta_ready"])
                elif q == 2:
                    pe.wait_ge(S["vector_step"], STEP["factors_ready"])
                for tt in range(TT):
                    for t in range(4):
                        last = nc.tensor.transpose(ps[:, 2 * q + tt, t * P:(t + 1) * P], src[:, t, tt * P:(tt + 1) * P], ident)
                    last.then_inc(S["factors_turned"], 1)
            pe.wait_ge(S["pool_step"], STEP["kr_ready"])
            for i, src in enumerate((betaT, gammaT)):
                for tt in range(TT):
                    if i == 0:
                        pe.wait_ge(S["tm_ready"], 4 + 4 * tt)
                    else:
                        pe.wait_ge(S["pairs_out"], tt + 1)
                    for t in range(4):
                        for par in range(2):
                            rows = slice(64 * par, 64 * par + 64)
                            last = mm(ps[:, 4 * tt + 2 * par + t // 2, (t % 2) * 256:(t % 2 + 1) * 256],
                                      src[rows, t, tt * P:(tt + 1) * P], KR[rows, t, :, tt * P:(tt + 1) * P], start=True, stop=True)
                            if (t, par) == (3, 0):
                                last.then_inc(S["pairs_done"], 1)
                    last.then_inc(S["pairs_done"], 1)
            pe.wait_ge(S["pairs_out"], 4)
            for tt in range(TT):
                for h in range(8):
                    last = mm(ps[:, tt, h * 64:(h + 1) * 64], bt_[:, tt * 8 + unit0(h), 0:P], V_tm[:, tt, h * 64:(h + 1) * 64],
                              start=True, stop=True)
            last.then_inc(S["tensor_step"], 1)
            pe.wait_ge(S["scalar_step"], STEP["bv_ready"])
            solve_pe(pe, 0)
            pe.wait_ge(S["XT_ready"], 24)
            for tt in range(TT):
                for h in range(8):
                    last = mm(ps[:, tt, h * 64:(h + 1) * 64], XT_[:, tt * 8 + unit0(h), :], BV[:, tt, h * 64:(h + 1) * 64],
                              start=True, stop=True)
            last.then_inc(S["tensor_step"], 1)
            for tt in range(TT):
                for h in range(8):
                    p0 = 64 * (h % 2)
                    last = mm(ps[p0:p0 + 64, 2 + tt, (h // 2) * P:(h // 2 + 1) * P], kappa_tm[:, tt, h * 64:(h + 1) * 64],
                              XT_[:, tt * 8 + unit0(h), :], start=True, stop=True)
            last.then_inc(S["tensor_step"], 1)
            for tt in range(TT):
                for t in range(4):
                    last = mm(ps[:, 5, tt * 8:(tt + 1) * 8], rk[:, t, tt * P:(tt + 1) * P], cst[:, C_HEAD + 8 * t:C_HEAD + 8 * t + 8],
                              start=(t == 0), stop=(t == 3))
            last.then_inc(S["tensor_step"], 1)
            pe.wait_ge(S["vector_step"], STEP["g_ready"])
            for c in range(4):
                tt, r0 = c // 2, 64 * (c % 2)
                pe.wait_ge(S["state_ready"], c + 1)
                for t in range(4):
                    last = mm(ps[r0:r0 + 64, 4, t * P:(t + 1) * P], XKT[:, tt, t, r0:r0 + 64], Sbd[:, t, :], start=True, stop=True)
                last.then_inc(S["u_done"], 1)
                for t in range(4):
                    last = mm(ps[r0:r0 + 64, 6 + tt, t * P:(t + 1) * P], KR[:, t, 1, c * 64:(c + 1) * 64], Sbd[:, t, :],
                              start=(t == 0), stop=False, skip_group_check=True)
                last.then_inc(S["state_used"], 1)
                for h in range(8):
                    mm(ps[r0:r0 + 64, 6 + tt, h * 64:(h + 1) * 64], bt_[:, tt * 8 + unit0(h), P + r0:P + r0 + 64],
                       V_tm[:, tt, h * 64:(h + 1) * 64], start=False, stop=False, skip_group_check=True)
                pe.wait_ge(S["u_ready"], c + 1)
                if c == 0:
                    pe.wait_ge(S["scalar_step"], STEP["bonus_ready"])
                if c < 3:
                    rows = slice(r0, r0 + 64)
                    for h in range(8):
                        p0 = 64 * (h % 2)
                        o = ps[p0:p0 + 64, 5, (h // 2) * 64:(h // 2 + 1) * 64]
                        hc = slice(h * 64, (h + 1) * 64)
                        mm(o, gamma_tm[rows, tt, hc], V_tm[rows, tt, hc], start=True, stop=False)
                        last = mm(o, beta_tm[rows, tt, hc], U_[rows, tt, hc], start=False, stop=True)
                    last.then_inc(S["incr_done"], 1)
                for h in range(8):
                    last = mm(ps[r0:r0 + 64, 6 + tt, h * 64:(h + 1) * 64], at_[:, tt * 8 + unit0(h), P + r0:P + r0 + 64],
                              U_[:, tt, h * 64:(h + 1) * 64], start=False, stop=(h == 7), skip_group_check=True)
                last.then_inc(S["y_done"], 1)
            def turn_outs(tt):
                pe.wait_ge(S["rwkv_out"], tt + 1)
                for half in range(2):
                    for k in range(4):
                        last = nc.tensor.transpose(ps[:, 4 + 2 * tt + half, k * P:(k + 1) * P], y_tok[:, tt, 4 * half + k::KT], ident)
                    last.then_inc(S["outs_turned"], 1)

            turn_outs(0)
            for h in range(2):
                n = base + 7 + h
                pe.wait_ge(*w_load(n))
                for tt in range(TT):
                    if h == 0:
                        if tt == 1:
                            turn_outs(1)
                        pe.wait_ge(S["outsT_ready"], 2 * tt + 2)
                    for kt in range(KT):
                        last = mm(ps[:, 2 * tt + h, :], xT[:, kt, tt * P:(tt + 1) * P], wv(n, CH)[:, kt, :],
                                  start=(kt == 0), stop=(kt == KT - 1))
                    if (h, tt) == (1, 0):
                        last.then_inc(S["tile_summed"], 1)
                last.then_inc(S["wide_used"], 1)

        def m0_act(act):
            A_ = nc.scalar.activation

            def unit_out(u):
                act.wait_ge(S["unit_done"], u + 1)
                if u + 2 < M0_UNITS:
                    split_high(act, "M0", u + 2)
                src = ps[:, u % 4, :].rearrange("p (t c) -> p t c", t=2)
                if u < 4:
                    nc.scalar.mul(qkT[:, 2 * u:2 * u + 2, :], src, 0.125 if u < 2 else 1.0).then_inc(S["unit_out"], 1)
                elif u < 6:
                    nc.scalar.copy(vA[:, :, (u - 4) * 256:(u - 3) * 256], src).then_inc(S["unit_out"], 1)
                else:
                    nc.scalar.copy(raw[:, 2 * (u - 6):2 * (u - 6) + 2, 1:SEQ + 1], src).then_inc(S["unit_out"], 1)

            def softmax_exp(qb):
                act.wait_ge(S["shifted"], 2 - qb)
                kw = (qb + 1) * P
                A_(sc[:, :, :, 0:kw], sc[:, :, :, 0:kw], ACT.Exp).then_inc(S["probs_ready"], 1)

            for u in range(6):
                unit_out(u)
            act.wait_ge(S["vector_step"], STEP["lam_sums"])
            A_(lam2, lam2, ACT.Exp).then_inc(S["scalar_step"], 1)
            softmax_exp(1)
            unit_out(6)
            unit_out(7)
            softmax_exp(0)
            for u in (8, 9, 10):
                unit_out(u)
            unit_out(11)
            unit_out(12)
            act.wait_ge(S["mixed_units"], 7)
            A_(mixT[0:64, 12, :], mixT[0:64, 12, :], ACT.Tanh).then_inc(S["scalar_step"], 1)
            A_(mixT[:, 13, :], mixT[:, 13, :], ACT.Sigmoid).then_inc(S["scalar_step"], 1)
            inv_root(act, kk_norm, "kk")
            act.wait_ge(S["mixer_in"], M0_IN)
            for r in range(2):
                act.wait_ge(S["lora_done"], r + 1)
                for t in range(4):
                    A_(N[2 * r][:, t, :], ps[:, 4 + 2 * r + t // 2, (t % 2) * SEQ:(t % 2 + 1) * SEQ], ACT.Sigmoid,
                       bias=cols[:, 14 + 4 * r + t:15 + 4 * r + t]).then_inc(S["decay_exp"], 1)
            act.wait_ge(S["tensor_step"], STEP["g_done"])
            nc.scalar.copy(g_tm, ps[:, 0:2, :]).then_inc(S["scalar_step"], 1)
            act.wait_ge(S["vector_step"], STEP["cum_ready"])
            A_(N[0], N[0], ACT.Exp, scale=-EM).then_inc(S["decays"], 1)
            A_(N[5], N[1], ACT.Exp, scale=-EM).then_inc(S["decays"], 1)
            act.wait_ge(S["decays"], 2)
            A_(N[1], N[1], ACT.Exp, scale=EM).then_inc(S["decays"], 1)
            for q in range(4):
                act.wait_ge(S["factors_turned"], 2 * q + 1)
                nc.scalar.copy(tm4[:, q, 0, :], ps[:, 2 * q, :]).then_inc(S["tm_a"], 1)
            act.wait_ge(S["tensor_step"], STEP["bv_done"])
            nc.scalar.copy(BV, ps[:, 0:2, :]).then_inc(S["scalar_step"], 1)
            solve_act(act, 0)
            inv_root(act, arms, "attention")
            act.wait_ge(S["tensor_step"], STEP["xk_done"])
            nc.scalar.copy(XKT, ps[:, 2:4, :].rearrange("p a (t c) -> p a t c", t=4)).then_inc(S["scalar_step"], 1)
            act.wait_ge(S["tensor_step"], STEP["bonus_done"])
            nc.scalar.copy(bonus, ps[:, 5, 0:16].rearrange("p (t h) -> p t h", t=TT)).then_inc(S["scalar_step"], 1)
            for tt in range(TT):
                inv_root(act, gvar[:, 8 * tt:8 * tt + 8], f"group_norm{tt}")
            for b in (0, 2):
                act.wait_ge(S["outs_turned"], b + 1)
                nc.scalar.copy(xT[:, 4 * (b % 2):4 * (b % 2) + 4, (b // 2) * P:(b // 2 + 1) * P],
                               ps[:, 4 + b, :].rearrange("p (k t) -> p k t", k=4)).then_inc(S["outsT_ready"], 1)

        def m0_dve(dve, v, link):
            ts_, tt_, stt = v.tensor_scalar, v.tensor_tensor, v.scalar_tensor_tensor

            def bc(c0, n=4):
                return spread(cols[:, c0:c0 + n], 2, [P, n, SEQ])

            def mix_unit(u):
                i = 2 * (u - 6)
                dve.wait_ge(S["unit_out"], u + 1)
                link(tt_(mixT[:, i:i + 2, :], raw[:, i:i + 2, 0:SEQ], raw[:, i:i + 2, 1:SEQ + 1], ALU.subtract))
                for t in (i, i + 1):
                    last = stt(out=mixT[:, t, :], in0=mixT[:, t, :], scalar=cols[:, t:t + 1], in1=raw[:, t, 1:SEQ + 1],
                               op0=ALU.mult, op1=ALU.add)
                    if t == i:
                        link(last)
                last.then_inc(S["mixed_units"], 1)

            def softmax_a(qb):
                kw = (qb + 1) * P
                k0 = (1 - qb) * P
                dve.wait_ge(S["scores_done"], 4 - 2 * qb)
                if qb == 0:
                    dve.wait_ge(S["attn_ready"], 1)
                for c in range(2):
                    if qb:
                        src = ps[:, 4 + 2 * c:6 + 2 * c, :].rearrange("p b (h k) -> p (b h) k", h=2)
                    else:
                        src = ps[:, 4 + c, :].rearrange("p (h k) -> p h k", h=4)
                    last = tt_(sc[:, c, :, 0:kw], src, alibi[:, :, k0:k0 + kw], ALU.add)
                    if c == 0:
                        link(last)
                last.then_inc(S["scores_read"], 1)
                dve.wait_ge(S["scores_read"], 2 - qb)
                link(v.tensor_reduce(smax, sc[:, :, :, 0:kw], AX, ALU.max))
                for c in range(2):
                    last = tt_(sc[:, c, :, 0:kw], sc[:, c, :, 0:kw], spread(smax[:, c, :], 2, [P, 4, kw]), ALU.subtract)
                    if c == 0:
                        link(last)
                last.then_inc(S["shifted"], 1)

            def softmax_b(qb):
                kw = (qb + 1) * P
                dve.wait_ge(S["probs_ready"], 2 - qb)
                link(v.tensor_reduce(ssum, sc[:, :, :, 0:kw], AX, ALU.add))
                link(v.reciprocal(ssum, ssum))
                link(ts_(ssum[:, 1, :], ssum[:, 1, :], lam[:, 0:1], None, ALU.mult))
                for c in range(2):
                    link(tt_(sc[:, c, :, 0:kw], sc[:, c, :, 0:kw], spread(ssum[:, c, :], 2, [P, 4, kw]), ALU.mult))
                if qb == 0:
                    dve.wait_ge(S["attn_turned"], 1)
                tt_(attn[:, :, 0:kw], sc[:, 0, :, 0:kw], sc[:, 1, :, 0:kw], ALU.subtract).then_inc(S["attn_ready"], 1)

            def attnT_out(qb):
                dve.wait_ge(S["attn_turned"], 2 - qb)
                if qb:
                    v.tensor_copy(attnT, ps[:, 6:8, :].rearrange("p b (h k c) -> p (b h) k c", h=2, k=2)).then_inc(S["attnT_ready"], 1)
                else:
                    dve.wait_ge(S["attended"], 1)
                    v.tensor_copy(attnT[:, :, 0, :], ps[:, 5, :].rearrange("p (h c) -> p h c", h=4)).then_inc(S["attnT_ready"], 1)

            def attended_out(qb):
                dve.wait_ge(S["attended"], 2 - qb)
                v.tensor_copy(y_tok[:, qb, 0:512], ps[:, 4 if qb else 6, :]).then_inc(S["attention_out"], 1)

            def beside_solve(n):
                o = y_tok[:, :, 0:512]
                sq = y_tok[:, :, 512:1024]
                o4 = o.rearrange("p t (h c) -> p t h c", h=4)
                if n == 4:
                    dve.wait_ge(S["attention_out"], 2)
                    link(tt_(sq, o, o, ALU.mult))
                elif n == 8:
                    link(v.tensor_reduce(arms, sq.rearrange("p t (h c) -> p t h c", h=4), AX, ALU.add))
                    ts_(arms, arms, 1.0 / P, 1e-5, ALU.mult, ALU.add).then_inc(S["square_ready"], 1)
                elif n == 19:
                    dve.wait_ge(S["root_ready"], 2 * ROOT["attention"])
                    link(tt_(o4, o4, spread(arms, 3, [P, TT, 4, P]), ALU.mult))
                    link(tt_(o4, o4, spread(spread(ang, 1, [P, 4, P]), 1, [P, TT, 4, P]), ALU.mult))

            for u in LOW_BY_VECTOR:
                split_low(dve, v, "M0", u)
            link(v.memset(raw[:, :, 0:1], 0.0))
            dve.wait_ge(S["mixer_in"], M0_IN)
            link(tt_(al[:, 0::2, :], al[:, 0::2, :], al[:, 1::2, :], ALU.mult))
            v.tensor_reduce(lam2, al[:, 0::2, :], AX, ALU.add).then_inc(S["vector_step"], 1)
            dve.wait_ge(S["scalar_step"], STEP["lam_exp"])
            LAM0 = 0.8 - 0.6 * math.exp(-0.3 * 0)
            link(ts_(lam, lam2[:, 0:1], lam2[:, 1:2], LAM0, ALU.subtract, ALU.add))
            link(ts_(ang, ang, 1.0 - LAM0, None, ALU.mult))
            link(ts_(al, spread(cst[:, C_IOTA:C_IOTA + 64], 1, [P, 4, 64]), 1.0, None, ALU.min))
            softmax_a(1)
            softmax_b(1)
            softmax_a(0)
            mix_unit(6)
            mix_unit(7)
            attnT_out(1)
            softmax_b(0)
            mix_unit(8)
            mix_unit(9)
            attnT_out(0)
            rT, kT = mixT[:, 0:4, :], mixT[:, 4:8, :]
            dve.wait_ge(S["mixed_units"], 4)
            link(tt_(kk_, kT, bc(22), ALU.mult))
            tt_(kk_norm, kk_, kk_, ALU.mult).then_inc(S["vector_step"], 1)
            attended_out(1)
            mix_unit(10)
            mix_unit(11)
            mix_unit(12)
            attended_out(0)
            dve.wait_ge(S["tensor_step"], STEP["kk_norm"])
            ts_(kk_norm, ps[:, 2:4, :].rearrange("p b (t c) -> p (b t) c", t=2), 1e-6, None, ALU.add).then_inc(S["square_ready"], 1)
            dve.wait_ge(S["mixed_units"], 7)
            dve.wait_ge(S["decay_exp"], 4)
            for t in range(4):
                last = v.tensor_tensor_scan(N[1][:, t, :], chunk_start, N[0][:, t, :], 0.0, ALU.mult, ALU.add)
            link(last)
            tt_(N[0], N[1], N[0], ALU.subtract).then_inc(S["vector_step"], 1)
            dve.wait_ge(S["decay_exp"], 8)
            for t in range(4):
                link(ts_(N[4][:, t, :], N[2][:, t, :], 1.0, cols[:, 26 + t:27 + t], ALU.subtract, ALU.mult))
            stt(out=N[4], in0=N[4], scalar=1.0, in1=kT, op0=ALU.add, op1=ALU.mult).then_inc(S["vector_step"], 1)
            dve.wait_ge(S["root_ready"], 2 * ROOT["kk"])
            link(tt_(kk_, kk_, kk_norm, ALU.mult))
            dve.wait_ge(S["decays"], 3)
            link(tt_(KR[:, :, 0, :], N[0], kk_, ALU.mult))
            link(tt_(kk_, kk_, N[2], ALU.mult))
            tt_(betaT, kk_, N[1], ALU.mult).then_inc(S["vector_step"], 1)
            link(v.tensor_copy(lamC, N[5][:, :, 63::64]))
            tt_(gammaT, N[4], N[1], ALU.mult).then_inc(S["vector_step"], 1)
            for q in range(4):
                dve.wait_ge(S["factors_turned"], 2 * q + 2)
                dve.wait_ge(S["tm_a"], q + 1)
                v.tensor_copy(tm4[:, q, 1, :], ps[:, 2 * q + 1, :]).then_inc(S["tm_ready"], 2)
            mask = spread(cst[:, C_STRICT:C_STRICT + 2 * P], 1, [P, 8, 2 * P])
            for i, dst in enumerate((at_, bt_)):
                for tt in range(TT):
                    dve.wait_ge(S["pairs_done"], 2 * (2 * i + tt) + 2)
                    tt_(dst[:, 8 * tt:8 * tt + 8, :], ps[:, 4 * tt:4 * tt + 4, :].rearrange("p b (u c) -> p (b u) c", u=2), mask, ALU.mult
                        ).then_inc(S["pairs_out"], 1)
                if i == 0:
                    dve.wait_ge(S["pairs_out"], 2)
                    v.engine_nop().then_inc(S["AT_ready"], 1)
            solve_dve(dve, v, 0, beside_solve)
            dve.wait_ge(S["tensor_step"], STEP["xg2_done"])
            v.tensor_copy(G_, ps[:, 0:2, :]).then_inc(S["vector_step"], 1)
            link(v.memset(U_, 0.0))
            dve.wait_ge(S["vector_step"], STEP["g_ready"])
            dve.wait_ge(S["scalar_step"], STEP["xk_ready"])
            v.memset(Sbd, 0.0).then_inc(S["state_ready"], 1)

            def group_stats(tt):
                Y, Yt, mu, var = Yr[:, tt], Ytmp[:, tt], gmu[:, 8 * tt:8 * tt + 8], gvar[:, 8 * tt:8 * tt + 8]
                link(v.tensor_reduce(mu, Y, AX, ALU.add))
                link(ts_(mu, mu, 1.0 / 64, None, ALU.mult))
                link(tt_(Y, Y, spread(mu, 2, [P, 8, 64]), ALU.subtract))
                link(tt_(Yt, Y, Y, ALU.mult))
                link(v.tensor_reduce(var, Yt, AX, ALU.add))
                ts_(var, var, 1.0 / 64, 64e-5, ALU.mult, ALU.add).then_inc(S["square_ready"], 1)

            def group_out(tt):
                Y, var = Yr[:, tt], gvar[:, 8 * tt:8 * tt + 8]
                Y2 = Y.rearrange("p h c -> p (h c)")
                dve.wait_ge(S["root_ready"], 2 * ROOT[f"group_norm{tt}"])
                link(tt_(Y, Y, spread(var, 2, [P, 8, 64]), ALU.mult))
                dve.wait_ge(S["pool_step"], STEP["gain_gated"])
                link(tt_(Y2, Y2, g_tm[:, tt, :], ALU.mult))
                tt_(y_tok[:, tt, 512:1024], Y2, bonus_v[:, tt, :], ALU.add).then_inc(S["rwkv_out"], 1)

            for c in range(4):
                tt, r0 = c // 2, 64 * (c % 2)
                rows = slice(r0, r0 + 64)
                dve.wait_ge(S["u_done"], c + 1)
                stt(out=U_[rows, tt, :], in0=ps[rows, 4, :], scalar=-1.0, in1=G_[rows, tt, :], op0=ALU.mult, op1=ALU.subtract
                    ).then_inc(S["u_ready"], 1)
                if c < 3:
                    dve.wait_ge(S["state_used"], c + 1)
                    dve.wait_ge(S["incr_done"], c + 1)
                    for par in range(2):
                        pr = slice(64 * par, 64 * par + 64)
                        s_ = Sbd[pr, :, 64 * par:64 * par + 64]
                        link(tt_(s_, s_, ps[pr, 5, 0:256].rearrange("p (t c) -> p t c", t=4), ALU.add))
                        last = tt_(s_, s_, spread(lamC[pr, :, c], 2, [64, 4, 64]), ALU.mult)
                        if par == 0:
                            link(last)
                    last.then_inc(S["state_ready"], 1)
                    dve.wait_ge(S["state_ready"], c + 2)
                if c % 2:
                    dve.wait_ge(S["y_done"], c + 1)
                    link(v.tensor_copy(Yr[:, tt], ps[:, 6 + tt, :].rearrange("p (h c) -> p h c", h=8)))
                if c == 2:
                    group_stats(0)
            group_out(0)
            group_stats(1)
            group_out(1)
            for b in (1, 3):
                dve.wait_ge(S["outs_turned"], b + 1)
                v.tensor_copy(xT[:, 4 * (b % 2):4 * (b % 2) + 4, (b // 2) * P:(b // 2 + 1) * P],
                              ps[:, 4 + b, :].rearrange("p (k t) -> p k t", k=4)).then_inc(S["outsT_ready"], 1)

        M1_UNITS, VH, KH = 24, 16, 8
        qkF = area(0, 16, SEQ)
        k_tm = area(4096, TT, KH, P)
        v_tm = area(6144, TT, VH, P)
        z_tm = area(10240, TT, VH, P)
        aT_ = area(14336, VH, P)
        St = area(16384, VH, P)
        craw = area(16384, 2, 2, SEQ + 4)
        cacc = area(17424, 2, 2, SEQ)
        ccols = area(18448, 32, 4)
        o_ms = area(18576, TT, VH)
        lngf = lng[:, :]
        w_ba = area(0, KT, 32, base=lngf)
        ong = area(256, P, base=lngf)
        alog = area(384, VH, base=lngf)
        dtb = area(400, VH, base=lngf)
        beta = area(416, TT, VH, base=lngf)
        xa = area(448, TT, VH, base=lngf)
        ab = area(480, TT, VH, base=lngf)
        gg = area(512, TT, VH, base=lngf)
        gcs = area(544, TT, VH, base=lngf)
        eg = area(576, TT, VH, base=lngf)
        kd = area(608, TT, VH, base=lngf)
        bg = area(640, TT, VH, base=lngf)
        glb = area(672, 4, VH, base=lngf)
        wflat = wide[:, :, :].rearrange("p a b -> p (a b)")
        X1, XT1, T11, QT1, AT1, vb, kbg, Ed = (area(2048 * i, VH, P, base=wflat) for i in range(8))
        Dr, A1, at1 = X1, XT1, T11
        u_, wT, kdec, vnew = (area(2048 * i, VH, P, base=nflat) for i in range(4))
        M1_IN = 16 * 5
        xF = area(6144, KT, SEQ)
        SUMS_AT = (7, 9, 11, 13)

        def squares(b):
            return area(4096 + 1024 * (b % 2), 4, SEQ)

        def norms(b):
            return area(11264 + 2048 * (b % 2), 4, SEQ)

        norm_pair = area(10240, 2, 2048)[:, :, 1024:2048]

        GSTEP = {name: n + 1 for n, name in enumerate(("craw_zero", "gates_ready", "kd_ready", "vnew_zero"))}
        POOL0 = 7 if "M0" in stages else 0
        had = 1 if "M0" in stages else 0
        U0, P0, B3, B4 = 13 * had, M0_IN * had, 3 * had, 4 * had

        def m1_loads(sp, wide_chunk):
            w_in = a["l1_w_in"].rearrange("(p k) c -> p k c", k=KT)
            n = wide_at["M1"]
            for c in range(12):
                wide_chunk(n + c, w_in[:, :, c * CH:(c + 1) * CH])
            w_out = a["l1_w_out"].rearrange("(k p) c -> p k c", p=P)
            sp.wait_ge(S["uw_out"], 4)
            for c in range(4):
                wide_chunk(n + 12 + c, w_out[:, 4 * c:4 * c + 4, :])
            sp.wait_ge(S["gdn_out"], 5)

        def m1_params(pool):
            split_low(pool, nc.gpsimd, "M1", 0)
            split_low(pool, nc.gpsimd, "M1", 1)
            if len(stages) > 1 and stages[0] != "M1":
                pool.wait_ge(S["ln_done"], 2 * stages.index("M1"))
            pool.dma_start(w_ba, a["l1_w_in"].rearrange("(p k) c -> p k c", k=KT)[:, :, 6144:6176]).then_inc(S["mixer_in"], 16)
            pool.dma_start(ccols, a["l1_conv_cols"].rearrange("p (t j) -> p t j", j=4)).then_inc(S["mixer_in"], 16)
            pool.dma_start(ong, a["l1_norm_g"].partition_broadcast(P)).then_inc(S["mixer_in"], 16)
            pool.dma_start(alog, a["l1_a_log"].partition_broadcast(P)).then_inc(S["mixer_in"], 16)
            pool.dma_start(dtb, a["l1_dt_bias"].partition_broadcast(P)).then_inc(S["mixer_in"], 16)
            TTg = nc.gpsimd.tensor_tensor
            split_low(pool, nc.gpsimd, "M1", 2)
            pool.wait_ge(S["xT_ready"], 4 * (stages.index("M1") + 1))
            TTg(xF, xT_hi[:, :, :].bitcast(F32), xT_lo1[:, :, :].bitcast(F32), ALU.add).then_inc(S["x_high"], 1)
            for u in range(4, M1_UNITS, 2):
                split_low(pool, nc.gpsimd, "M1", u)
            for r in range(2):
                pool.wait_ge(S["gdn_step"], GSTEP["gates_ready"])
                pool.wait_ge(S["unit_out"], U0 + M1_UNITS)
                if r:
                    pool.wait_ge(S["uw_out"], 2)
                for b in range(4):
                    TTg(Dr[:, 4 * b:4 * b + 4, :], spread(cm(C_SEG), 1, [P, 4, P]),
                        spread(gg[:, r, 4 * b:4 * b + 4], 2, [P, 4, P]), ALU.mult).then_inc(S["seg_ready"], 1)
                kk = spread(k_tm[:, r], 2, [P, KH, 2, P])
                pool.wait_ge(S["k_tm_ready"], 4)
                TTg(kbg.rearrange("p (h r) c -> p h r c", r=2), kk,
                    spread(bg[:, r, :].rearrange("p (h r) -> p h r", r=2), 3, [P, KH, 2, P]), ALU.mult).then_inc(S["kbg_ready"], 1)
                if r:
                    pool.wait_ge(S["incr_done"], B3 + 8)
                TTg(kdec.rearrange("p (h r) c -> p h r c", r=2), kk,
                    spread(kd[:, r, :].rearrange("p (h r) -> p h r", r=2), 3, [P, KH, 2, P]), ALU.mult).then_inc(S["kdec_ready"], 1)
                solve_pool(pool, SOLVE1 + r, AT1)
            pool.wait_ge(S["outs_turned"], B4 + 4)
            split_low(pool, nc.gpsimd, "M1", M1_UNITS)
            pool.wait_ge(S["av_done"], 16)
            split_low(pool, nc.gpsimd, "M1", M1_UNITS + 1)
            for b in range(4):
                blk = slice(4 * b, 4 * b + 4)
                pool.wait_ge(S["o_out"], 12 + b + 1)
                TTg(z_tm[:, 1, blk], v_tm[:, 1, blk], z_tm[:, 1, blk], ALU.mult).then_inc(S["pool_step"], 1)
            for u in (4, 6):
                split_low(pool, nc.gpsimd, "M1", M1_UNITS + u)
            pool.wait_ge(S["gdn_out"], 5)

        def m1_pe(pe):
            mm = nc.tensor.matmul
            tr = nc.tensor.transpose
            base = wide_at["M1"]
            for u in range(M1_UNITS):
                project(pe, "M1", u, u >= 16)
                if u == 3:
                    pe.wait_ge(S["mixer_in"], P0 + M1_IN)
                    pe.wait_ge(S["x_high"], X0["M1"] + 5)
                    for tt in range(TT):
                        for kt in range(KT):
                            last = mm(ps[:, 5, tt * 32:(tt + 1) * 32], xF[:, kt, tt * P:(tt + 1) * P], w_ba[:, kt, :],
                                      start=(kt == 0), stop=(kt == KT - 1))
                    last.then_inc(S["gate_products"], 1)
                if u == 5:
                    pe.wait_ge(S["gdn_step"], GSTEP["gates_ready"])
                    for tt in range(TT):
                        mm(ps[:, 7, tt * VH:(tt + 1) * VH], cm(C_INCL), gg[:, tt, :], start=True, stop=True)
                        mm(ps[:, 7, (2 + tt) * VH:(3 + tt) * VH], cm(C_HALF), gg[:, tt, :], start=True, stop=True)
                        for hf in range(2):
                            for o in range(2):
                                c = 2 * tt + hf
                                last = mm(ps[64 * o:64 * o + 64, 7, (4 + c) * VH:(5 + c) * VH],
                                          cst[:, C_HALF + 64 * hf:C_HALF + 64 * hf + 64], gg[:, tt, :], start=True, stop=True)
                    last.then_inc(S["gate_products"], 1)
                if 10 <= u <= 17:
                    w = u - 2
                    pe.wait_ge(S["conv_act"], w + 1)
                    if w >= 10:
                        pe.wait_ge(S["v_out"], w - 9)
                    for tt in range(TT):
                        for t in range(2):
                            last = tr(ps[:, 4 + w % 2, tt * 256 + t * P:tt * 256 + (t + 1) * P], cacc[:, w % 2, t, tt * P:(tt + 1) * P], ident)
                    last.then_inc(S["v_turned"], 1)
                if u in SUMS_AT:
                    b = SUMS_AT.index(u)
                    pe.wait_ge(S["sq_ready"], b + 1)
                    if b:
                        pe.wait_ge(S["square_ready"], ROOT[f"qk{b - 1}"])
                    else:
                        pe.wait_ge(S["gsums_out"], 3)
                    for t in range(4):
                        last = mm(ps[:, 6 + t // 2, (t % 2) * SEQ:(t % 2 + 1) * SEQ], cm(C_ONES), squares(b)[:, t, :], start=True, stop=True)
                    last.then_inc(S["ss_done"], 1)
                if u in (18, 20):
                    b = (u - 18) // 2
                    pe.wait_ge(S["qk_normed"], 3 + b)
                    if b:
                        pe.wait_ge(S["k_tm_ready"], 2)
                    for tt in range(TT):
                        for t in range(4):
                            last = tr(ps[:, 6 + tt, t * P:(t + 1) * P], qkF[:, 8 + 4 * b + t, tt * P:(tt + 1) * P], ident)
                        last.then_inc(S["k_turned"], 1)
            def turn_outs(tt):
                for b in range(4):
                    pe.wait_ge(S["gdn_out"], 1 + tt * (b + 1))
                    for k in range(4):
                        last = tr(ps[:, 4 * tt + b, k * P:(k + 1) * P], v_tm[:, tt, 4 * b + k, :], ident)
                    last.then_inc(S["outs_turned"], 1)

            for r in range(2):
                tok = slice(r * P, (r + 1) * P)
                for b in range(4):
                    pe.wait_ge(S["seg_ready"], 4 * r + b + 1)
                    if r == 0:
                        pe.wait_ge(S["unit_out"], U0 + M1_UNITS)
                    else:
                        pe.wait_ge(S["state_ready"], B4 + 8 + b + 1)
                    mm(ps[:, b, :], cm(C_INCL), Dr[:, 4 * b:4 * b + 4, :].rearrange("p u c -> p (u c)"), start=True, stop=True
                       ).then_inc(S["dsum_done"], 1)
                if r == 0:
                    pe.wait_ge(S["k_tm_ready"], 4)
                    pe.wait_ge(S["v_out"], 8)
                else:
                    pe.wait_ge(S["o_out"], 8)
                for i, q0 in enumerate((8, 0)):
                    for h in range(KH):
                        last = mm(ps[:, 4 + 2 * i + h // 4, (h % 4) * P:(h % 4 + 1) * P], qkF[:, q0 + h, tok], qkF[:, 8 + h, tok],
                                  start=True, stop=True)
                    last.then_inc(S["kkqk_done"], 1)
                for b in range(4):
                    pe.wait_ge(S["A_ready"], 4 * r + b + 1)
                    for t in range(4):
                        last = tr(ps[:, b, t * P:(t + 1) * P], A1[:, 4 * b + t, :], ident)
                    last.then_inc(S["A_turned"], 1)
                for b in range(4):
                    pe.wait_ge(S["at_ready"], 4 * r + 4)
                    for t in range(4):
                        last = tr(ps[:, 4 + b, t * P:(t + 1) * P], at1[:, 4 * b + t, :], ident)
                    last.then_inc(S["at_turned"], 1)
                pe.wait_ge(S["aT_out"], 4 * r + 4)
                solve_pe(pe, SOLVE1 + r)
                pe.wait_ge(S["XT_ready"], 24 * (SOLVE1 + r) + 24)
                pe.wait_ge(S["vb_ready"], r + 1)
                pe.wait_ge(S["kbg_ready"], r + 1)
                for b in range(4):
                    for t in range(4):
                        last = mm(ps[:, b, t * P:(t + 1) * P], XT1[:, 4 * b + t, :], vb[:, 4 * b + t, :], start=True, stop=True)
                    last.then_inc(S["u1_done"], 1)
                for b in range(4):
                    for t in range(4):
                        last = mm(ps[:, 4 + b, t * P:(t + 1) * P], kbg[:, 4 * b + t, :], XT1[:, 4 * b + t, :], start=True, stop=True)
                    last.then_inc(S["w1_done"], 1)
                pe.wait_ge(S["uw_out"], 2 * r + 2)
                pe.wait_ge(S["kdec_ready"], r + 1)
                for hf in range(2):
                    c = 2 * r + hf
                    r0 = 64 * hf
                    rows = slice(r0, r0 + 64)
                    for b in range(4):
                        pe.wait_ge(S["state_ready"], B4 + 4 * c + b + 1)
                        for t in range(4):
                            last = mm(ps[rows, b, t * P:(t + 1) * P], wT[:, 4 * b + t, rows], St[:, 4 * b + t, :], start=True, stop=True)
                        last.then_inc(S["wS_done"], 1)
                        if hf:
                            pe.wait_ge(S["o_out"], 4 * (c - 1) + b + 1)
                        for t in range(2):
                            last = mm(ps[rows, 4 + b, t * 2 * P:(t + 1) * 2 * P], qkF[:, 2 * b + t, c * 64:(c + 1) * 64],
                                      St[:, 4 * b + 2 * t:4 * b + 2 * t + 2, :].rearrange("p u c -> p (u c)"), start=True, stop=True)
                        last.then_inc(S["qS_done"], 1)
                    for b in range(4):
                        pe.wait_ge(S["vnew_ready"], 4 * c + b + 1)
                        if c == 3:
                            continue
                        for t in range(4):
                            last = mm(ps[:, b, t * P:(t + 1) * P], kdec[rows, 4 * b + t, :], vnew[rows, 4 * b + t, :], start=True, stop=True)
                        last.then_inc(S["incr_done"], 1)
                    if c == 3:
                        turn_outs(0)
                    for b in range(4):
                        pe.wait_ge(S["qS_read"], 4 * c + b + 1)
                        for t in range(4):
                            last = mm(ps[rows, 4 + b, t * P:(t + 1) * P], aT_[:, 4 * b + t, rows], vnew[:, 4 * b + t, :], start=True, stop=True)
                        last.then_inc(S["av_done"], 1)
            def project_out(v, tt):
                j, h = divmod(v, 2)
                u = M1_UNITS + v
                pe.wait_ge(S["w_high"], W0["M1"] + u + 1)
                tok = slice(tt * P, (tt + 1) * P)
                for n in range(12):
                    k, part = (n // 2, n % 2) if n < 8 else (n - 8, 0)
                    head = 4 * j + k
                    y = yT_hi[:, head, tok] if part == 0 else (yT_lo0 if head < 8 else xT_hi)[:, head % 8, tok]
                    if n == 8 and tt == 0:
                        pe.wait_ge(S[f"w_low{u % 2}"], (W0["M1"] + 1 - u % 2) // 2 + u // 2 + 1)
                    last = mm(ps[:, 2 * tt + h, :], y, parts(u % 2, 0 if n < 8 else 1, u, "M1")[:, k], start=(j == 0 and n == 0),
                              stop=(j == 3 and n == 11))
                    if n == 8 and tt == 0 and h == 1:
                        last.then_inc(S["wide_used"], 1)
                if tt:
                    last.then_inc(S["unit_done"], 1)
                elif v == 7:
                    last.then_inc(S["tile_summed"], 1)

            pe.wait_ge(S["outsT_ready"], B4 + 4)
            project_out(0, 0)
            project_out(1, 0)
            turn_outs(1)
            for v in range(8):
                if v % 2 == 0:
                    pe.wait_ge(S["outsT_ready"], B4 + 4 + v // 2 + 1)
                if v >= 2:
                    project_out(v, 0)
                project_out(v, 1)

        def m1_act(act):
            A_ = nc.scalar.activation
            def gates():
                act.wait_ge(S["gate_products"], 1)
                ba = ps[:, 5, 0:64].rearrange("p (t c) -> p t c", t=TT)
                A_(beta, ba[:, :, 0:VH], ACT.Exp, scale=-1.0).then_inc(S["beta_exp"], 1)
                A_(alog, alog, ACT.Exp).then_inc(S["beta_exp"], 1)
                act.wait_ge(S["abs_ready"], 1)
                A_(ab, ab, ACT.Exp, scale=-1.0).then_inc(S["abs_exp"], 1)
                act.wait_ge(S["abs_ready"], 2)
                A_(ab, ab, ACT.Ln).then_inc(S["abs_exp"], 1)

            def silu_unit(u):
                act.wait_ge(S["conv_done"], u + 1)
                dst = qkF[:, 2 * u:2 * u + 2, :] if u < 8 else cacc[:, u % 2]
                A_(dst, cacc[:, u % 2], ACT.Silu).then_inc(S["conv_act"], 1)

            def v_unit(u):
                act.wait_ge(S["v_turned"], u - 7)
                nc.scalar.copy(v_tm[:, :, 2 * (u - 8):2 * (u - 8) + 2, :],
                               ps[:, 4 + u % 2, :].rearrange("p (a b c) -> p a b c", a=TT, b=2)).then_inc(S["v_out"], 1)

            for u in range(M1_UNITS):
                if u == 4:
                    gates()
                act.wait_ge(S["unit_done"], U0 + u + 1)
                if u == 20:
                    act.wait_ge(S["qk_normed"], 4)
                if u < 16:
                    if u >= 2:
                        act.wait_ge(S["conv_done"], u - 1)
                    else:
                        act.wait_ge(S["gdn_step"], GSTEP["craw_zero"])
                    nc.scalar.copy(craw[:, u % 2, :, 3:SEQ + 3], ps[:, u % 4, :].rearrange("p (t c) -> p t c", t=2)
                                   ).then_inc(S["unit_out"], 1)
                else:
                    A_(z_tm[:, :, 2 * (u - 16):2 * (u - 16) + 2, :], ps[:, u % 4, :].rearrange("p (a b c) -> p a b c", a=TT, b=2),
                       ACT.Silu).then_inc(S["unit_out"], 1)
                if u + 2 < M1_UNITS:
                    split_high(act, "M1", u + 2)
                if 1 <= u <= 16:
                    silu_unit(u - 1)
                if 11 <= u <= 18:
                    v_unit(u - 3)
                if u == 6:
                    act.wait_ge(S["gate_products"], 2)
                    A_(eg, ps[:, 7, 0:2 * VH].rearrange("p (t h) -> p t h", t=TT), ACT.Exp).then_inc(S["gsums_out"], 1)
                    A_(glb, ps[:, 7, 4 * VH:8 * VH].rearrange("p (t h) -> p t h", t=4), ACT.Exp).then_inc(S["gsums_out"], 1)
                    act.wait_ge(S["gdn_step"], GSTEP["kd_ready"])
                    A_(kd, kd, ACT.Exp).then_inc(S["kd_exp"], 1)
                if u in (11, 15):
                    inv_root(act, norm_pair, "qk1" if u == 11 else "qk3", 2)
            for r in range(2):
                for b in range(4):
                    act.wait_ge(S["dsum_done"], 4 * r + b + 1)
                    A_(Ed[:, 4 * b:4 * b + 4, :], ps[:, b, :].rearrange("p (u c) -> p u c", u=4), ACT.Exp).then_inc(S["seg_exp"], 1)
                for b in range(4):
                    act.wait_ge(S["at_turned"], 4 * r + b + 1)
                    if r:
                        act.wait_ge(S["av_done"], 8)
                    nc.scalar.copy(aT_[:, 4 * b:4 * b + 4, :], ps[:, 4 + b, :].rearrange("p (u c) -> p u c", u=4)).then_inc(S["aT_out"], 1)
                solve_act(act, SOLVE1 + r)
                if r:
                    inv_root(act, o_ms[:, 0, :], "gdn0")
                act.wait_ge(S["w1_done"], 4 * r + 4)
                nc.scalar.copy(wT, ps[:, 4:8, :].rearrange("p b (u c) -> p (b u) c", u=4)).then_inc(S["uw_out"], 1)
            act.wait_ge(S["vnew_ready"], 16)
            split_high(act, "M1", M1_UNITS)

            def outs_high(i):
                tt, q = divmod(i, 4)
                act.wait_ge(S["outs_turned"], B4 + i + 1)
                nc.scalar.copy(yT_hi[:, 4 * q:4 * q + 4, tt * P:(tt + 1) * P], ps[:, i, :].rearrange("p (k t) -> p k t", k=4)
                               ).then_inc(S["x_high"], 1)

            for i in range(4):
                outs_high(i)
            act.wait_ge(S["av_done"], 16)
            split_high(act, "M1", M1_UNITS + 1)
            inv_root(act, o_ms[:, 1, 0:8], "gdn1")
            inv_root(act, o_ms[:, 1, 8:16], "gdn2")
            for i in range(4, 8):
                outs_high(i)
            for u in range(2, 8):
                split_high(act, "M1", M1_UNITS + u)

        def m1_dve(dve, v, link):
            ts_, tt_, stt = v.tensor_scalar, v.tensor_tensor, v.scalar_tensor_tensor
            v.memset(craw[:, :, :, 0:3], 0.0).then_inc(S["gdn_step"], 1)
            def gates():
                dve.wait_ge(S["gate_products"], 1)
                dve.wait_ge(S["beta_exp"], 2)
                link(tt_(xa, ps[:, 5, 0:64].rearrange("p (t c) -> p t c", t=TT)[:, :, VH:2 * VH], spread(dtb, 1, [P, TT, VH]), ALU.add))
                link(ts_(ab, xa, -1.0, None, ALU.mult))
                tt_(ab, ab, xa, ALU.max).then_inc(S["abs_ready"], 1)
                dve.wait_ge(S["abs_exp"], 1)
                ts_(ab, ab, 1.0, None, ALU.add).then_inc(S["abs_ready"], 1)
                link(ts_(beta, beta, 1.0, None, ALU.add))
                link(v.reciprocal(beta, beta))
                dve.wait_ge(S["abs_exp"], 2)
                link(stt(out=gg, in0=xa, scalar=0.0, in1=ab, op0=ALU.max, op1=ALU.add))
                stt(out=gg, in0=gg, scalar=-1.0, in1=spread(alog, 1, [P, TT, VH]), op0=ALU.mult, op1=ALU.mult).then_inc(S["gdn_step"], 1)

            def conv(u):
                dve.wait_ge(S["unit_out"], U0 + u + 1)
                if 2 <= u < 10:
                    dve.wait_ge(S["conv_act"], u - 1)
                elif u >= 10:
                    dve.wait_ge(S["v_turned"], u - 9)
                for j in range(4):
                    for t in range(2):
                        w = ccols[:, 2 * u + t, j:j + 1]
                        src = craw[:, u % 2, t, j:j + SEQ]
                        dst = cacc[:, u % 2, t, :]
                        if j == 0:
                            last = ts_(dst, src, w, None, ALU.mult)
                        else:
                            last = stt(out=dst, in0=src, scalar=w, in1=dst, op0=ALU.mult, op1=ALU.add)
                        if (j, t) != (3, 1):
                            link(last)
                last.then_inc(S["conv_done"], 1)

            for u in range(22):
                if u == 0:
                    dve.wait_ge(S["mixer_in"], P0 + M1_IN)
                if u == 4:
                    gates()
                if u < 16:
                    conv(u)
                if u % 2:
                    split_low(dve, v, "M1", u + 2)
                if u == 6:
                    dve.wait_ge(S["gate_products"], 2)
                    dve.wait_ge(S["gsums_out"], 2)
                    link(v.tensor_copy(gcs, ps[:, 7, 0:2 * VH].rearrange("p (t h) -> p t h", t=TT)))
                    tt_(kd, ps[:, 7, 2 * VH:4 * VH].rearrange("p (t h) -> p t h", t=TT), gcs, ALU.subtract).then_inc(S["gdn_step"], 1)
                    link(tt_(bg, beta, eg, ALU.mult))
                    dve.wait_ge(S["gdn_step"], GSTEP["kd_ready"])
                    v.engine_nop().then_inc(S["gsums_out"], 1)
                if u + 1 in SUMS_AT:
                    b = SUMS_AT.index(u + 1)
                    dve.wait_ge(S["conv_act"], 2 * b + 2)
                    if b >= 2:
                        dve.wait_ge(S["ss_done"], b - 1)
                    q4 = qkF[:, 4 * b:4 * b + 4, :]
                    tt_(squares(b), q4, q4, ALU.mult).then_inc(S["sq_ready"], 1)
                if u in (12, 16):
                    for b in ((0, 1) if u == 12 else (2, 3)):
                        dve.wait_ge(S["root_ready"], 2 * ROOT["qk1" if u == 12 else "qk3"])
                        q4 = qkF[:, 4 * b:4 * b + 4, :]
                        tt_(q4, q4, norms(b), ALU.mult).then_inc(S["qk_normed"], 1)
                if u - 1 in SUMS_AT:
                    b = SUMS_AT.index(u - 1)
                    dve.wait_ge(S["ss_done"], b + 1)
                    if b >= 2:
                        dve.wait_ge(S["qk_normed"], b - 1)
                    ts_(norms(b), ps[:, 6:8, :].rearrange("p b (t c) -> p (b t) c", t=2), 1e-6, float(P) if b < 2 else 1.0,
                        ALU.add, ALU.mult).then_inc(S["square_ready"], 1)
                if u in (19, 21):
                    b = (u - 19) // 2
                    for tt in range(TT):
                        dve.wait_ge(S["k_turned"], 2 * b + tt + 1)
                        v.tensor_copy(k_tm[:, tt, 4 * b:4 * b + 4, :], ps[:, 6 + tt, :].rearrange("p (t c) -> p t c", t=4)
                                      ).then_inc(S["k_tm_ready"], 1)
            dve.wait_ge(S["qk_normed"], 4)
            dve.wait_ge(S["v_turned"], 8)
            dve.wait_ge(S["unit_out"], U0 + M1_UNITS)
            v.memset(St, 0.0).then_inc(S["state_ready"], 1)
            for _ in range(3):
                dve.wait_ge(S["state_ready"], B4 + 1)
                v.engine_nop().then_inc(S["state_ready"], 1)
            v.memset(vnew, 0.0).then_inc(S["gdn_step"], 1)
            dve.wait_ge(S["gdn_step"], GSTEP["vnew_zero"])
            def head_norm(step):
                o = v_tm[:, 0]
                if step == 0:
                    dve.wait_ge(S["o_out"], 8)
                    link(tt_(Ed, o, o, ALU.mult))
                elif step == 1:
                    link(v.tensor_reduce(o_ms[:, 0, :], Ed, AX, ALU.add))
                    ts_(o_ms[:, 0, :], o_ms[:, 0, :], 1.0 / P, 1e-6, ALU.mult, ALU.add).then_inc(S["square_ready"], 1)
                elif step == 2:
                    link(tt_(o, o, z_tm[:, 0], ALU.mult))
                else:
                    dve.wait_ge(S["root_ready"], 2 * ROOT["gdn0"])
                    tt_(o, o, spread(o_ms[:, 0, :], 2, [P, VH, P]), ALU.mult).then_inc(S["gdn_out"], 1)

            def beside_solve(r, n):
                if r == 0:
                    if n in (8, 12):
                        z = z_tm[:, n // 4 - 2]
                        link(tt_(z, z, spread(ong, 1, [P, VH, P]), ALU.mult))
                elif n in (4, 8, 12, 19):
                    head_norm(3 if n == 19 else n // 4 - 1)

            def outs_low(i):
                tt, q = divmod(i, 4)
                tok = slice(tt * P, (tt + 1) * P)
                dst = yT_lo0 if q < 2 else xT_hi
                dve.wait_ge(S["x_high"], X0["M1"] + 5 + i + 1)
                tt_(dst[:, 4 * (q % 2):4 * (q % 2) + 4, tok], ps[:, i, :].rearrange("p (k t) -> p k t", k=4),
                    yT_hi[:, 4 * q:4 * q + 4, tok].bitcast(F32), ALU.subtract).then_inc(S["outsT_ready"], 1)

            for r in range(2):
                for b in range(4):
                    blk = slice(4 * b, 4 * b + 4)
                    dve.wait_ge(S["seg_exp"], 4 * r + b + 1)
                    link(tt_(Ed[:, blk, :], Ed[:, blk, :], spread(cm(C_LOW), 1, [P, 4, P]), ALU.mult))
                dve.wait_ge(S["kkqk_done"], 2 * r + 2)
                for b in range(4):
                    blk = slice(4 * b, 4 * b + 4)
                    e4 = Ed[:, blk, :].rearrange("p (h r) c -> p h r c", r=2)

                    def pair(bank):
                        return spread(ps[:, bank + b // 2, (b % 2) * 2 * P:(b % 2 + 1) * 2 * P].rearrange("p (h c) -> p h c", h=2), 2, [P, 2, 2, P])
                    link(tt_(A1[:, blk, :].rearrange("p (h r) c -> p h r c", r=2), e4, pair(4), ALU.mult))
                    tt_(A1[:, blk, :], A1[:, blk, :], spread(beta[:, r, blk], 2, [P, 4, P]), ALU.mult).then_inc(S["A_ready"], 1)
                    tt_(at1[:, blk, :].rearrange("p (h r) c -> p h r c", r=2), e4, pair(6), ALU.mult).then_inc(S["at_ready"], 1)
                for b in range(4):
                    dve.wait_ge(S["A_turned"], 4 * r + b + 1)
                    last = v.tensor_copy(AT1[:, 4 * b:4 * b + 4, :], ps[:, b, :].rearrange("p (u c) -> p u c", u=4))
                    if b < 3:
                        link(last)
                last.then_inc(S["AT_ready"], 1)
                tt_(vb, v_tm[:, r], spread(beta[:, r, :], 2, [P, VH, P]), ALU.mult).then_inc(S["vb_ready"], 1)
                dve.wait_ge(S["A_turned"], 4 * r + 4)
                dve.wait_ge(S["at_turned"], 4 * r + 4)
                solve_dve(dve, v, SOLVE1 + r, lambda n: beside_solve(r, n))
                dve.wait_ge(S["u1_done"], 4 * r + 4)
                v.tensor_copy(u_, ps[:, 0:4, :].rearrange("p b (u c) -> p (b u) c", u=4)).then_inc(S["uw_out"], 1)
                dve.wait_ge(S["uw_out"], 2 * r + 2)
                for hf in range(2):
                    c = 2 * r + hf
                    rows = slice(64 * hf, 64 * hf + 64)

                    def bank(n):
                        return ps[rows, n, :].rearrange("p (u c) -> p u c", u=4)
                    for b in range(4):
                        blk = slice(4 * b, 4 * b + 4)
                        dve.wait_ge(S["wS_done"], 4 * c + b + 1)
                        tt_(vnew[rows, blk, :], u_[rows, blk, :], bank(b), ALU.subtract).then_inc(S["vnew_ready"], 1)
                    for b in range(4):
                        blk = slice(4 * b, 4 * b + 4)
                        dve.wait_ge(S["qS_done"], 4 * c + b + 1)
                        tt_(v_tm[rows, r, blk, :], bank(4 + b), spread(eg[rows, r, blk], 2, [64, 4, P]), ALU.mult).then_inc(S["qS_read"], 1)
                        if c == 3:
                            continue
                        link(tt_(St[:, blk, :], St[:, blk, :], spread(glb[:, c, blk], 2, [P, 4, P]), ALU.mult))
                        dve.wait_ge(S["incr_done"], B3 + 4 * c + b + 1)
                        tt_(St[:, blk, :], St[:, blk, :], ps[:, b, :].rearrange("p (u c) -> p u c", u=4), ALU.add).then_inc(S["state_ready"], 1)
                    if c == 3:
                        for i in range(4):
                            outs_low(i)
                    for b in range(4):
                        blk = slice(4 * b, 4 * b + 4)
                        dve.wait_ge(S["qS_read"], 4 * c + b + 1)
                        dve.wait_ge(S["av_done"], 4 * c + b + 1)
                        tt_(v_tm[rows, r, blk, :], v_tm[rows, r, blk, :], bank(4 + b), ALU.add).then_inc(S["o_out"], 1)
                        if c == 3:
                            dve.wait_ge(S["o_out"], 12 + b + 1)
                            squared = u_[:, 0:4, :]
                            link(tt_(squared, v_tm[:, 1, blk], v_tm[:, 1, blk], ALU.mult))
                            link(v.tensor_reduce(o_ms[:, 1, blk], squared, AX, ALU.add))
                            if b % 2:
                                half = o_ms[:, 1, 4 * b - 4:4 * b + 4]
                                ts_(half, half, 1.0 / P, 1e-6, ALU.mult, ALU.add).then_inc(S["square_ready"], 1)
                    if c < 3:
                        dve.wait_ge(S["state_ready"], B4 + 4 * c + 8)

            for b in range(4):
                blk = slice(4 * b, 4 * b + 4)
                dve.wait_ge(S["root_ready"], 2 * ROOT["gdn2" if b >= 2 else "gdn1"])
                dve.wait_ge(S["pool_step"], POOL0 + b + 1)
                tt_(v_tm[:, 1, blk], z_tm[:, 1, blk], spread(o_ms[:, 1, blk], 2, [P, 4, P]), ALU.mult).then_inc(S["gdn_out"], 1)
            for i in range(4, 8):
                outs_low(i)
            for u in (2, 3, 5, 7):
                split_low(dve, v, "M1", M1_UNITS + u)

        mixer_loads, mixer_params, mixer_pe, mixer_act, mixer_dve = {}, {}, {}, {}, {}
        mixer_loads["M0"], mixer_params["M0"], mixer_pe["M0"], mixer_act["M0"], mixer_dve["M0"] = m0_loads, m0_params, m0_pe, m0_act, m0_dve
        mixer_loads["M1"], mixer_params["M1"], mixer_pe["M1"], mixer_act["M1"], mixer_dve["M1"] = m1_loads, m1_params, m1_pe, m1_act, m1_dve

        for name in OVER:
            S["over_" + name]

        block = ctx.enter_context(nc.Block())

        @block.sync
        def _(sp):
            sp.dma_start(ident, a["constants"][:, C_ID:C_ID + P]).then_inc(S["x_in"], 16)
            sp.dma_start(x_tok[:, :, :], a["x"][0].rearrange("(t p) d -> p t d", p=P)).then_inc(S["x_in"], 16)

            def tables():
                sp.dma_start(cst[:, C_ID + P:], a["constants"][:, C_ID + P:]).then_inc(S["tables_in"], 16)

            if stages[0][0] != "M":
                tables()

            def wide_chunk(n, src):
                sp.wait_ge(S["wide_used"], n + 1)
                nk, w = src.shape[1:]
                dst = wide[:, n % RING, 0:nk * w].rearrange("p (k c) -> p k c", k=nk)
                for k0, k1 in ((0, nk // 4), (nk // 4, nk // 2), (nk // 2, nk)):
                    sp.dma_start(dst[:, k0:k1, :], src[:, k0:k1, :]).then_inc(w_load(n)[0], 16)
                if n == 0:
                    tables()

            def gate_up(slot, used, value, sem, g, u):
                sp.wait_ge(used, value)
                dst = wide[:, slot, :].rearrange("p (h n) -> p h n", h=2)
                sp.dma_start(dst[:, 0, :], g).then_inc(sem, 16)
                sp.dma_start(dst[:, 1, 0:NARROW // 2], u[:, 0:NARROW // 2]).then_inc(sem, 16)
                sp.dma_start(dst[:, 1, NARROW // 2:], u[:, NARROW // 2:]).then_inc(sem, 16)

            def down(slot, used, value, sem, d):
                sp.wait_ge(used, value)
                sp.dma_start(narrow[:, slot, :], d).then_inc(sem, 16)

            def moe_loads(st):
                pfx = f"l{st[1]}_"
                n, m = wide_at[st], narrow_at[st]
                sg = a[pfx + "sh_gate"].rearrange("(p k) f -> p (k f)", k=KT)
                su = a[pfx + "sh_up"].rearrange("(p k) f -> p (k f)", k=KT)
                sd = a[pfx + "sh_down"].rearrange("(p k) f -> p (k f)", k=2)
                gate_up(n % RING, S["wide_used"], n + 1, w_load(n)[0], sg, su)
                down(m % RING, S["narrow_used"], m + 1, n_load(m)[0], sd)
                eg = a[pfx + "exp_gate"].rearrange("e (p k) f -> p e (k f)", k=KT)
                eu = a[pfx + "exp_up"].rearrange("e (p k) f -> p e (k f)", k=KT)
                ed = a[pfx + "exp_down"].rearrange("e (p k) f -> p e (k f)", k=2)
                n, m = n + 1, m + 1

                def expert(e, j, wide_part, narrow_part):
                    if wide_part:
                        gate_up((n + j) % RING, S["wide_used"], e + (n + j + 1), w_load(n + j)[0],
                                eg[:, bass.ds(e + j, 1), :].rearrange("p e n -> p (e n)"),
                                eu[:, bass.ds(e + j, 1), :].rearrange("p e n -> p (e n)"))
                    if narrow_part:
                        down((m + j) % RING, S["narrow_used"], e + (m + j + 1), n_load(m + j)[0],
                             ed[:, bass.ds(e + j, 1), :].rearrange("p e n -> p (e n)"))

                for j in range(RING - 1):
                    expert(0, j, 1, 0)
                for j in range(RING - 1):
                    expert(0, j, 0, 1)
                expert(0, RING - 1, 1, 1)
                with sp.Fori(1, ITERS) as it:
                    for j in range(EPI):
                        expert(it * EPI, j, 1, 0)
                    for j in range(EPI):
                        expert(it * EPI, j, 0, 1)
                k = moe_no[st]
                sp.wait_ge(S["flag_ready"], k + 1)
                many = sp.value_load(flag[0:1, 0:1])
                with sp.If(many > SLOTS):
                    sp.wait_ge(S["pair_combined"], 2 * ITERS * (k + 1))
                    o = "over_"
                    with sp.Fori(0, ROUNDS - 1) as r:
                        with sp.Fori(0, ITERS) as it:
                            for j in range(EPI):
                                gate_up(j, S[o + "wide_used"], r * (ITERS * EPI) + it * EPI + (j + 1), S[f"{o}wide_loaded{j}"],
                                        eg[:, bass.ds(it * EPI + j, 1), :].rearrange("p e n -> p (e n)"),
                                        eu[:, bass.ds(it * EPI + j, 1), :].rearrange("p e n -> p (e n)"))
                            for j in range(EPI):
                                down(j, S[o + "narrow_used"], r * (ITERS * EPI) + it * EPI + (j + 1), S[f"{o}narrow_loaded{j}"],
                                     ed[:, bass.ds(it * EPI + j, 1), :].rearrange("p e n -> p (e n)"))
                    sp.wait_ge(S[o + "pair_combined"], 2 * O_ITERS)
                    sp.wait_ge(S["ln_done"], 2 * stages.index(st) + 2)
                    for name in sorted(S):
                        if name.startswith(o):
                            sp.sem_clear(S[name])

            for st in stages:
                if st[0] == "M":
                    mixer_loads[st](sp, wide_chunk)
                else:
                    moe_loads(st)
            for tt in range(TT):
                sp.wait_ge(S["ln_done"], 2 * len(stages) - 1 + tt)
                sp.dma_start(out[0, tt * P:(tt + 1) * P, :], x_tok[:, tt, :]).then_inc(S["stored"], 16)
            sp.wait_ge(S["stored"], 32)

        @block.gpsimd
        def _(pool):
            for i, st in enumerate(stages):
                pfx = f"l{st[1]}_"
                if st[0] == "M":
                    mixer_params[st](pool)
                else:
                    if i:
                        pool.wait_ge(S["ln_done"], 2 * i)
                    pool.dma_start(router_w, a[pfx + "router_w"].rearrange("(p k) e -> p k e", k=KT)).then_inc(S["router_in"], 16)
                    pool.dma_start(rb, a[pfx + "router_b"].partition_broadcast(P)).then_inc(S["router_in"], 16)
                if i:
                    pool.wait_ge(S["ln_done"], 2 * i)
                ln = pfx + ("ln1_" if st[0] == "M" else "ln2_")
                pool.dma_start(lng[:, :], a[ln + "g"].partition_broadcast(P)).then_inc(S["ln_in"], 16)
                pool.dma_start(lnb[:, :], a[ln + "b"].partition_broadcast(P)).then_inc(S["ln_in"], 16)

        @block.tensor
        def _(pe):
            mm = nc.tensor.matmul

            def turn_x(i):
                if i == 0:
                    pe.wait_ge(S["x_in"], 32)
                for b in range(4):
                    tt, half = divmod(b, 2)
                    if i:
                        pe.wait_ge(S["ln_done"], 2 * i - 1 + tt)
                    for k in range(4):
                        kt = 4 * half + k
                        last = nc.tensor.transpose(ps[:, 4 + b, k * P:(k + 1) * P], x_tok[:, tt, kt::KT], ident)
                    last.then_inc(S["x_turned"], 1)

            def gather(o):
                for kt in range(KT):
                    c = (kt % 2) * EPI * SLOTS
                    for tt in range(TT):
                        for part in range(2):
                            last = mm(ps[:, 4 + kt // 2, c:c + EPI * SLOTS], h_parts[:, tt, part, kt, :],
                                      oh[:, tt].rearrange("p e s -> p (e s)"),
                                      start=(tt == 0 and part == 0), stop=(tt == 1 and part == 1))
                    if kt % 2:
                        last.then_inc(S[o + "gathered"], 1)

            def expert_loop(o, iters, base, wide0, narrow0, k):
                q = S
                with pe.Fori(0, iters) as it:
                    pe.wait_ge(q[o + "onehot_ready"], it + (base + k + 1))
                    gather(o)
                    for p in range(2):
                        for e in range(2):
                            n = wide0 + 2 * p + e
                            pe.wait_ge(q[f"{o}wide_loaded{n % RING}"], it * 48 + 48 * (n // RING + 1))
                        for kt in range(KT):
                            if p == 0 and kt % 2 == 0:
                                pe.wait_ge(q[o + ("gathered_lo" if kt < 4 else "gathered_hi")], it * 2 + (2 * base + kt % 4 // 2 + 1))
                            for e in range(2):
                                last = mm(ps[64 * e:64 * e + 64, 4 + p, :], hTe[:, p, kt, 64 * e:64 * e + 64],
                                          gu_view((wide0 + 2 * p + e) % RING, kt), start=(kt == 0), stop=(kt == KT - 1))
                                if kt == KT - 1:
                                    last.then_inc(q[o + ("wide_used" if e == 0 else "gate_up_done")], 1)
                                if (p, kt, e) == (1, 0, 0):
                                    last.then_inc(q[o + "wide_used"], 1)
                        if p == 0:
                            pe.wait_ge(q[o + "gated_ready"], it + (base + k + 1))
                            for g in range(2):
                                for tt in range(TT):
                                    t = nc.tensor.transpose(ps[:, 7, g * SEQ + tt * P:g * SEQ + (tt + 1) * P],
                                                            ohg[:, tt, 2 * g:2 * g + 2, :].rearrange("p e s -> p (e s)"), ident)
                            t.then_inc(q[o + "gates_turned"], 1)
                    for p in range(2):
                        def turn_pair(p):
                            pe.wait_ge(q[o + "act_ready"], it * 2 + (2 * base + p + 1))
                            for j in range(2):
                                t = nc.tensor.transpose(ps[:, 4 + p, j * P:(1 + j) * P], act_tok[:, p, j::2], ident)
                                if (p, j) == (0, 0):
                                    t.then_inc(q[o + "wide_used"], 1)
                            t.then_inc(q[o + "pair_turned"], 1)
                        if p == 0:
                            turn_pair(0)
                        pe.wait_ge(q[o + "turned_ready"], it * 2 + (2 * base + p + 1))
                        for e in range(2):
                            n = narrow0 + 2 * p + e
                            pe.wait_ge(q[f"{o}narrow_loaded{n % RING}"], it * 16 + 16 * (n // RING + 1))
                        for h in range(2):
                            for j in range(2):
                                for e in range(2):
                                    slot = (narrow0 + 2 * p + e) % RING
                                    last = mm(ps[64 * e:64 * e + 64, 6 + h, :],
                                              turned[:, p, j * P + 64 * e:j * P + 64 * e + 64],
                                              narrow[:, slot, j * D + h * 512:j * D + h * 512 + 512],
                                              start=(j == 0), stop=(j == 1))
                                    if j == 1 and e == 0 and h == 1:
                                        last.then_inc(q[o + "narrow_used"], 1)
                            last.then_inc(q[o + "down_done"], 1)
                        if p == 0:
                            turn_pair(1)
                        for h in range(2):
                            pe.wait_ge(q[o + "y_lo"], it * 4 + (4 * base + 2 * p + h + 1))
                            pe.wait_ge(q[o + "y_hi"], it * 4 + (4 * base + 2 * p + h + 1))
                            for part in range(2):
                                for tt in range(TT):
                                    last = mm(ps[:, 2 * tt + h, :], ohT[:, p, tt * P:(tt + 1) * P],
                                              y_parts[:, p, part, h * 512:(h + 1) * 512],
                                              start=False, stop=False, skip_group_check=True)
                                    if (h, part, tt) == (0, 0, 0):
                                        last.then_inc(q[o + "narrow_used"], 1)
                        last.then_inc(q[o + "pair_combined"], 1)

            pe.sem_inc(S["wide_used"], RING)
            pe.sem_inc(S["narrow_used"], RING)
            for i, st in enumerate(stages):
                turn_x(i)
                pe.wait_ge(S["xT_ready"], 4 * (i + 1))
                if st[0] == "M":
                    mixer_pe[st](pe)
                    continue
                k = moe_no[st]
                n, m = wide_at[st], narrow_at[st]
                pe.wait_ge(S["router_in"], 32 * (k + 1))
                for tt in range(TT):
                    for kt in range(KT):
                        last = mm(ps[:, 4, tt * NE:(tt + 1) * NE], xT[:, kt, tt * P:(tt + 1) * P], router_w[:, kt, :],
                                  start=(kt == 0), stop=(kt == KT - 1))
                last.then_inc(S["logits_done"], 1)
                pe.wait_ge(*w_load(n))
                for g in range(2):
                    for j in range(2):
                        for kt in range(KT):
                            last = mm(ps[:, 6 + g, j * SEQ:(j + 1) * SEQ], gu_view(n % RING, kt)[:, g, j::2], xT[:, kt, :],
                                      start=(kt == 0), stop=(kt == KT - 1))
                last.then_inc(S["shared_up"], 1)
                pe.wait_ge(S["sel_ready"], k + 1)
                mm(ps[:, 5, 0:NE], cm(C_TRIU), sel[:, 0, :], start=True, stop=True).then_inc(S["wide_used"], 1)
                mm(ps[:, 5, NE:2 * NE], cm(C_ONES), sel[:, 0, :], start=True, stop=False)
                mm(ps[:, 5, NE:2 * NE], cm(C_TRIU), sel[:, 1, :], start=False, stop=True)
                mm(ps[:, 5, 2 * NE:3 * NE], cm(C_ONES), sel[:, 0, :], start=True, stop=False)
                mm(ps[:, 5, 2 * NE:3 * NE], cm(C_ONES), sel[:, 1, :], start=False, stop=True).then_inc(S["ranks_done"], 1)
                pe.wait_ge(S["shared_act"], k + 1)
                pe.wait_ge(*n_load(m))
                for tt in range(TT):
                    for h in range(2):
                        for j in range(2):
                            last = mm(ps[:, 2 * tt + h, :], shT[:, j, tt * P:(tt + 1) * P],
                                      narrow[:, m % RING, j * D + h * 512:j * D + h * 512 + 512],
                                      start=(j == 0), stop=False, skip_group_check=True)
                last.then_inc(S["narrow_used"], 1)
                pe.wait_ge(S["parts_ready"], k + 1)
                expert_loop("", ITERS, k * ITERS, n + 1, m + 1, k)
                pe.wait_ge(S["flag_ready"], k + 1)
                many = pe.value_load(flag[0:1, 0:1])
                with pe.If(many > SLOTS):
                    o = "over_"
                    pe.sem_inc(S[o + "wide_used"], RING)
                    pe.sem_inc(S[o + "narrow_used"], RING)
                    expert_loop(o, O_ITERS, 0, 0, 0, 0)

        @block.scalar
        def _(act):
            def turn_x(i):
                st = stages[i]
                if st[0] == "M":
                    if i:
                        split_high(act, st, 0)
                        split_high(act, st, 1)
                    for b in range(4):
                        act.wait_ge(S["x_turned"], 4 * i + b + 1)
                        tt, half = divmod(b, 2)
                        nc.scalar.copy(xT_hi[:, 4 * half:4 * half + 4, tt * P:(tt + 1) * P],
                                       ps[:, 4 + b, :].rearrange("p (k t) -> p k t", k=4)).then_inc(S["x_high"], 1)
                    if i == 0:
                        split_high(act, st, 0)
                        split_high(act, st, 1)
                    return
                for b in (0, 2):
                    act.wait_ge(S["x_turned"], 4 * i + b + 1)
                    tt, half = divmod(b, 2)
                    nc.scalar.copy(xT[:, 4 * half:4 * half + 4, tt * P:(tt + 1) * P],
                                   ps[:, 4 + b, :].rearrange("p (k t) -> p k t", k=4)).then_inc(S["xT_ready"], 1)

            def expert_loop(o, iters, base):
                with act.Fori(0, iters) as it:
                    for b in range(2):
                        act.wait_ge(S[o + "gathered"], it * 4 + (4 * base + b + 1))
                        nc.scalar.copy(hTe[:, :, 2 * b:2 * b + 2, :].rearrange("p q k s -> p k q s"),
                                       ps[:, 4 + b, :].rearrange("p (k q s) -> p k q s", k=2, q=2)).then_inc(S[o + "gathered_lo"], 1)
                    for p in range(2):
                        act.wait_ge(S[o + "gate_up_done"], it * 2 + (2 * base + p + 1))
                        nc.scalar.activation(silu_g[:, p, :], ps[:, 4 + p, 0:DE], ACT.Silu).then_inc(S[o + "silu_ready"], 1)
                    for p in range(2):
                        for h in range(2):
                            act.wait_ge(S[o + "down_done"], it * 4 + (4 * base + 2 * p + h + 1))
                            nc.scalar.copy(y_parts[:, p, 0, h * 512:(h + 1) * 512], ps[:, 6 + h, :]
                                           ).then_inc(S[o + "y_lo"], 1)

            def load_ln_table():
                nc.scalar.activation(unused[:, :], cst[:, C_ONES:C_ONES + 1], ACT.Ln)

            for i, st in enumerate(stages):
                turn_x(i)
                if st[0] == "M":
                    mixer_act[st](act)
                    load_ln_table()
                    inv_root(act, rstd[:, :], "ln_" + st)
                    continue
                k = moe_no[st]
                act.wait_ge(S["logits_done"], k + 1)
                nc.scalar.activation(scores, ps[:, 4, 0:TT * NE].rearrange("p (t e) -> p t e", t=TT), ACT.Exp, scale=-1.0
                                     ).then_inc(S["exp_scores"], 1)
                act.wait_ge(S["shared_up"], k + 1)
                nc.scalar.activation(sh_silu, ps[:, 6, :].rearrange("p (j t) -> p j t", j=2), ACT.Silu).then_inc(S["shared_silu"], 1)
                expert_loop("", ITERS, k * ITERS)
                act.wait_ge(S["flag_ready"], k + 1)
                many = act.value_load(flag[0:1, 0:1])
                with act.If(many > SLOTS):
                    expert_loop("over_", O_ITERS, 0)
                load_ln_table()
                inv_root(act, rstd[:, :], "ln_" + st)

        @block.vector
        def _(dve):
            v = nc.vector
            order = [0]

            def link(ins):
                order[0] += 1
                ins.then_inc(S["dve_order"], 1)
                dve.wait_ge(S["dve_order"], order[0])

            def turn_x(i):
                st = stages[i]
                if st[0] == "M":
                    for b in range(4):
                        dve.wait_ge(S["x_high"], X0[st] + b + 1)
                        tt, half = divmod(b, 2)
                        tok = slice(tt * P, (tt + 1) * P)
                        v.tensor_tensor(x_low4(st, half)[:, :, tok], ps[:, 4 + b, :].rearrange("p (k t) -> p k t", k=4),
                                        xT_hi[:, 4 * half:4 * half + 4, tok].bitcast(F32), ALU.subtract).then_inc(S["xT_ready"], 1)
                    return
                for b in (1, 3):
                    dve.wait_ge(S["x_turned"], 4 * i + b + 1)
                    tt, half = divmod(b, 2)
                    v.tensor_copy(xT[:, 4 * half:4 * half + 4, tt * P:(tt + 1) * P],
                                  ps[:, 4 + b, :].rearrange("p (k t) -> p k t", k=4)).then_inc(S["xT_ready"], 1)

            def layer_norm(i):
                for tt in range(TT):
                    if stages[i][0] == "M":
                        if tt == 0:
                            dve.wait_ge(S["tile_summed"], mixers.index(stages[i]) + 1)
                        elif stages[i] == "M0":
                            dve.wait_ge(S["wide_used"], RING + wide_at["M0"] + N_M["M0"])
                        else:
                            dve.wait_ge(S["unit_done"], W0["M1"] + UNITS["M1"] + 8)
                    link(v.scalar_tensor_tensor(out=x_tok[:, tt, :], in0=x_tok[:, tt, :], scalar=ALPHA,
                                                in1=ps[:, 2 * tt:2 * tt + 2, :].rearrange("p b c -> p (b c)"),
                                                op0=ALU.mult, op1=ALU.add))
                    for h in range(2):
                        last = v.bn_stats(out=stats[:, tt, h, :], in_=x_tok[:, tt, h * 512:(h + 1) * 512])
                    link(last)
                    link(v.bn_aggr(out=mv[:, tt, :], in_=stats[:, tt, :, :]))
                v.tensor_scalar(rstd[:, :], mv[:, :, 1], LN_EPS, None, ALU.add).then_inc(S["square_ready"], 1)
                for tt in range(TT):
                    link(v.tensor_scalar(x_tok[:, tt, :], x_tok[:, tt, :], mv[:, tt, 0:1], None, ALU.subtract))
                dve.wait_ge(S["root_ready"], 2 * ROOT["ln_" + stages[i]])
                dve.wait_ge(S["ln_in"], 32 * (i + 1))
                for tt in range(TT):
                    link(v.scalar_tensor_tensor(out=x_tok[:, tt, :], in0=x_tok[:, tt, :], scalar=rstd[:, tt:tt + 1],
                                                in1=lng[:, :], op0=ALU.mult, op1=ALU.mult))
                    v.tensor_tensor(x_tok[:, tt, :], x_tok[:, tt, :], lnb[:, :], ALU.add).then_inc(S["ln_done"], 1)
                dve.wait_ge(S["ln_done"], 2 * i + 2)

            def one_hots(o, col):
                v.tensor_tensor(oh[:, :, :, :], spread(spread(cm(C_IOTA, SLOTS), 1, [P, EPI, SLOTS]), 1, [P, TT, EPI, SLOTS]),
                                spread(pos_r[:, :, bass.ds(col, EPI)], 3, [P, TT, EPI, SLOTS]), ALU.is_equal
                                ).then_inc(S[o + "onehot_ready"], 1)

            def gated(o, col, value):
                dve.wait_ge(S[o + "onehot_ready"], value)
                v.tensor_tensor(ohg, oh[:, :, :, :].bitcast(F32), spread(gate_r[:, :, bass.ds(col, EPI)], 3, [P, TT, EPI, SLOTS]), ALU.mult
                                ).then_inc(S[o + "gated_ready"], 1)

            def expert_loop(o, iters, base, col0, k):
                one_hots(o, col0)
                gated(o, col0, base + k + 1)
                with dve.Fori(0, iters) as it:
                    for b in range(2, 4):
                        dve.wait_ge(S[o + "gathered"], it * 4 + (4 * base + b + 1))
                        v.tensor_copy(hTe[:, :, 2 * b:2 * b + 2, :].rearrange("p q k s -> p k q s"),
                                      ps[:, 4 + b, :].rearrange("p (k q s) -> p k q s", k=2, q=2)).then_inc(S[o + "gathered_hi"], 1)
                    dve.wait_ge(S[o + "gates_turned"], it + (base + 1))
                    gT = ps[:, 7, :].rearrange("p (q t) -> p q t", q=2)
                    v.tensor_reduce(slot_gate, gT, AX, ALU.add).then_inc(S[o + "gates_out"], 1)
                    v.tensor_scalar(ohT[:, :, :], gT, 0.0, None, ALU.is_gt).then_inc(S[o + "gates_out"], 1)
                    dve.wait_ge(S[o + "gates_out"], it * 2 + (2 * base + 2))
                    one_hots(o, it * EPI + (col0 + EPI))
                    gated(o, it * EPI + (col0 + EPI), it + (base + k + 2))

                    def times_up(p):
                        dve.wait_ge(S[o + "silu_ready"], it * 2 + (2 * base + p + 1))
                        v.scalar_tensor_tensor(out=act_tok[:, p, :], in0=silu_g[:, p, :], scalar=slot_gate[:, p:p + 1],
                                               in1=ps[:, 4 + p, DE:2 * DE], op0=ALU.mult, op1=ALU.mult
                                               ).then_inc(S[o + "act_ready"], 1)

                    def turned_out(p):
                        dve.wait_ge(S[o + "pair_turned"], it * 2 + (2 * base + p + 1))
                        v.tensor_copy(turned[:, p, :], ps[:, 4 + p, 0:2 * P]).then_inc(S[o + "turned_ready"], 1)

                    def y_out(p, h):
                        dve.wait_ge(S[o + "y_lo"], it * 4 + (4 * base + 2 * p + h + 1))
                        v.tensor_tensor(y_parts[:, p, 1, h * 512:(h + 1) * 512], ps[:, 6 + h, :],
                                        y_parts[:, p, 0, h * 512:(h + 1) * 512].bitcast(F32), ALU.subtract).then_inc(S[o + "y_hi"], 1)

                    times_up(0)
                    turned_out(0)
                    times_up(1)
                    y_out(0, 0)
                    turned_out(1)
                    y_out(0, 1)
                    y_out(1, 0)
                    y_out(1, 1)

            for i, st in enumerate(stages):
                turn_x(i)
                if i == 0:
                    dve.wait_ge(S["tables_in"], 16)
                if st[0] == "M":
                    mixer_dve[st](dve, v, link)
                    layer_norm(i)
                    continue
                k = moe_no[st]
                dve.wait_ge(S["exp_scores"], k + 1)
                link(v.tensor_scalar(scores, scores, 1.0, None, ALU.add))
                link(v.reciprocal(scores, scores))
                dve.wait_ge(S["router_in"], 32 * (k + 1))
                link(v.tensor_tensor(choice, scores, spread(rb, 1, [P, TT, NE]), ALU.add))
                for tt in range(TT):
                    for g in range(NG):
                        last = v.max(out=grp_max[:, tt, g, :], in_=choice[:, tt, g * GE:(g + 1) * GE])
                        link(last)
                link(v.tensor_tensor(grp, grp_max[:, :, :, 0], grp_max[:, :, :, 1], ALU.add))
                left = spread(grp, 2, [P, TT, NG, NG])
                right = spread(grp, 3, [P, TT, NG, NG])
                link(v.tensor_tensor(grp_gt, left, right, ALU.is_gt))
                link(v.tensor_tensor(grp_eq, left, right, ALU.is_equal))
                link(v.tensor_tensor(grp_eq, grp_eq, spread(cm(C_G8, NG * NG).rearrange("p (a b) -> p a b", a=NG), 1, [P, TT, NG, NG]), ALU.mult))
                link(v.tensor_tensor(grp_gt, grp_gt, grp_eq, ALU.add))
                link(v.tensor_reduce(grp_rank, grp_gt, AX, ALU.add))
                link(v.tensor_scalar(grp_off, grp_rank, float(TOPG), -FAR, ALU.is_ge, ALU.mult))
                c4 = choice.rearrange("p t (g e) -> p t g e", g=NG)
                link(v.tensor_tensor(c4, c4, spread(grp_off, 3, [P, TT, NG, GE]), ALU.add))
                for tt in range(TT):
                    link(v.max(out=top8[:, tt, :], in_=choice[:, tt, :]))
                    link(v.match_replace(out=choice_rep[:, tt, :], in_to_replace=top8[:, tt, :], in_values=choice[:, tt, :],
                                         imm_value=-3.0 * FAR))
                v.tensor_tensor(sel, choice, choice_rep, ALU.is_gt).then_inc(S["sel_ready"], 1)
                dve.wait_ge(S["sel_ready"], k + 1)
                link(v.tensor_tensor(gate_one, sel, scores, ALU.mult))
                link(v.tensor_reduce(gate_sum, gate_one, AX, ALU.add))
                link(v.reciprocal(gate_inv, gate_sum))
                link(v.tensor_tensor(gate_one, gate_one, spread(gate_inv, 2, [P, TT, NE]), ALU.mult))
                for r in range(ROUNDS):
                    link(v.tensor_scalar(gate_r[:, :, r * NE:(r + 1) * NE], gate_one, ROUTE_SCALE, None, ALU.mult))
                link(v.memset(gate_r[:, :, ROUNDS * NE:], 0.0))
                dve.wait_ge(S["shared_silu"], k + 1)
                v.tensor_tensor(shT, sh_silu, ps[:, 7, :].rearrange("p (j t) -> p j t", j=2), ALU.mult).then_inc(S["shared_act"], 1)
                dve.wait_ge(S["ranks_done"], k + 1)
                link(v.scalar_tensor_tensor(out=pos_one, in0=ps[:, 5, 0:TT * NE].rearrange("p (t e) -> p t e", t=TT), scalar=1.0,
                                            in1=sel, op0=ALU.add, op1=ALU.mult))
                for r in range(ROUNDS):
                    link(v.tensor_scalar(pos_r[:, :, r * NE:(r + 1) * NE], pos_one, -1.0 - r * SLOTS, None, ALU.add))
                link(v.memset(pos_r[:, :, ROUNDS * NE:], -1.0))
                link(v.tensor_reduce(cnt[:, 0:1], ps[:, 5, 2 * NE:3 * NE], AX, ALU.max))
                v.tensor_copy(flag[:, 0:1], cnt[:, 0:1]).then_inc(S["flag_ready"], 1)
                xk = x_tok[:, :, :].rearrange("p t (q k) -> p t k q", k=KT)
                for tt in range(TT):
                    link(v.tensor_copy(h_parts[:, tt, 0], xk[:, tt]))
                    last = v.tensor_tensor(h_parts[:, tt, 1], xk[:, tt], h_parts[:, tt, 0].bitcast(F32), ALU.subtract)
                last.then_inc(S["parts_ready"], 1)
                expert_loop("", ITERS, k * ITERS, 0, k)
                dve.wait_ge(S["flag_ready"], k + 1)
                many = dve.value_load(flag[0:1, 0:1])
                with dve.If(many > SLOTS):
                    dve.wait_ge(S["gated_ready"], (ITERS + 1) * (k + 1))
                    dve.wait_ge(S["pair_combined"], 2 * ITERS * (k + 1))
                    expert_loop("over_", O_ITERS, 0, NE, 0)
                    dve.wait_ge(S["over_pair_combined"], 2 * O_ITERS)
                dve.wait_ge(S["pair_combined"], 2 * ITERS * (k + 1))
                layer_norm(i)


def host_layout(a):
    a = dict(a)
    if "l0_b_mix" in a:
        names = ("l0_b_mix", "l0_b_w0", "l0_b_a0", "l0_b_k_k", "l0_b_k_a", "l0_b_r_k")
        a["l0_b_cols"] = np.ascontiguousarray(np.concatenate([np.asarray(a.pop(n)).reshape(-1, P) for n in names]).T)
    if "l1_conv_w" in a:
        a["l1_conv_cols"] = np.ascontiguousarray(np.asarray(a.pop("l1_conv_w")).reshape(4, 32, P).transpose(2, 1, 0).reshape(P, 128))
    return a


def kernel(**inputs):
    import concourse.bacc as bacc
    from concourse.bass_utils import run_bass_kernel_spmd

    arrays = host_layout({n: np.asarray(v) for n, v in inputs.items()})
    arrays["constants"], arrays["alibi"] = constants()
    nc = bacc.Bacc("TRN2", target_bir_lowering=False, num_devices=1)
    dram, a = {}, {}
    for name, value in arrays.items():
        value = np.ascontiguousarray(value)
        dram[f"in_{name}"] = value
        a[name] = nc.dram_tensor(f"in_{name}", value.shape, mybir.dt.from_np(value.dtype), kind="ExternalInput").ap()
    out = nc.dram_tensor("out_dram", (1, SEQ, D), F32, kind="ExternalOutput").ap()
    build_program(nc, a, out)
    return run_bass_kernel_spmd(nc, [dram], core_ids=[0]).results[0]["out_dram"]
```
